# Optimizing a Trainium2 kernel written in Bass

```python
import math
import jax, jax.numpy as jnp
from jax import lax
import numpy as np
import jax
import jax.numpy as jnp

D_MODEL = 1024
BATCH = 1
SEQ = 512
DEPTH = 1

N_META = 16
HEAD_DIM = 64
SWA_Q_HEADS = D_MODEL // (2 * HEAD_DIM)
SWA_KV_HEADS = max(SWA_Q_HEADS // 4, 1)
SWA_GROUP = SWA_Q_HEADS // SWA_KV_HEADS
FOX_HEADS = D_MODEL // (2 * HEAD_DIM)
SWA_Q_W = SWA_Q_HEADS * HEAD_DIM
SWA_KV_W = SWA_KV_HEADS * HEAD_DIM
FOX_W = FOX_HEADS * HEAD_DIM
D_MIX = SWA_Q_W + FOX_W
OFF_QA = SWA_Q_W
OFF_KA = OFF_QA + SWA_KV_W
OFF_VA = OFF_KA + SWA_KV_W
OFF_QB = OFF_VA + FOX_W
OFF_KB = OFF_QB + FOX_W
OFF_VB = OFF_KB + FOX_W
D_PROJ = OFF_VB + FOX_HEADS
WINDOW = 128
BLOCK = 128
N_BUCKETS = 32
MAX_DISTANCE = 128
D_FF = -(-8 * D_MODEL // (3 * 256)) * 256
EPS = 1e-6
NEG_INF = -1e30


def rms_norm(x, g):
    xf = x.astype(jnp.float32)
    y = xf * lax.rsqrt(jnp.mean(xf * xf, axis=-1, keepdims=True) + EPS)
    return (y * g.astype(jnp.float32)).astype(x.dtype)

def t5_bucket(dist):
    n = jnp.maximum(dist, 0).astype(jnp.int32)
    max_exact = N_BUCKETS // 2
    nf = jnp.maximum(n, 1).astype(jnp.float32)
    large = max_exact + (jnp.log(nf / max_exact) / math.log(MAX_DISTANCE / max_exact)
                         * (N_BUCKETS - max_exact)).astype(jnp.int32)
    large = jnp.minimum(large, N_BUCKETS - 1)
    return jnp.where(n < max_exact, n, large)

def softmax_with_sink(s, sink):
    sink_r = sink.reshape((1,) + sink.shape + (1,) * (s.ndim - 3))
    col = jnp.broadcast_to(sink_r, s.shape[:-1] + (1,))
    p = jax.nn.softmax(jnp.concatenate([s, col], axis=-1), axis=-1)
    return p[..., :-1]

def swa_sink_attention(q, k, v, sinks, rel_bias):
    B, L = q.shape[0], q.shape[1]
    n_blk = (L - N_META) // BLOCK
    scale = HEAD_DIM ** -0.5
    sink = sinks.astype(jnp.float32).reshape(SWA_KV_HEADS, SWA_GROUP)
    tab = rel_bias.astype(jnp.float32)
    mi = jnp.arange(N_META)
    km, vm = k[:, :N_META], v[:, :N_META]

    qm = q[:, :N_META].reshape(B, N_META, SWA_KV_HEADS, SWA_GROUP, HEAD_DIM)
    d_mm = mi[:, None] - mi[None, :]
    b_mm = tab[t5_bucket(d_mm)].transpose(2, 0, 1).reshape(SWA_KV_HEADS, SWA_GROUP, N_META, N_META)
    s_mm = jnp.einsum('bqhgd,bkhd->bhgqk', qm, km, preferred_element_type=jnp.float32) * scale + b_mm
    s_mm = jnp.where(d_mm >= 0, s_mm, NEG_INF)
    p_mm = softmax_with_sink(s_mm, sink).astype(v.dtype)
    o_meta = jnp.einsum('bhgqk,bkhd->bqhgd', p_mm, vm).reshape(B, N_META, SWA_Q_HEADS, HEAD_DIM)

    qr = q[:, N_META:].reshape(B, n_blk, BLOCK, SWA_KV_HEADS, SWA_GROUP, HEAD_DIM)
    kr = k[:, N_META:].reshape(B, n_blk, BLOCK, SWA_KV_HEADS, HEAD_DIM)
    vr = v[:, N_META:].reshape(B, n_blk, BLOCK, SWA_KV_HEADS, HEAD_DIM)

    def with_prev(t):
        prev = jnp.pad(t, ((0, 0), (1, 0), (0, 0), (0, 0), (0, 0)))[:, :-1]
        return jnp.concatenate([prev, t], axis=2)

    kw, vw = with_prev(kr), with_prev(vr)
    qi = jnp.arange(BLOCK)[:, None]
    ki = jnp.arange(2 * BLOCK)[None, :]
    d_w = qi + BLOCK - ki
    b_w = tab[t5_bucket(d_w)].transpose(2, 0, 1).reshape(SWA_KV_HEADS, SWA_GROUP, 1, BLOCK, 2 * BLOCK)
    blk = jnp.arange(n_blk)[:, None, None]
    valid_w = ((d_w >= 0) & (d_w < WINDOW))[None] & ((blk > 0) | (ki >= BLOCK)[None])
    s_w = jnp.einsum('bnqhgd,bnkhd->bhgnqk', qr, kw, preferred_element_type=jnp.float32) * scale + b_w
    s_w = jnp.where(valid_w, s_w, NEG_INF)
    d_m = N_META + blk * BLOCK + qi[None] - mi[None, None, :]
    b_m = tab[t5_bucket(d_m)].transpose(3, 0, 1, 2).reshape(SWA_KV_HEADS, SWA_GROUP, n_blk, BLOCK, N_META)
    s_m = jnp.einsum('bnqhgd,bmhd->bhgnqm', qr, km, preferred_element_type=jnp.float32) * scale + b_m
    p = softmax_with_sink(jnp.concatenate([s_m, s_w], axis=-1), sink).astype(v.dtype)
    o = (jnp.einsum('bhgnqm,bmhd->bnqhgd', p[..., :N_META], vm)
         + jnp.einsum('bhgnqk,bnkhd->bnqhgd', p[..., N_META:], vw))
    o_real = o.reshape(B, n_blk * BLOCK, SWA_Q_HEADS, HEAD_DIM)
    return jnp.concatenate([o_meta, o_real], axis=1)

def forgetting_attention(q, k, v, f_logit):
    B, L = q.shape[0], q.shape[1]
    n_blk = (L - N_META) // BLOCK
    scale = HEAD_DIM ** -0.5
    cum = jnp.cumsum(jax.nn.log_sigmoid(f_logit.astype(jnp.float32)), axis=1).transpose(0, 2, 1)

    mi = jnp.arange(N_META)
    s = jnp.einsum('bqhd,bkhd->bhqk', q[:, :N_META], k[:, :N_META], preferred_element_type=jnp.float32) * scale
    s = s + cum[:, :, :N_META, None] - cum[:, :, None, :N_META]
    s = jnp.where(mi[:, None] >= mi[None, :], s, NEG_INF)
    p = jax.nn.softmax(s, axis=-1).astype(v.dtype)
    o_meta = jnp.einsum('bhqk,bkhd->bqhd', p, v[:, :N_META])

    qb = q[:, N_META:].reshape(B, n_blk, BLOCK, FOX_HEADS, HEAD_DIM).transpose(1, 0, 2, 3, 4)
    cb = cum[:, :, N_META:].reshape(B, FOX_HEADS, n_blk, BLOCK).transpose(2, 0, 1, 3)
    k_pos = jnp.arange(L)

    def one_block(args):
        q_blk, c_blk, b = args
        q_pos = N_META + b * BLOCK + jnp.arange(BLOCK)
        sb = jnp.einsum('bqhd,bkhd->bhqk', q_blk, k, preferred_element_type=jnp.float32) * scale
        sb = sb + c_blk[..., None] - cum[:, :, None, :]
        sb = jnp.where(k_pos[None, :] <= q_pos[:, None], sb, NEG_INF)
        pb = jax.nn.softmax(sb, axis=-1).astype(v.dtype)
        return jnp.einsum('bhqk,bkhd->bqhd', pb, v)

    o = lax.map(one_block, (qb, cb, jnp.arange(n_blk)))
    o_real = o.transpose(1, 0, 2, 3, 4).reshape(B, n_blk * BLOCK, FOX_HEADS, HEAD_DIM)
    return jnp.concatenate([o_meta, o_real], axis=1)

def first_inputs(seed: int = 0) -> dict:
    key = jax.random.key(seed)
    ks = jax.random.split(key, 14)
    f32 = jnp.float32
    gain = lambda k: 1.0 + 0.05 * jax.random.normal(k, (DEPTH, D_MODEL), f32)
    return {
        "x": jax.random.normal(ks[0], (BATCH, SEQ, D_MODEL), f32),
        "meta_tokens": jax.random.normal(ks[1], (N_META, D_MODEL), f32),
        "rel_bias": 0.5 * jax.random.normal(ks[2], (N_BUCKETS, SWA_Q_HEADS), f32),
        "ln_pre_mix": gain(ks[3]),
        "ln_post_mix": gain(ks[4]),
        "ln_pre_ffn": gain(ks[5]),
        "ln_post_ffn": gain(ks[6]),
        "w_in": jax.random.normal(ks[7], (DEPTH, D_MODEL, D_PROJ), f32) * D_MODEL ** -0.5,
        "b_forget": jax.random.uniform(ks[8], (DEPTH, FOX_HEADS), f32, minval=1.0, maxval=5.0),
        "sinks": 0.5 * jax.random.normal(ks[9], (DEPTH, SWA_Q_HEADS), f32),
        "w_out": jax.random.normal(ks[10], (DEPTH, D_MIX, D_MODEL), f32) * D_MIX ** -0.5,
        "w_gate_up": jax.random.normal(ks[11], (DEPTH, D_MODEL, 2 * D_FF), f32) * D_MODEL ** -0.5,
        "w_down": jax.random.normal(ks[12], (DEPTH, D_FF, D_MODEL), f32) * D_FF ** -0.5,
    }

def first_block(x, meta_tokens, rel_bias, ln_pre_mix, ln_post_mix, ln_pre_ffn, ln_post_ffn,
              w_in, b_forget, sinks, w_out, w_gate_up, w_down):
    B = x.shape[0]
    meta = jnp.broadcast_to(meta_tokens[None].astype(x.dtype), (B, N_META, D_MODEL))
    h = jnp.concatenate([meta, x], axis=1)
    L = h.shape[1]
    for layer in range(DEPTH):
        hn = rms_norm(h, ln_pre_mix[layer])
        proj = jnp.einsum('bld,dc->blc', hn, w_in[layer])
        q_a = proj[..., :OFF_QA].reshape(B, L, SWA_Q_HEADS, HEAD_DIM)
        k_a = proj[..., OFF_QA:OFF_KA].reshape(B, L, SWA_KV_HEADS, HEAD_DIM)
        v_a = proj[..., OFF_KA:OFF_VA].reshape(B, L, SWA_KV_HEADS, HEAD_DIM)
        q_b = proj[..., OFF_VA:OFF_QB].reshape(B, L, FOX_HEADS, HEAD_DIM)
        k_b = proj[..., OFF_QB:OFF_KB].reshape(B, L, FOX_HEADS, HEAD_DIM)
        v_b = proj[..., OFF_KB:OFF_VB].reshape(B, L, FOX_HEADS, HEAD_DIM)
        f_b = proj[..., OFF_VB:] + b_forget[layer].astype(proj.dtype)
        o_a = swa_sink_attention(q_a, k_a, v_a, sinks[layer], rel_bias)
        o_b = forgetting_attention(q_b, k_b, v_b, f_b)
        mix = jnp.concatenate([o_a.reshape(B, L, SWA_Q_W), o_b.reshape(B, L, FOX_W)], axis=-1)
        h = h + rms_norm(jnp.einsum('blc,cd->bld', mix, w_out[layer]), ln_post_mix[layer])
        hn = rms_norm(h, ln_pre_ffn[layer])
        gu = jnp.einsum('bld,df->blf', hn, w_gate_up[layer])
        ff = jnp.einsum('blf,fd->bld', jax.nn.silu(gu[..., :D_FF]) * gu[..., D_FF:], w_down[layer])
        h = h + rms_norm(ff, ln_post_ffn[layer])
    return h[:, N_META:]


CHUNK = 64

A_HEADS = 8
A_DK = 128
A_DV = 128
A_QK = A_HEADS * A_DK
A_V = A_HEADS * A_DV
CONV_W = 4
CONV_CH = 2 * A_QK + A_V

B_HEADS = 8
B_DK = 128
B_DV = 128
B_K = B_HEADS * B_DK
B_V = B_HEADS * B_DV

IN_SPLITS = (A_QK, A_QK, A_V, A_HEADS, A_HEADS, A_V, B_K, B_V, B_K, B_V, D_MODEL, D_MODEL)
IN_WIDTH = 3 * A_QK + 2 * A_V + 2 * A_HEADS + 2 * B_K + 2 * B_V + 2 * D_MODEL

N_KEYS = 128
N_EXPERTS = N_KEYS * N_KEYS
P_HEADS = 8
P_DKEY = 256
P_DHALF = P_DKEY // 2
P_TOPK = 16
P_TOKEN_BLOCK = 128


def _rmsnorm(x, g):
    xf = x.astype(jnp.float32)
    y = xf * lax.rsqrt(jnp.mean(xf * xf, axis=-1, keepdims=True) + EPS) * g.astype(jnp.float32)
    return y.astype(x.dtype)

def _l2norm(x):
    return x * lax.rsqrt(jnp.sum(x * x, axis=-1, keepdims=True) + EPS)

def _split_cols(p):
    outs = []
    off = 0
    for w in IN_SPLITS:
        outs.append(p[..., off:off + w])
        off += w
    return outs

def _causal_conv_silu(x, w):
    k_w = w.shape[0]
    t = x.shape[1]
    xp = jnp.pad(x, ((0, 0), (k_w - 1, 0), (0, 0)))
    y = sum(xp[:, j:j + t] * w[j] for j in range(k_w))
    return jax.nn.silu(y)

def _to_chunks(x):
    b, t, h, d = x.shape
    return x.reshape(b, t // CHUNK, CHUNK, h, d).transpose(1, 0, 3, 2, 4)

def _to_chunks_s(x):
    b, t, h = x.shape
    return x.reshape(b, t // CHUNK, CHUNK, h).transpose(1, 0, 3, 2)

def _from_chunks(o):
    n, b, h, c, d = o.shape
    return o.transpose(1, 0, 3, 2, 4).reshape(b, n * c, h, d)

def _gated_delta_rule(q, k, v, beta, g):
    dk = q.shape[-1]
    dv = v.shape[-1]
    q = _l2norm(q) * (dk ** -0.5)
    k = _l2norm(k)
    qc, kc, vc = _to_chunks(q), _to_chunks(k), _to_chunks(v)
    bc = _to_chunks_s(beta)
    G = jnp.cumsum(_to_chunks_s(g), axis=-1)
    causal = jnp.tril(jnp.ones((CHUNK, CHUNK), dtype=bool))
    diff = G[..., :, None] - G[..., None, :]
    decay = jnp.where(causal, jnp.exp(jnp.where(causal, diff, 0.0)), 0.0)
    kb = kc * bc[..., None]
    a_kk = jnp.einsum('nbhid,nbhjd->nbhij', kb, kc) * decay
    lhs = jnp.eye(CHUNK, dtype=jnp.float32) + jnp.tril(a_kk, -1)
    rhs = jnp.concatenate([vc * bc[..., None], kb * jnp.exp(G)[..., None]], axis=-1)
    sol = lax.linalg.triangular_solve(lhs, rhs, left_side=True, lower=True, unit_diagonal=True)
    u, w = sol[..., :dv], sol[..., dv:]
    a_qk = jnp.einsum('nbhid,nbhjd->nbhij', qc, kc) * decay
    q_dec = qc * jnp.exp(G)[..., None]
    k_dec = kc * jnp.exp(G[..., -1:] - G)[..., None]
    g_last = jnp.exp(G[..., -1])

    def step(S, inp):
        u_n, w_n, aqk_n, qd_n, kd_n, gl_n = inp
        v_new = u_n - jnp.einsum('bhcd,bhde->bhce', w_n, S)
        o = jnp.einsum('bhcd,bhde->bhce', qd_n, S) + jnp.einsum('bhij,bhje->bhie', aqk_n, v_new)
        S = S * gl_n[..., None, None] + jnp.einsum('bhcd,bhce->bhde', kd_n, v_new)
        return S, o

    s0 = jnp.zeros((q.shape[0], q.shape[2], dk, dv), jnp.float32)
    _, o = lax.scan(step, s0, (u, w, a_qk, q_dec, k_dec, g_last))
    return _from_chunks(o)

def _hgrn2_recurrence(q, k, v, log_f):
    dk = q.shape[-1]
    dv = v.shape[-1]
    qc, kc, vc = _to_chunks(q), _to_chunks(k), _to_chunks(v)
    bc = jnp.cumsum(_to_chunks(log_f), axis=-2)
    causal3 = jnp.tril(jnp.ones((CHUNK, CHUNK), dtype=bool))[:, :, None]

    def step(S, inp):
        q_n, k_n, v_n, b_n = inp
        diff = b_n[..., :, None, :] - b_n[..., None, :, :]
        dec = jnp.where(causal3, jnp.exp(jnp.where(causal3, diff, 0.0)), 0.0)
        a = jnp.einsum('bhid,bhjd,bhijd->bhij', q_n, k_n, dec)
        o = jnp.einsum('bhid,bhde->bhie', q_n * jnp.exp(b_n), S) + jnp.einsum('bhij,bhje->bhie', a, v_n)
        b_last = b_n[..., -1:, :]
        S = S * jnp.exp(b_last)[..., 0, :, None] + jnp.einsum('bhjd,bhje->bhde', k_n * jnp.exp(b_last - b_n), v_n)
        return S, o

    s0 = jnp.zeros((q.shape[0], q.shape[2], dk, dv), jnp.float32)
    _, o = lax.scan(step, s0, (qc, kc, vc, bc))
    return _from_chunks(o)

def _peer(x, w_pq, sub_keys, expert_u, expert_v):
    b, t, d = x.shape
    n_tok = b * t
    xf = x.reshape(n_tok, d)
    q = (xf @ w_pq).reshape(n_tok, P_HEADS, 2, P_DHALF)
    s = jnp.einsum('thpd,phkd->thpk', q, sub_keys)
    top_s, top_i = lax.top_k(s, P_TOPK)
    cand_s = (top_s[:, :, 0, :, None] + top_s[:, :, 1, None, :]).reshape(n_tok, P_HEADS, P_TOPK * P_TOPK)
    cand_i = (top_i[:, :, 0, :, None] * N_KEYS + top_i[:, :, 1, None, :]).reshape(n_tok, P_HEADS, P_TOPK * P_TOPK)
    best_s, pos = lax.top_k(cand_s, P_TOPK)
    idx = jnp.take_along_axis(cand_i, pos, axis=-1)
    gate = jax.nn.softmax(best_s.astype(jnp.float32), axis=-1).astype(x.dtype)
    n_blk = n_tok // P_TOKEN_BLOCK
    xb = xf.reshape(n_blk, P_TOKEN_BLOCK, d)
    ib = idx.reshape(n_blk, P_TOKEN_BLOCK, P_HEADS * P_TOPK)
    gb = gate.reshape(n_blk, P_TOKEN_BLOCK, P_HEADS * P_TOPK)

    def block(args):
        xt, it, gt = args
        u = expert_u[it]
        h = jax.nn.gelu(jnp.einsum('td,tkd->tk', xt, u), approximate=False)
        v = expert_v[it]
        return jnp.einsum('tk,tkd->td', gt * h, v)

    y = lax.map(block, (xb, ib, gb))
    return y.reshape(b, t, d)

def second_inputs(seed: int = 0) -> dict:
    key = jax.random.key(seed)
    ks = jax.random.split(key, 20)

    def nrm(k, shape, scale):
        return jax.random.normal(k, shape, jnp.float32) * scale

    x = nrm(ks[0], (BATCH, SEQ, D_MODEL), 1.0)
    norm1 = 1.0 + nrm(ks[1], (DEPTH, D_MODEL), 0.02)
    w_in = nrm(ks[2], (DEPTH, D_MODEL, IN_WIDTH), D_MODEL ** -0.5)
    conv_a = nrm(ks[3], (DEPTH, CONV_W, CONV_CH), CONV_W ** -0.5)
    a_log = jnp.log(jax.random.uniform(ks[4], (DEPTH, A_HEADS), jnp.float32, 1.0, 16.0))
    dt = jnp.exp(jax.random.uniform(ks[5], (DEPTH, A_HEADS), jnp.float32, math.log(1e-3), math.log(1e-1)))
    dt_bias = dt + jnp.log(-jnp.expm1(-dt))
    a_onorm = 1.0 + nrm(ks[6], (DEPTH, A_DV), 0.02)
    b_lower_bound = 1.0 + nrm(ks[7], (DEPTH + 1, B_K), 0.1)
    b_onorm = 1.0 + nrm(ks[8], (DEPTH, B_DV), 0.02)
    w_branch_a = nrm(ks[9], (DEPTH, A_V, D_MODEL), A_V ** -0.5)
    w_branch_b = nrm(ks[10], (DEPTH, B_V, D_MODEL), B_V ** -0.5)
    w_out = nrm(ks[11], (DEPTH, D_MODEL, D_MODEL), D_MODEL ** -0.5)
    norm2 = 1.0 + nrm(ks[12], (DEPTH, D_MODEL), 0.02)
    w_pq = nrm(ks[13], (DEPTH, D_MODEL, P_HEADS * P_DKEY), D_MODEL ** -0.5)
    sub_keys = nrm(ks[14], (DEPTH, 2, P_HEADS, N_KEYS, P_DHALF), P_DHALF ** -0.5)
    expert_u = nrm(ks[15], (DEPTH, N_EXPERTS, D_MODEL), D_MODEL ** -0.5)
    expert_v = nrm(ks[16], (DEPTH, N_EXPERTS, D_MODEL), P_HEADS ** -0.5)
    final_norm = 1.0 + nrm(ks[17], (D_MODEL,), 0.02)
    return {'x': x, 'norm1': norm1, 'w_in': w_in, 'conv_a': conv_a, 'a_log': a_log,
            'dt_bias': dt_bias, 'a_onorm': a_onorm, 'b_lower_bound': b_lower_bound,
            'b_onorm': b_onorm, 'w_branch_a': w_branch_a, 'w_branch_b': w_branch_b,
            'w_out': w_out, 'norm2': norm2, 'w_pq': w_pq, 'sub_keys': sub_keys,
            'expert_u': expert_u, 'expert_v': expert_v, 'final_norm': final_norm}

def second_block(x, norm1, w_in, conv_a, a_log, dt_bias, a_onorm, b_lower_bound, b_onorm,
              w_branch_a, w_branch_b, w_out, norm2, w_pq, sub_keys, expert_u, expert_v,
              final_norm):
    dt = x.dtype
    bsz, t, _ = x.shape
    f32 = jnp.float32
    lower_bounds = jnp.cumsum(jax.nn.softmax(b_lower_bound.astype(f32), axis=0), axis=0)
    for l in range(DEPTH):
        h = _rmsnorm(x, norm1[l])
        proj = h @ w_in[l]
        a_q, a_k, a_v, a_beta, a_alpha, a_gate, b_f, b_i, b_q, b_gate, g_a, g_b = _split_cols(proj)

        qkv = _causal_conv_silu(jnp.concatenate([a_q, a_k, a_v], axis=-1), conv_a[l]).astype(f32)
        qa = qkv[..., :A_QK].reshape(bsz, t, A_HEADS, A_DK)
        ka = qkv[..., A_QK:2 * A_QK].reshape(bsz, t, A_HEADS, A_DK)
        va = qkv[..., 2 * A_QK:].reshape(bsz, t, A_HEADS, A_DV)
        beta = jax.nn.sigmoid(a_beta.astype(f32))
        log_alpha = -jnp.exp(a_log[l].astype(f32)) * jax.nn.softplus(a_alpha.astype(f32) + dt_bias[l].astype(f32))
        o_a = _gated_delta_rule(qa, ka, va, beta, log_alpha)
        o_a = _rmsnorm(o_a, a_onorm[l]) * jax.nn.silu(a_gate.astype(f32)).reshape(bsz, t, A_HEADS, A_DV)
        y_a = o_a.reshape(bsz, t, A_V).astype(dt) @ w_branch_a[l]

        lb = lower_bounds[l].reshape(B_HEADS, B_DK)
        f_gate = lb + (1.0 - lb) * jax.nn.sigmoid(b_f.astype(f32).reshape(bsz, t, B_HEADS, B_DK))
        qb = jax.nn.silu(b_q.astype(f32)).reshape(bsz, t, B_HEADS, B_DK)
        ib = b_i.astype(f32).reshape(bsz, t, B_HEADS, B_DV)
        o_b = _hgrn2_recurrence(qb, 1.0 - f_gate, ib, jnp.log(f_gate))
        o_b = _rmsnorm(o_b, b_onorm[l]) * jax.nn.sigmoid(b_gate.astype(f32)).reshape(bsz, t, B_HEADS, B_DV)
        y_b = o_b.reshape(bsz, t, B_V).astype(dt) @ w_branch_b[l]

        mix = jax.nn.sigmoid(g_a) * y_a + jax.nn.sigmoid(g_b) * y_b
        x = x + mix @ w_out[l]

        h2 = _rmsnorm(x, norm2[l])
        x = x + _peer(h2, w_pq[l], sub_keys[l], expert_u[l], expert_v[l])
    return _rmsnorm(x, final_norm)


def setup_inputs(seed=0):
    out = dict(first_inputs(seed))
    for name, value in second_inputs(seed + 1).items():
        if name != "x":
            out[name + "_2"] = value
    return out


def reference(
    x, meta_tokens, rel_bias, ln_pre_mix, ln_post_mix, ln_pre_ffn, ln_post_ffn, w_in, b_forget,
    sinks, w_out, w_gate_up, w_down, norm1_2, w_in_2, conv_a_2, a_log_2, dt_bias_2, a_onorm_2,
    b_lower_bound_2, b_onorm_2, w_branch_a_2, w_branch_b_2, w_out_2, norm2_2, w_pq_2,
    sub_keys_2, expert_u_2, expert_v_2, final_norm_2,
):
    x = first_block(
        x, meta_tokens, rel_bias, ln_pre_mix, ln_post_mix, ln_pre_ffn, ln_post_ffn, w_in,
        b_forget, sinks, w_out, w_gate_up, w_down,
    )
    return second_block(
        x, norm1_2, w_in_2, conv_a_2, a_log_2, dt_bias_2, a_onorm_2, b_lower_bound_2, b_onorm_2,
        w_branch_a_2, w_branch_b_2, w_out_2, norm2_2, w_pq_2, sub_keys_2, expert_u_2,
        expert_v_2, final_norm_2,
    )


_drawn_inputs = setup_inputs


def setup_inputs(seed=0):
    import zlib

    import numpy as np

    out = dict(_drawn_inputs(seed))
    spreads = {}
    factors = {'sinks': 8.0,
     'norm1_2': 4.811,
     'a_onorm_2': 19.729,
     'b_lower_bound_2': 31.036,
     'b_onorm_2': 64.0,
     'norm2_2': 30.224,
     'final_norm_2': 8.08}
    for name, (base, spread) in spreads.items():
        noise = np.random.default_rng([zlib.crc32(name.encode()), seed]).standard_normal(out[name].shape)
        drawn = base * np.exp(spread * noise) if base else spread * noise
        out[name] = jnp.asarray(drawn.astype(out[name].dtype))
    for name, factor in factors.items():
        out[name] = (out[name] * factor).astype(out[name].dtype)
    return out
```

```python
from contextlib import ExitStack

import numpy as np

import concourse.bass as bass
from concourse import mybir

F32 = mybir.dt.float32
I32 = mybir.dt.int32
U32 = mybir.dt.uint32
ALU = mybir.AluOpType
ACT = mybir.ActivationFunctionType
AX = mybir.AxisListType.X

P = 128
D = 1024
DT = D // P
META = 16
SEQ = 512
L = META + SEQ
HL = L // 2
TT = SEQ // P
HD = 64
H = 8
KV = 2
WIN = 128
BUCKETS = 32
MAX_DISTANCE = 128
DFF = 2816
FT = DFF // P
EPS = 1e-6
NEG = -1e30
C = 64
NC = SEQ // C
LEVELS = [1, 2, 4, 8, 16, 32]
PH = 8
TOPK = 16
NKEYS = 128
NEXP = NKEYS * NKEYS
PAIRS = PH * TOPK
UV = 8
PARTS = 4
PART = PAIRS // PARTS
NPARTS = TT * PARTS
RING = 4
DOWN_CH = 3

STREAM = [("in1", 18), ("out1", 8), ("gate_up", 2 * FT), ("down", DT * DOWN_CH),
          ("a_q", 8), ("a_k", 8), ("a_v", 8), ("a_gate", 8), ("branch_a", 8), ("g_a", 8),
          ("b_f", 8), ("b_i", 8), ("b_q", 8), ("b_gate", 8), ("branch_b", 8), ("g_b", 8),
          ("out2", 8), ("pq", 16)]
CHUNKS = sum(n for _, n in STREAM)
TILE = {"toeplitz": 0}
_at = 1
for _name, _n in STREAM:
    TILE[_name] = _at
    _at += {"gate_up": 0, "down": DT}.get(_name, _n)
FIRST_OF = {}
_at = 0
for _name, _n in STREAM:
    FIRST_OF[_name] = _at
    _at += _n

CONST = {}
_at = 0
for _name, _w in [("ident", P), ("flip", P), ("ones", P), ("causal", P), ("chunk_causal", P), ("level", P * len(LEVELS)),
                  ("sel", H * P), ("reset", SEQ), ("iota16", TOPK)]:
    CONST[_name] = (_at, _at + _w)
    _at += _w
CONST_W = _at
TOE_W = 2 * WIN + WIN - 1
TOE_M = L + META - 1
TOE = 1024
PARAM = {}
_at = 0
for _name, _w in [("ln_pre_mix", DT), ("ln_post_mix", DT), ("ln_pre_ffn", DT), ("ln_post_ffn", DT),
                  ("norm1", DT), ("norm2", DT), ("lower0", H), ("lower1", H), ("a_onorm", 1), ("b_onorm", 1),
                  ("conv", 24 * 4), ("b_forget", 1), ("a_log", 1), ("dt_bias", 1), ("rel", H),
                  ("w_f", DT * H), ("w_beta", DT * H), ("w_alpha", DT * H)]:
    PARAM[_name] = (_at, _at + _w)
    _at += _w
PARAM_W = _at


def build(nc, xT, weights, params, consts, placing, toeplitz, sinks, keys, final_norm, experts, out):
    with ExitStack() as ctx:
        def sb(name, shape, dt=F32):
            return ctx.enter_context(nc.sbuf_tensor(name, shape, dt))

        def sem(name):
            return ctx.enter_context(nc.semaphore(name))

        h_rest = nc.dram_tensor("h_rest", [P, DT, SEQ], F32, kind="Internal")
        scratch = nc.dram_tensor("toeplitz_rows", [H, TOE], F32, kind="Internal")

        ps = ctx.enter_context(nc.psum_tensor("ps", [P, 8, 512], F32))
        ring = sb("ring", [P, RING, DT, P])
        con = sb("con", [P, CONST_W])
        par = sb("par", [P, PARAM_W])
        h_all = sb("h_all", [P, DT, L])
        n_all = sb("n_all", [P, DT, L])
        arena = sb("arena", [P, 8 * DT * SEQ])
        rstd = sb("rstd", [P, L])
        gtmp = sb("gtmp", [P, 2, L])
        small = sb("small", [P, 64])

        def const(name):
            a, b = CONST[name]
            return con[:, a:b]

        def param(name):
            a, b = PARAM[name]
            return par[:, a:b]

        ident, ones, causal = const("ident"), const("ones"), const("causal")
        level_mask = const("level").rearrange("p (l i) -> p l i", i=P)
        sel = const("sel").rearrange("p (h i) -> p h i", i=P)
        conv_w = param("conv").rearrange("p (t j) -> p t j", j=4)
        w_f = param("w_f").rearrange("p (k h) -> p k h", h=H)
        w_beta = param("w_beta").rearrange("p (k h) -> p k h", h=H)
        w_alpha = param("w_alpha").rearrange("p (k h) -> p k h", h=H)

        slot = DT * SEQ
        flat_h = h_all[:, :, :].rearrange("p k t -> p (k t)")

        def region(at, *shape):
            n = int(np.prod(shape))
            v = arena[:, at:at + n] if at < 8 * slot else flat_h[:, at - 8 * slot:at - 8 * slot + n]
            if len(shape) == 2:
                v = v.rearrange("p (a b) -> p a b", b=shape[1])
            if len(shape) == 3:
                v = v.rearrange("p (a b c) -> p a b c", b=shape[1], c=shape[2])
            return v

        B = [at * slot for at in range(9)]
        at = 0
        qk1 = region(at, 13, L); at += 13 * L
        v1 = region(at, 5, 640); at += 5 * 640
        mix1 = region(at, DT, L); at += DT * L
        bias_wr = region(at - DT * L, H, 2 * WIN)
        bias_mr = region(at - DT * L + H * 2 * WIN, 5, H, META)
        bias_w = region(at, H, 2 * WIN); at += H * 2 * WIN
        bias_m = region(at, 5, H, META); at += 5 * H * META
        logit = region(at, 2, L + 2); at += 2 * (L + 2)
        prob = region(at, 4, L + 2); at += 4 * (L + 2)
        probT = region(at, 2, 5 * P); at += 2 * 5 * P
        toe_c = region(at, TOE); at += TOE
        toe_r = region(at, TOE); at += TOE
        f_row = region(at, L); at += L
        f_abs = region(at, L); at += L
        negcum = region(at, L); at += L
        ones_row = region(at, L); at += L
        sink = region(at, H); at += H
        assert at <= 8 * slot
        y1 = region(0, DT, L)
        ff = region(DT * L, FT, L)
        def tokens(n):
            return region(B[n], DT, SEQ)

        def blocks(n):
            return region(B[n], TT, H, P)

        rows = region(B[6], SEQ)
        rowG, rowE = region(B[6] + SEQ, SEQ), region(B[6] + 2 * SEQ, SEQ)
        rowX, rowY = region(B[5], SEQ), region(B[5] + SEQ, SEQ)
        glast = sb("glast", [P, H, NC])
        state = sb("state", [P, H, P])
        vnew = sb("vnew", [P, H, P])
        rowT = vnew[:, 0:TT, :]
        wide = vnew[:, 0:7, :].rearrange("p a b -> p (a b)")
        lbound = sb("lbound", [P, 4, H])

        consts_in = sem("consts_in")
        h_moved = sem("h_moved")
        toe_out = sem("toe_out")
        bias_in = sem("bias_in")
        chunk_in = [sem(f"chunk_in{i}") for i in range(RING)]
        chunk_done = sem("chunk_done")
        evac = sem("evac")
        phase = sem("phase")
        pe_link = sem("pe_link")
        act_link = sem("act_link")
        dve_link = sem("dve_link")
        sq_ready = sem("sq_ready")
        sumsq_ready = sem("sumsq_ready")
        rstd_ready = sem("rstd_ready")
        norm_ready = sem("norm_ready")
        toe_ready = sem("toe_ready")
        f_ready = sem("f_ready")
        f_act = sem("f_act")
        f_dve = sem("f_dve")
        scores_ready = sem("scores_ready")
        scores_taken = sem("scores_taken")
        logits_ready = sem("logits_ready")
        exp_done = sem("exp_done")
        probs_ready = sem("probs_ready")
        probsT_ready = sem("probsT_ready")
        probsT_taken = sem("probsT_taken")
        mixed = sem("mixed")
        mixed_taken = sem("mixed_taken")
        gated = sem("gated")
        ff_done = sem("ff_done")
        conv_in = sem("conv_in")
        conv_done = sem("conv_done")
        silu_done = sem("silu_done")
        s = {name: sem(name) for name in (
            "l2_sq", "l2_sum", "l2_rstd", "l2_done", "small_mm", "row_act", "row_dve", "rowT_ready",
            "rowT_taken", "bc_ready", "bc_taken", "dec_ready", "dec_exp", "dec_done", "kk_ready", "kk_taken",
            "tr_ready", "tr_taken", "inv_set", "inv_t", "inv_t_taken", "inv_x", "inv_x_taken", "inv_mask",
            "uw_ready", "uw_taken", "ks_ready", "vnew_ready", "os_ready", "o_taken", "state_ready",
            "lev_diff", "lev_exp", "lev_k", "lev_q", "lev_mm", "lev_taken", "hb_dve", "hb_act",
            "sc_mm", "sc_taken", "idx_ready", "gate_in", "gate_exp", "tok_mm", "tok_out",
            "dots", "gelu", "diag", "v_used", "y_ready", "y_act", "y_out", "stored")}
        uv_in = [sem(f"uv_in{i}") for i in range(UV)]

        block = ctx.enter_context(nc.Block())

        def meet(eng, n):
            eng.drain().then_inc(phase, 1)
            eng.wait_ge(phase, 4 * n)

        ITEMS = [(tt, kind, hd) for tt in range(TT + 1) for kind in range(2) for hd in range(H)]

        def item(n):
            tt, kind, hd = ITEMS[n]
            q0, qn = (0, META) if tt == 0 else (META + P * (tt - 1), P)
            tiles = [0] if tt == 0 else [0] + ([tt - 1] if kind == 0 and tt > 1 else
                                               list(range(1, tt)) if kind == 1 else []) + [tt]
            segs, col = [], 0
            for t in tiles:
                k0, kn = (0, META) if t == 0 else (META + P * (t - 1), P)
                segs.append((t, k0, kn, col))
                col += kn
            half, tile = (hd // 4, hd % 4) if kind == 0 else (hd % 2, hd // 2)
            return tt, kind, hd, q0, qn, segs, col, slice(HD * half, HD * half + HD), tile

        uv = region(0, UV, 2 * D)
        at = UV * 2 * D
        sk = region(at, 2 * PH, NKEYS); at += 2 * PH * NKEYS
        qpk = region(at, 2 * PH, SEQ); at += 2 * PH * SEQ
        fin_g = region(at, D); at += D
        diag = region(at, UV, P); at += UV * P
        top_v = region(at, 4, TOPK); at += 4 * TOPK
        top_f = region(at, 4, TOPK); at += 4 * TOPK
        top_i = region(at, 4, TOPK).bitcast(U32); at += 4 * TOPK
        cand = region(at, 4 * TOPK * TOPK); at += 4 * TOPK * TOPK
        pair_sum = region(at, 2, TOPK * TOPK); at += 2 * TOPK * TOPK
        best = region(at, 2, TOPK); at += 2 * TOPK
        pos_u = region(at, 2, TOPK).bitcast(U32); at += 2 * TOPK
        pos_h = region(at, 2, 2 * TOPK).bitcast(U32); at += 4 * TOPK
        pos_f = region(at, 2, 2 * TOPK); at += 4 * TOPK
        e_hl = region(at, 2, PART); at += 2 * PART
        idxu = region(at, TT, PAIRS).bitcast(U32); at += TT * PAIRS
        gates = region(at, TT, PAIRS); at += TT * PAIRS
        assert at <= 8 * slot, at
        h2tok = [ring[:, i, :, :].rearrange("p a b -> p (a b)") for i in range(2)]
        outb, squares = (ring[:, i, :, :].rearrange("p a b -> p (a b)") for i in (2, 3))
        hdot = sb("hdot", [P, UV])
        hgel = sb("hgel", [P, UV])
        gsum = sb("gsum", [P, 2])

        @block.sync
        def _(sp):
            for j in range(RING):
                sp.dma_start(ring[:, j], weights[j].rearrange("p (k m) -> p k m", m=P)).then_inc(chunk_in[j], 16)
            with sp.Fori(0, (CHUNKS - RING) // RING) as i:
                for j in range(RING):
                    sp.wait_ge(chunk_done, i * RING + (j + 1))
                    sp.dma_start(ring[:, j], weights[bass.ds(i * RING + (RING + j), 1)].rearrange(
                        "o p (k m) -> (o p) k m", m=P)).then_inc(chunk_in[j], 16)
            for n in range(CHUNKS - CHUNKS % RING, CHUNKS):
                sp.wait_ge(chunk_done, n - RING + 1)
                sp.dma_start(ring[:, n % RING], weights[n].rearrange("p (k m) -> p k m", m=P)
                             ).then_inc(chunk_in[n % RING], 16)
            for t in range(TT):
                sp.wait_ge(s["y_out"], t + 1)
                sp.dma_start(out[t * P:(t + 1) * P, :], outb).then_inc(s["stored"], 16)
            sp.wait_ge(s["stored"], 16 * TT)

        @block.tensor
        def _(pe):
            mm, tr = nc.tensor.matmul, nc.tensor.transpose
            count = {"chunk": 0, "evac": 0, "sq": 0, "norm": 0, "link": 0}

            def take():
                n = count["chunk"]
                count["chunk"] += 1
                pe.wait_ge(chunk_in[n % RING], 16 * (n // RING + 1))
                return ring[:, n % RING]

            def banks():
                n = count["evac"]
                count["evac"] += 1
                if n >= 3:
                    pe.wait_ge(evac, n - 2)
                return 2 * (n % 3)

            def project(tiles, src, width, base=0):
                for n in range(tiles):
                    w = take()
                    b = banks()
                    halves = 2 if width > 512 else 1
                    hw = width // halves
                    for half in range(halves):
                        for k in range(DT):
                            last = mm(ps[:, b + half, 0:hw], w[:, k, :],
                                      src[:, k, base + half * hw:base + half * hw + hw],
                                      start=(k == 0), stop=(k == DT - 1))
                    last.then_inc(chunk_done, 1)

            def token_major(tiles, src, meta):
                for n in range(tiles):
                    w = take()
                    b = banks()
                    if meta:
                        for k in range(DT):
                            mm(ps[0:META, b + 1, 0:P], src[:, k, 0:META], w[:, k, :], start=(k == 0), stop=(k == DT - 1))
                    for t in range(TT):
                        c0 = META + t * P
                        for k in range(DT):
                            last = mm(ps[:, b, t * P:(t + 1) * P], src[:, k, c0:c0 + P], w[:, k, :],
                                      start=(k == 0), stop=(k == DT - 1))
                    last.then_inc(chunk_done, 1)

            def sum_squares(src, width, base=0):
                count["sq"] += 1
                pe.wait_ge(sq_ready, count["sq"])
                halves = 2 if width > 512 else 1
                hw = width // halves
                for half in range(halves):
                    for k in range(DT):
                        last = mm(ps[:, 6 + half, 0:hw], ones, src[:, k, base + half * hw:base + half * hw + hw],
                                  start=(k == 0), stop=(k == DT - 1))
                last.then_inc(sumsq_ready, 1)

            def normed():
                count["norm"] += 1
                pe.wait_ge(norm_ready, count["norm"])

            pe.wait_ge(consts_in, 16 * 5)
            for half in range(2):
                last = mm(ps[0:H, half, :], param("rel")[0:BUCKETS + 1, :], toe_c[0:BUCKETS + 1, half * 512:half * 512 + 512],
                          start=True, stop=True)
            last.then_inc(toe_ready, 1)
            sum_squares(n_all, L)
            normed()
            pe.wait_ge(evac, 1)
            count["evac"] = 1
            for half in range(2):
                for k in range(DT):
                    last = mm(ps[0:H, 6 + half, 0:HL], w_f[:, k, :], n_all[:, k, half * HL:half * HL + HL],
                              start=(k == 0), stop=(k == DT - 1))
            last.then_inc(f_ready, 1)
            project(13, n_all, L)
            meet(pe, 1)
            token_major(5, n_all, True)
            pe.wait_ge(evac, TILE["out1"])
            pe.wait_ge(bias_in, 16 * (TT + 2))
            flip = const("flip")
            flat_w = bias_wr.rearrange("p h k -> p (h k)")
            flat_m = bias_mr.rearrange("p t h m -> p (t h m)")
            for j in range(4):
                mm(ps[:, j, :], flip, flat_w[:, j * 512:j * 512 + 512], start=True, stop=True)
            mm(ps[:, 4, :], flip, flat_m[:, P:5 * P], start=True, stop=True)
            mm(ps[0:META, 5, 0:P], flip[0:META, P - META:P], flat_m[0:META, 0:P], start=True, stop=True
               ).then_inc(toe_ready, 1)
            meet(pe, 2)

            def scores(n):
                tt, kind, hd, q0, qn, segs, cols, rws, tile = item(n)
                if n >= 2:
                    pe.wait_ge(scores_taken, n - 1)
                q = qk1[rws, tile + (0 if kind == 0 else 5), q0:q0 + qn]
                b = 2 * (n % 2)
                if kind == 0:
                    runs = [(0, META, 0)] + ([(segs[1][1], cols - META, META)] if tt else [])
                    for k0, kn, c0 in runs:
                        last = mm(ps[0:qn, b, c0:c0 + kn], q, qk1[rws, 4, k0:k0 + kn], start=True, stop=True)
                else:
                    for k0 in range(0, cols, 512):
                        kn = min(512, cols - k0)
                        mm(ps[0:qn, b + k0 // 512, 0:kn], q, qk1[rws, 9 + tile, k0:k0 + kn], start=True, stop=False)
                        last = mm(ps[0:qn, b + k0 // 512, 0:kn], sel[0:H, hd, 0:qn], negcum[0:H, k0:k0 + kn],
                                  start=False, stop=True)
                last.then_inc(scores_ready, 1)

            def turn(n):
                tt, kind, hd, q0, qn, segs, cols, rws, tile = item(n)
                pe.wait_ge(probs_ready, n + 1)
                if n >= 1:
                    pe.wait_ge(probsT_taken, n)
                for j, (t, k0, kn, c0) in enumerate(segs):
                    last = tr(ps[0:kn, 4 + j // 4, (j % 4) * P:(j % 4) * P + qn], prob[0:qn, n % 4, c0:c0 + kn],
                              ident[0:qn, 0:qn])
                last.then_inc(probsT_ready, 1)

            def weigh(n):
                tt, kind, hd, q0, qn, segs, cols, rws, tile = item(n)
                pe.wait_ge(probsT_taken, n + 1)
                if n >= 2:
                    pe.wait_ge(mixed_taken, n - 1)
                v0 = HD * (hd // 4) if kind == 0 else P + HD * hd
                for j, (t, k0, kn, c0) in enumerate(segs):
                    last = mm(ps[rws, 6 + n % 2, 0:qn], v1[0:kn, t, v0:v0 + HD], probT[0:kn, n % 2, j * P:j * P + qn],
                              start=(j == 0), stop=(j == len(segs) - 1))
                last.then_inc(mixed, 1)

            for n in range(len(ITEMS) + 3):
                if n < len(ITEMS):
                    scores(n)
                if 2 <= n < len(ITEMS) + 2:
                    turn(n - 2)
                if n >= 3:
                    weigh(n - 3)
            meet(pe, 3)
            project(8, mix1, L)
            sum_squares(n_all, L)
            meet(pe, 4)
            sum_squares(n_all, L)
            normed()
            c0 = count["chunk"]
            with pe.Fori(0, FT // 2) as i:
                for j in range(4):
                    w = ring[:, (c0 + j) % RING]
                    pe.wait_ge(chunk_in[(c0 + j) % RING], (i + ((c0 + j) // RING + 1)) * 16)
                    if j % 2 == 0:
                        pe.wait_ge(ff_done, i * 2 + (j // 2 + 1))
                    for half in range(2):
                        for k in range(DT):
                            last = mm(ps[:, 2 * j + half, 0:HL], w[:, k, :], n_all[:, k, half * HL:half * HL + HL],
                                      start=(k == 0), stop=(k == DT - 1))
                    last.then_inc(chunk_done, 1)
            count["chunk"] += 2 * FT
            meet(pe, 5)
            for m in range(DT):
                b = banks()
                for c in range(DOWN_CH):
                    w = take()
                    for k in range(c * DT, min(c * DT + DT, FT)):
                        for half in range(2):
                            last = mm(ps[:, b + half, 0:HL], w[:, k - c * DT, :],
                                      ff[:, k, half * HL:half * HL + HL], start=(k == 0), stop=(k == FT - 1))
                    last.then_inc(chunk_done, 1)
            sum_squares(n_all, L)
            meet(pe, 6)

            sum_squares(n_all, SEQ, META)
            normed()
            for w, b in ((w_beta, 6), (w_alpha, 7)):
                for k in range(DT):
                    last = mm(ps[0:H, b, :], w[:, k, :], n_all[:, k, META:L], start=(k == 0), stop=(k == DT - 1))
            last.then_inc(s["small_mm"], 1)
            project(24, n_all, SEQ, META)
            meet(pe, 7)
            norm_tiles = 0

            def head_sums(tiles):
                nonlocal norm_tiles
                for n in range(tiles):
                    pe.wait_ge(s["l2_sq"], norm_tiles + 1)
                    if n >= 2:
                        pe.wait_ge(s["l2_rstd"], norm_tiles - 1)
                    mm(ps[:, n % 2, :], ones, gtmp[:, n % 2, 0:SEQ], start=True, stop=True).then_inc(s["l2_sum"], 1)
                    norm_tiles += 1

            head_sums(16)
            pe.wait_ge(s["row_dve"], 5)
            for t in range(TT):
                last = tr(ps[:, 2, t * P:(t + 1) * P], rows[:, t * P:(t + 1) * P], ident)
            last.then_inc(s["rowT_ready"], 1)
            meet(pe, 8)
            bc = 0
            for which in range(3):
                src = (rowE, rowG, rows)[which]
                for hd in range(H):
                    if bc >= 4:
                        pe.wait_ge(s["bc_taken"], bc - 3)
                    mm(ps[:, bc % 4, :], sel[0:H, hd, :], src[0:H, :], start=True, stop=True).then_inc(s["bc_ready"], 1)
                    bc += 1
                if which == 1:
                    for hd in range(H):
                        last = mm(ps[:, 6, hd * NC:(hd + 1) * NC], sel[0:H, hd, :],
                                  rowE[0:H, C - 1:SEQ:C], start=True, stop=True)
                    last.then_inc(s["small_mm"], 1)
                    QT, KT = tokens(0), tokens(1)
                    for g in range(8):
                        t = g // 2
                        if g >= 2:
                            pe.wait_ge(s["kk_taken"], g - 1)
                        for j in range(4):
                            kk = KT[:, 4 * (g % 2) + j, t * P:(t + 1) * P]
                            last = mm(ps[:, 4 + g % 2, j * P:(j + 1) * P], kk, kk, start=True, stop=True)
                        last.then_inc(s["kk_ready"], 1)
            for g in range(8):
                t = g // 2
                pe.wait_ge(s["kk_taken"], 8 + g - 1)
                for j in range(4):
                    hd = 4 * (g % 2) + j
                    last = mm(ps[:, 4 + g % 2, j * P:(j + 1) * P], KT[:, hd, t * P:(t + 1) * P],
                              QT[:, hd, t * P:(t + 1) * P], start=True, stop=True)
                last.then_inc(s["kk_ready"], 1)
            meet(pe, 9)
            turned = 0

            def turn_groups(groups, source, banks=(0, 1)):
                nonlocal turned
                for g in range(groups):
                    if g >= 2:
                        pe.wait_ge(s["tr_taken"], turned - 1)
                    for j in range(4):
                        last = tr(ps[:, banks[g % 2], j * P:(j + 1) * P], source(g, j), ident)
                    last.then_inc(s["tr_ready"], 1)
                    turned += 1

            def by_token(T_):
                return lambda g, j: T_[:, 4 * (g % 2) + j, (g // 2) * P:(g // 2 + 1) * P]

            turn_groups(8, by_token(tokens(2)))
            pe.wait_ge(s["tr_taken"], 8)
            turn_groups(8, by_token(KT))
            meet(pe, 10)
            X, XT, T1, LT = blocks(1), blocks(2), blocks(8), blocks(5)
            def grp(A, g, j):
                return A[:, g // 2, 4 * (g % 2) + j, :]
            pe.wait_ge(s["inv_set"], 1)
            turn_groups(8, lambda g, j: grp(XT, g, j))
            pe.wait_ge(s["tr_taken"], 24)
            for lv in range(1, len(LEVELS)):
                last_level = lv == len(LEVELS) - 1
                for g in range(8):
                    pe.wait_ge(s["inv_mask"], 8 * (lv - 1) + g + 1)
                    n = 8 * (lv - 1) + g
                    if n >= 2:
                        pe.wait_ge(s["inv_t_taken"], n - 1)
                    if lv > 1:
                        pe.wait_ge(s["inv_x_taken"], 8 * (lv - 2) + g + 1)
                    for j in range(4):
                        last = mm(ps[:, g % 2, j * P:(j + 1) * P], gtmp[:, g % 2, j * P:(j + 1) * P], grp(X, g, j), start=True, stop=True)
                    last.then_inc(s["inv_t"], 1)
                for g in range(8):
                    n = 8 * (lv - 1) + g
                    pe.wait_ge(s["inv_t_taken"], n + 1)
                    if n >= 2:
                        pe.wait_ge(s["inv_x_taken"], n - 1)
                    for j in range(4):
                        if not last_level:
                            mm(ps[:, 2 + g % 2, j * P:(j + 1) * P], grp(XT, g, j), grp(T1, g, j), start=True, stop=True)
                        last = mm(ps[:, 4 + g % 2, j * P:(j + 1) * P], grp(T1, g, j), grp(XT, g, j), start=True, stop=True)
                    last.then_inc(s["inv_x"], 1)
            meet(pe, 11)
            VB, KG, KD = blocks(6), blocks(7), blocks(0)
            for g in range(8):
                if g >= 2:
                    pe.wait_ge(s["uw_taken"], g - 1)
                for j in range(4):
                    mm(ps[:, g % 2, j * P:(j + 1) * P], grp(XT, g, j), grp(VB, g, j), start=True, stop=True)
                    last = mm(ps[:, 2 + g % 2, j * P:(j + 1) * P], grp(KG, g, j), grp(XT, g, j), start=True, stop=True)
                last.then_inc(s["uw_ready"], 1)
            meet(pe, 12)
            QD, AT, WT = tokens(3), blocks(4), blocks(1)
            for c in range(NC):
                t, r = c // 2, slice(C * (c % 2), C * (c % 2) + C)
                for g in range(2):
                    n = 2 * c + g
                    pe.wait_ge(s["state_ready"], n + 1)
                    for j in range(4):
                        hd = 4 * g + j
                        last = mm(ps[r, g, j * P:(j + 1) * P], WT[:, t, hd, r], state[:, hd, :], start=True, stop=True)
                    last.then_inc(s["ks_ready"], 1)
                for g in range(2):
                    n = 2 * c + g
                    pe.wait_ge(s["vnew_ready"], n + 1)
                    if n >= 2:
                        pe.wait_ge(s["o_taken"], n - 1)
                    for j in range(4):
                        hd = 4 * g + j
                        mm(ps[:, 2 + g, j * C:(j + 1) * C], state[:, hd, :], QD[:, hd, c * C:(c + 1) * C],
                           start=True, stop=False)
                        mm(ps[:, 2 + g, j * C:(j + 1) * C], vnew[r, hd, :], AT[r, t, hd, r], start=False, stop=True)
                    for j in range(4):
                        hd = 4 * g + j
                        last = mm(ps[:, 4 + g, j * P:(j + 1) * P], KD[r, t, hd, :], vnew[r, hd, :], start=True, stop=True)
                    last.then_inc(s["os_ready"], 1)
            meet(pe, 13)
            head_sums(8)
            meet(pe, 14)
            project(8, n_all, SEQ, META)
            meet(pe, 15)
            project(8, tokens(8), SEQ)
            project(8, n_all, SEQ, META)
            meet(pe, 16)
            project(8, n_all, SEQ, META)
            token_major(8, n_all, False)
            project(8, n_all, SEQ, META)
            meet(pe, 17)
            QB, KB, QL, KL = tokens(6), tokens(3), tokens(0), tokens(8)
            for lv in range(len(LEVELS) + 1):
                if lv:
                    pe.wait_ge(s["lev_k"], lv)
                    pe.wait_ge(s["lev_q"], lv)
                for g in range(8):
                    n = 8 * lv + g
                    if n >= 4:
                        pe.wait_ge(s["lev_taken"], n - 3)
                    for j in range(4):
                        hd, cs = 4 * (g % 2) + j, slice((g // 2) * P, (g // 2 + 1) * P)
                        last = mm(ps[:, g % 4, j * P:(j + 1) * P], (KL if lv else KB)[:, hd, cs],
                                  (QL if lv else QB)[:, hd, cs], start=True, stop=True)
                    last.then_inc(s["lev_mm"], 1)
            pe.wait_ge(s["hb_dve"], 2)
            turn_groups(8, by_token(KL), (4, 5))
            meet(pe, 18)
            AT2, QE, VI, KD2 = blocks(2), tokens(7), blocks(5), blocks(0)
            for c in range(NC):
                t, r = c // 2, slice(C * (c % 2), C * (c % 2) + C)
                for g in range(2):
                    n = 2 * c + g
                    pe.wait_ge(s["state_ready"], 18 + n + 1)
                    pe.wait_ge(s["o_taken"], 16 + n - 1 if n >= 2 else 16)
                    for j in range(4):
                        hd = 4 * g + j
                        mm(ps[:, 2 + g, j * C:(j + 1) * C], state[:, hd, :], QE[:, hd, c * C:(c + 1) * C],
                           start=True, stop=False)
                        mm(ps[:, 2 + g, j * C:(j + 1) * C], VI[r, t, hd, :], AT2[r, t, hd, r], start=False, stop=True)
                    for j in range(4):
                        hd = 4 * g + j
                        last = mm(ps[:, 4 + g, j * P:(j + 1) * P], KD2[r, t, hd, :], VI[r, t, hd, :], start=True, stop=True)
                    last.then_inc(s["os_ready"], 1)
            meet(pe, 19)
            head_sums(8)
            meet(pe, 20)
            project(8, n_all, SEQ, META)
            meet(pe, 21)
            project(8, tokens(3), SEQ)
            project(8, n_all, SEQ, META)
            meet(pe, 22)
            project(8, tokens(1), SEQ)
            meet(pe, 23)
            sum_squares(n_all, SEQ, META)
            normed()
            project(16, n_all, SEQ, META)
            meet(pe, 24)
            def key_scores(n):
                t, part = n // PARTS, n % PARTS
                if n >= 2:
                    pe.wait_ge(s["sc_taken"], n - 1)
                for j in range(4):
                    last = mm(ps[:, 4 + n % 2, j * P:(j + 1) * P], qpk[:, 4 * part + j, t * P:(t + 1) * P],
                              sk[:, 4 * part + j, :], start=True, stop=True)
                last.then_inc(s["sc_mm"], 1)

            def by_tokens(t):
                if t >= 1:
                    pe.wait_ge(s["tok_out"], 2 * t)
                for half in range(2):
                    for j in range(4):
                        last = tr(ps[:, 6 + half, j * P:(j + 1) * P],
                                  n_all[:, 4 * half + j, META + t * P:META + (t + 1) * P], ident)
                last.then_inc(s["tok_mm"], 1)

            key_scores(0)
            key_scores(1)
            by_tokens(0)
            for n in range(NPARTS):
                t = n // PARTS
                yb = 2 * (t % 2)
                if n + 2 < NPARTS:
                    key_scores(n + 2)
                if n % PARTS == 0:
                    if t >= 2:
                        pe.wait_ge(s["y_out"], t - 1)
                    for half in range(2):
                        for j in range(3):
                            mm(ps[:, yb + half, :], h_all[:, 4 * half + j, META + t * P:META + (t + 1) * P],
                               wide[:, (3 - j) * P:(7 - j) * P], start=(j == 0), stop=False)
                    if t + 1 < TT:
                        by_tokens(t + 1)
                with pe.Fori(0, PART // UV) as i:
                    for j in range(UV):
                        pe.wait_ge(s["diag"], (i * UV) + (n * PART + j + 1))
                        for half in range(2):
                            last = mm(ps[:, yb + half, :], diag[:, j, :], uv[:, j, D + half * 512:D + half * 512 + 512],
                                      start=False, stop=False)
                        last.then_inc(s["v_used"], 1)
                if n % PARTS == PARTS - 1:
                    for half in range(2):
                        last = mm(ps[:, yb + half, :], h_all[:, 4 * half + 3, META + t * P:META + (t + 1) * P],
                                  wide[:, 0:4 * P], start=False, stop=True)
                    last.then_inc(s["y_ready"], 1)

        @block.scalar
        def _(act):
            fn = nc.scalar.activation
            count = {"chunk": 0, "sumsq": 0, "link": 0, "gated": 0, "ltile": 0}

            def link(ins):
                count["link"] += 1
                ins.then_inc(act_link, 1)
                act.wait_ge(act_link, count["link"])

            def tile():
                count["chunk"] += 1
                act.wait_ge(chunk_done, count["chunk"])

            def square(dst, src):
                fn(dst, src, ACT.Square).then_inc(sq_ready, 1)

            def inverse_root(width):
                count["sumsq"] += 1
                act.wait_ge(sumsq_ready, count["sumsq"])
                halves = 2 if width > 512 else 1
                hw = width // halves
                link(fn(rstd[:, 0:width].rearrange("p (a b) -> p a b", b=hw), ps[:, 6:6 + halves, 0:hw], ACT.Ln,
                        scale=1.0 / D, bias=small[:, 0:1]))
                fn(rstd[:, 0:width], rstd[:, 0:width], ACT.Exp, scale=-0.5).then_inc(rstd_ready, 1)

            def bank_of(name, n):
                return 2 * ((TILE[name] + n) % 3)

            def two(name, n):
                b = bank_of(name, n)
                return ps[:, b:b + 2, 0:HL]

            def view2(x):
                return x.rearrange("p (a b) -> p a b", b=HL)

            act.dma_start(con[:, :], consts).then_inc(consts_in, 16)
            act.dma_start(par[:, :], params).then_inc(consts_in, 16)
            act.dma_start(toe_c, toeplitz).then_inc(consts_in, 16)
            act.dma_start(h_all[:, :, :], xT.rearrange("(k p) t -> p k t", p=P)).then_inc(consts_in, 16)
            act.dma_start(sink, sinks.partition_broadcast(P)).then_inc(consts_in, 16)
            act.wait_ge(consts_in, 16 * 5)
            act.wait_ge(dve_link, 1)
            square(n_all[:, :, :], h_all[:, :, :])
            act.wait_ge(toe_ready, 1)
            fn(toe_r[0:H, :].rearrange("p (a b) -> p a b", b=512), ps[0:H, 0:2, :], ACT.Copy).then_inc(evac, 1)
            act.wait_ge(evac, 1)
            act.dma_start(scratch.ap(), toe_r[0:H, :]).then_inc(toe_out, 16)
            act.wait_ge(toe_out, 16)
            act.dma_start(bias_wr, bass.AP(scratch, 0, [[1, P], [TOE, H], [1, 2 * WIN]])).then_inc(bias_in, 16)
            for t in range(TT + 1):
                q0 = 0 if t == 0 else META + P * (t - 1)
                qn = META if t == 0 else P
                act.dma_start(bias_mr[0:qn, t], bass.AP(scratch, TOE_W + L - q0 - qn, [[1, qn], [TOE, H], [1, META]])
                              ).then_inc(bias_in, 16)
            inverse_root(L)
            act.wait_ge(f_ready, 1)
            fn(f_row[0:H, :].rearrange("p (a b) -> p a b", b=HL), ps[0:H, 6:8, 0:HL], ACT.Identity,
               bias=param("b_forget")[0:H, :]).then_inc(f_act, 1)
            act.wait_ge(f_dve, 1)
            link(fn(f_abs[0:H, :], f_abs[0:H, :], ACT.Exp, scale=-1.0))
            fn(f_abs[0:H, :], f_abs[0:H, :], ACT.Ln, bias=small[0:H, 1:2]).then_inc(f_act, 1)
            for n in range(13):
                tile()
                fn(view2(qk1[:, n, :]), two("in1", n), ACT.Copy,
                   scale=HD ** -0.5 if n < 4 or 5 <= n < 9 else 1.0).then_inc(evac, 1)
            meet(act, 1)
            for n in range(5):
                tile()
                b = bank_of("in1", 13 + n)
                fn(v1[0:META, 0, n * P:(n + 1) * P], ps[0:META, b + 1, 0:P], ACT.Copy)
                fn(v1[:, 1:5, n * P:(n + 1) * P], ps[:, b, :].rearrange("p (t m) -> p t m", m=P), ACT.Copy
                   ).then_inc(evac, 1)
            act.wait_ge(toe_ready, 2)
            fn(bias_w.rearrange("p (a c) k -> p a (c k)", c=2), ps[:, 0:4, :], ACT.Copy)
            fn(bias_m[:, 1:5].rearrange("p t h m -> p (t h m)"), ps[:, 4, :], ACT.Copy)
            fn(bias_m[0:META, 0].rearrange("p h m -> p (h m)"), ps[0:META, 5, 0:P], ACT.Copy)
            meet(act, 2)

            def exps(n):
                tt, kind, hd, q0, qn, segs, cols, rws, tl = item(n)
                act.wait_ge(logits_ready, n + 1)
                if n >= 4:
                    act.wait_ge(probsT_ready, n - 3)
                w = cols + (1 if kind == 0 else 0)
                fn(prob[0:qn, n % 4, 0:w], logit[0:qn, n % 2, 0:w], ACT.Exp, bias=small[0:qn, 32 + n % 4:33 + n % 4],
                   accum_out=small[0:qn, 36 + n % 4:37 + n % 4]).then_inc(exp_done, 1)

            def take_turned(n):
                tt, kind, hd, q0, qn, segs, cols, rws, tl = item(n)
                act.wait_ge(probsT_ready, n + 1)
                if n >= 2:
                    act.wait_ge(mixed, n - 1)
                flat = ps[:, 4:6, :].rearrange("p a b -> p (a b)")
                last = fn(probT[0:META, n % 2, 0:qn], flat[0:META, 0:qn], ACT.Copy)
                if len(segs) > 1:
                    last = fn(probT[:, n % 2, P:len(segs) * P], flat[:, P:len(segs) * P], ACT.Copy)
                last.then_inc(probsT_taken, 1)

            def take_mixed(n):
                tt, kind, hd, q0, qn, segs, cols, rws, tl = item(n)
                act.wait_ge(mixed, n + 1)
                fn(mix1[rws, tl + 4 * kind, q0:q0 + qn], ps[rws, 6 + n % 2, 0:qn], ACT.Copy).then_inc(mixed_taken, 1)

            for n in range(len(ITEMS) + 3):
                if n < len(ITEMS):
                    exps(n)
                if 2 <= n < len(ITEMS) + 2:
                    take_turned(n - 2)
                if n >= 3:
                    take_mixed(n - 3)
            meet(act, 3)
            for n in range(8):
                tile()
                fn(view2(y1[:, n, :]), two("out1", n), ACT.Copy).then_inc(evac, 1)
            act.wait_ge(evac, TILE["down"])
            square(n_all[:, :, :], y1)
            inverse_root(L)
            meet(act, 4)
            square(n_all[:, :, :], h_all[:, :, :])
            inverse_root(L)
            c0 = count["chunk"]
            with act.Fori(0, FT // 2) as i:
                for j in range(2):
                    act.wait_ge(chunk_done, i * 4 + (c0 + 2 * j + 1))
                    act.wait_ge(ff_done, i * 2 + (j + 1))
                    fn(view2(gtmp[:, j, :]), ps[:, 4 * j:4 * j + 2, 0:HL], ACT.Silu).then_inc(gated, 1)
            count["chunk"] += 2 * FT
            meet(act, 5)
            for n in range(DT):
                count["chunk"] += DOWN_CH
                act.wait_ge(chunk_done, count["chunk"])
                fn(view2(y1[:, n, :]), two("down", n), ACT.Copy).then_inc(evac, 1)
            act.wait_ge(evac, TILE["a_q"])
            square(n_all[:, :, :], y1)
            inverse_root(L)
            meet(act, 6)
            act.dma_start(h_rest.ap(), h_all[:, :, META:L]).then_inc(h_moved, 16)
            square(n_all[:, :, META:L], h_all[:, :, META:L])
            inverse_root(SEQ)
            act.wait_ge(s["small_mm"], 1)
            fn(rowY[0:H, :], ps[0:H, 6, :], ACT.Copy)
            fn(rowX[0:H, :], ps[0:H, 7, :], ACT.Identity, bias=param("dt_bias")[0:H, :]).then_inc(s["row_act"], 1)
            cx = region(B[3], 2, SEQ + 4)
            acc = region(B[4], 2, SEQ)
            dst3 = [tokens(0), tokens(1), tokens(2)]
            for n in range(25):
                if n < 24:
                    tile()
                    if n >= 2:
                        act.wait_ge(conv_done, n - 1)
                    fn(cx[:, n % 2, 3:3 + SEQ], ps[:, bank_of("a_q", n), :], ACT.Copy).then_inc(evac, 1)
                if n >= 1:
                    act.wait_ge(conv_done, n)
                    fn(dst3[(n - 1) // 8][:, (n - 1) % 8, :], acc[:, (n - 1) % 2, :], ACT.Silu).then_inc(silu_done, 1)
            meet(act, 7)
            norm_tiles = 0

            def head_norms(tiles, source, eps_col, scale):
                nonlocal norm_tiles
                base = norm_tiles

                def sq(n):
                    if n >= 2:
                        act.wait_ge(s["l2_sum"], base + n - 1)
                    fn(gtmp[:, n % 2, 0:SEQ], source(n), ACT.Square).then_inc(s["l2_sq"], 1)

                sq(0)
                for n in range(tiles):
                    if n + 1 < tiles:
                        sq(n + 1)
                    act.wait_ge(s["l2_sum"], base + n + 1)
                    if n >= 2:
                        act.wait_ge(s["l2_done"], base + n - 1)
                    r = normr[:, n % 2, :]
                    link(fn(r, ps[:, n % 2, :], ACT.Ln, scale=scale, bias=small[:, 0:1]))
                    fn(r, r, ACT.Exp, scale=-0.5).then_inc(s["l2_rstd"], 1)
                norm_tiles += tiles

            normr = region(B[3], 2, SEQ)
            head_norms(16, lambda n: tokens(n // 8)[:, n % 8, :], 0, 1.0)
            act.wait_ge(s["row_dve"], 1)
            link(fn(rows[0:H, :], rowY[0:H, :], ACT.Sigmoid))
            link(fn(rowE[0:H, :], rowE[0:H, :], ACT.Exp, scale=-1.0))
            link(fn(rowE[0:H, :], rowE[0:H, :], ACT.Ln, bias=small[0:H, 1:2]))
            fn(small[0:H, 4:5], param("a_log")[0:H, :], ACT.Exp).then_inc(s["row_act"], 1)
            act.wait_ge(s["row_dve"], 3)
            fn(rowE[0:H, :], rowG[0:H, :], ACT.Exp)
            fn(rows[64:64 + H, :], rowX[0:H, :], ACT.Exp).then_inc(s["row_act"], 1)
            act.wait_ge(s["rowT_ready"], 1)
            fn(rowT[:, :, :], ps[:, 2, :].rearrange("p (t r) -> p t r", r=P), ACT.Copy).then_inc(s["rowT_taken"], 1)
            meet(act, 8)
            DEC = blocks(4)
            act.wait_ge(s["small_mm"], 2)
            fn(glast[:, :, :], ps[:, 6, 0:H * NC].rearrange("p (h c) -> p h c", c=NC), ACT.Copy)
            act.wait_ge(s["dec_ready"], 1)
            for t in range(TT):
                fn(DEC[:, t], DEC[:, t], ACT.Exp).then_inc(s["dec_exp"], 1)
            meet(act, 9)
            VB, KG, KD = blocks(6), blocks(7), blocks(0)
            for g in range(8):
                act.wait_ge(s["tr_ready"], g + 1)
                for j in range(4):
                    hd = 4 * (g % 2) + j
                    last = fn(VB[:, g // 2, hd, :], ps[:, g % 2, j * P:(j + 1) * P], ACT.Copy,
                              scale=rowT[:, g // 2, hd:hd + 1])
                last.then_inc(s["tr_taken"], 1)
            for g in range(8):
                act.wait_ge(s["tr_ready"], 8 + g + 1)
                for j in range(4):
                    hd = 4 * (g % 2) + j
                    fn(KG[:, g // 2, hd, :], ps[:, g % 2, j * P:(j + 1) * P], ACT.Copy,
                       scale=rowT[:, g // 2, 32 + hd:33 + hd])
                    last = fn(KD[:, g // 2, hd, :], ps[:, g % 2, j * P:(j + 1) * P], ACT.Copy,
                              scale=rowT[:, g // 2, 64 + hd:65 + hd])
                last.then_inc(s["tr_taken"], 1)
            act.wait_ge(h_moved, 16)
            meet(act, 10)

            def quad(A, g):
                return A[:, g // 2, 4 * (g % 2):4 * (g % 2) + 4, :]

            def bank(b):
                return ps[:, b, :].rearrange("p (j m) -> p j m", m=P)

            X, XT, T1 = blocks(1), blocks(2), blocks(8)
            for g in range(8):
                act.wait_ge(s["tr_ready"], 16 + g + 1)
                fn(quad(X, g), bank(g % 2), ACT.Copy).then_inc(s["tr_taken"], 1)
            for lv in range(1, len(LEVELS)):
                for g in range(8):
                    n = 8 * (lv - 1) + g
                    act.wait_ge(s["inv_t"], n + 1)
                    if n >= 8:
                        act.wait_ge(s["inv_x"], n - 7)
                    fn(quad(T1, g), bank(g % 2), ACT.Copy).then_inc(s["inv_t_taken"], 1)
            meet(act, 11)
            U, WT = blocks(5), blocks(1)
            for g in range(8):
                act.wait_ge(s["uw_ready"], g + 1)
                fn(quad(U, g), bank(g % 2), ACT.Copy)
                fn(quad(WT, g), bank(2 + g % 2), ACT.Copy).then_inc(s["uw_taken"], 1)
            meet(act, 12)

            def outputs(OT, done):
                for n in range(2 * NC):
                    c, g = n // 2, n % 2
                    act.wait_ge(s["os_ready"], done + n + 1)
                    fn(OT[:, 4 * g:4 * g + 4, c * C:(c + 1) * C], ps[:, 2 + g, 0:4 * C].rearrange("p (j i) -> p j i", i=C),
                       ACT.Copy).then_inc(s["o_taken"], 1)

            OA = tokens(8)
            outputs(OA, 0)
            meet(act, 13)
            normr = region(B[3], 2, SEQ)
            head_norms(8, lambda n: OA[:, n, :], 0, 1.0 / P)
            meet(act, 14)

            def gates_of(name, func):
                for n in range(8):
                    tile()
                    at = TILE[name] + n
                    if n >= 2:
                        act.wait_ge(evac, at - 1)
                    fn(gtmp[:, at % 2, 0:SEQ], ps[:, bank_of(name, n), :], func).then_inc(gated, 1)

            def copies_of(name, target, func=ACT.Copy):
                for n in range(8):
                    tile()
                    fn(target[:, n, :], ps[:, bank_of(name, n), :], func).then_inc(evac, 1)

            gates_of("a_gate", ACT.Silu)
            meet(act, 15)
            YA = tokens(0)
            copies_of("branch_a", YA)
            gates_of("g_a", ACT.Sigmoid)
            meet(act, 16)
            FG, BC = tokens(2), tokens(4)
            link(fn(lbound[:, 2, :], lbound[:, 0, :], ACT.Exp))
            fn(lbound[:, 3, :], lbound[:, 1, :], ACT.Exp).then_inc(s["hb_act"], 1)
            gates_of("b_f", ACT.Sigmoid)
            act.wait_ge(evac, TILE["b_i"])
            VI = blocks(5)
            for n in range(8):
                tile()
                fn(VI[:, :, n, :], ps[:, bank_of("b_i", n), :].rearrange("p (t m) -> p t m", m=P), ACT.Copy
                   ).then_inc(evac, 1)
            copies_of("b_q", tokens(6), ACT.Silu)
            for n in range(8):
                fn(FG[:, n, :], FG[:, n, :], ACT.Ln).then_inc(s["hb_act"], 1)
            meet(act, 17)
            E = tokens(7)
            for lv in range(len(LEVELS)):
                act.wait_ge(s["lev_diff"], lv + 1)
                fn(E, E, ACT.Exp).then_inc(s["lev_exp"], 1)
            act.wait_ge(s["hb_dve"], 1)
            fn(E, E, ACT.Exp).then_inc(s["lev_exp"], 1)
            KD2 = blocks(0)
            for g in range(8):
                act.wait_ge(s["tr_ready"], 24 + g + 1)
                fn(quad(KD2, g), bank(4 + g % 2), ACT.Copy).then_inc(s["tr_taken"], 1)
            act.wait_ge(s["hb_dve"], 2)
            fn(glast[:, :, :], BC[:, :, C - 1:SEQ:C], ACT.Exp)
            fn(E, BC, ACT.Exp).then_inc(s["lev_exp"], 1)
            meet(act, 18)
            act.dma_start(h_all[:, :, META:L], h_rest.ap()).then_inc(h_moved, 16)
            OBt = tokens(3)
            outputs(OBt, 16)
            meet(act, 19)
            normr = region(B[4], 2, SEQ)
            head_norms(8, lambda n: OBt[:, n, :], 0, 1.0 / P)
            meet(act, 20)
            gates_of("b_gate", ACT.Sigmoid)
            meet(act, 21)
            copies_of("branch_b", YA)
            gates_of("g_b", ACT.Sigmoid)
            meet(act, 22)
            count["chunk"] += 8
            act.dma_start(sk, keys.rearrange("p (n k) -> p n k", k=NKEYS)).then_inc(consts_in, 16)
            meet(act, 23)
            square(n_all[:, :, META:L], h_all[:, :, META:L])
            inverse_root(SEQ)
            for n in range(16):
                tile()
                fn(qpk[:, n, :], ps[:, bank_of("pq", n), :], ACT.Copy).then_inc(evac, 1)
            act.dma_start(wide, placing).then_inc(consts_in, 16)
            act.wait_ge(consts_in, 16 * 7)
            act.dma_start(fin_g, final_norm.partition_broadcast(P)).then_inc(consts_in, 16)
            act.wait_ge(consts_in, 16 * 8)
            meet(act, 24)
            def gate_exp(n):
                act.wait_ge(s["gate_in"], n + 1)
                gt = gates[:, n // PARTS, (n % PARTS) * PART:(n % PARTS + 1) * PART]
                fn(gt, gt, ACT.Exp).then_inc(s["gate_exp"], 1)

            def tok_copy(t):
                act.wait_ge(s["tok_mm"], t + 1)
                if t >= 2:
                    act.wait_ge(s["dots"], (PAIRS // 2) * (t - 1))
                for half in range(2):
                    fn(h2tok[t % 2][:, half * 512:half * 512 + 512], ps[:, 6 + half, :], ACT.Copy).then_inc(s["tok_out"], 1)

            tok_copy(0)
            gate_exp(0)
            gate_exp(1)
            for n in range(NPARTS):
                t = n // PARTS
                if n % PARTS == 0 and t + 1 < TT:
                    tok_copy(t + 1)
                with act.Fori(0, PART // UV) as i:
                    for g in range(UV // 2):
                        act.wait_ge(s["dots"], i * (UV // 2) + (PART // 2 * n + g + 1))
                        fn(hgel[:, 2 * g:2 * g + 2], hdot[:, 2 * g:2 * g + 2], ACT.Gelu).then_inc(s["gelu"], 1)
                if n + 2 < NPARTS:
                    gate_exp(n + 2)
                if n % PARTS == PARTS - 1:
                    act.wait_ge(s["y_ready"], t + 1)
                    if t >= 1:
                        act.wait_ge(s["y_out"], t)
                    link(fn(squares, ps[:, 2 * (t % 2):2 * (t % 2) + 2, :].rearrange("p a b -> p (a b)"), ACT.Square,
                            accum_out=small[:, 40:41]))
                    link(fn(small[:, 41:42], small[:, 40:41], ACT.Ln, scale=1.0 / D, bias=small[:, 0:1]))
                    fn(small[:, 42:43], small[:, 41:42], ACT.Exp, scale=-0.5).then_inc(s["y_act"], 1)

        @block.vector
        def _(dve):
            v = nc.vector
            count = {"link": 0, "rstd": 0, "chunk": 0, "gated": 0}

            def link(ins):
                count["link"] += 1
                ins.then_inc(dve_link, 1)
                dve.wait_ge(dve_link, count["link"])

            def normalise(dst, src, gain, width):
                count["rstd"] += 1
                dve.wait_ge(rstd_ready, count["rstd"])
                for k in range(DT):
                    last = v.scalar_tensor_tensor(dst[:, k, :], src[:, k, :], gain[:, k:k + 1], rstd[:, 0:width],
                                                  ALU.mult, ALU.mult)
                last.then_inc(norm_ready, 1)

            def add_normed(src, gain, width):
                count["rstd"] += 1
                dve.wait_ge(rstd_ready, count["rstd"])
                for k in range(DT):
                    last = v.scalar_tensor_tensor(src[:, k, :], src[:, k, :], gain[:, k:k + 1], rstd[:, 0:width],
                                                  ALU.mult, ALU.mult)
                link(last)
                link(v.tensor_tensor(h_all[:, :, :], h_all[:, :, :], src, ALU.add))

            v.memset(small[:, 0:1], EPS)
            v.memset(small[:, 1:2], 1.0)
            link(v.memset(ones_row[0:H, :], 1.0))
            dve.wait_ge(consts_in, 16 * 5)
            normalise(n_all, h_all, param("ln_pre_mix"), L)
            dve.wait_ge(f_act, 1)
            v.scalar_tensor_tensor(f_abs[0:H, :], f_row[0:H, :], -1.0, f_row[0:H, :], ALU.mult, ALU.max
                                   ).then_inc(f_dve, 1)
            dve.wait_ge(f_act, 2)
            link(v.scalar_tensor_tensor(f_row[0:H, :], f_row[0:H, :], 0.0, f_abs[0:H, :], ALU.min, ALU.subtract))
            link(v.tensor_tensor_scan(f_abs[0:H, :], ones_row[0:H, :], f_row[0:H, :], 0.0, ALU.mult, ALU.add))
            v.tensor_scalar(negcum[0:H, :], f_abs[0:H, :], -1.0, None, ALU.mult)
            meet(dve, 1)
            meet(dve, 2)

            def logits(n):
                tt, kind, hd, q0, qn, segs, cols, rws, tl = item(n)
                dve.wait_ge(scores_ready, n + 1)
                if n >= 2:
                    dve.wait_ge(exp_done, n - 1)
                b = 2 * (n % 2)
                lg = logit[0:qn, n % 2, :]
                if kind == 0:
                    last = v.tensor_tensor(lg[:, 0:META], ps[0:qn, b, 0:META], bias_m[0:qn, tt, hd, :], ALU.add)
                    if tt:
                        wn = cols - META
                        last = v.tensor_tensor(lg[:, META:cols], ps[0:qn, b, META:cols],
                                               bias_w[:, hd, 2 * WIN - wn:2 * WIN], ALU.add)
                    last.then_inc(scores_taken, 1)
                    link(v.tensor_copy(lg[:, cols:cols + 1], sink[0:qn, hd:hd + 1]))
                    w = cols + 1
                else:
                    d0 = cols - qn
                    for a, e in ((0, min(d0, 512)),):
                        if e > a:
                            v.tensor_copy(lg[:, a:e], ps[0:qn, b, a:e])
                    for a, e in ((d0, min(cols, 512)), (max(512, d0), cols)):
                        if e > a:
                            last = v.tensor_tensor(lg[:, a:e], ps[0:qn, b + a // 512, a % 512:a % 512 + e - a],
                                                   causal[0:qn, a - d0:e - d0], ALU.add)
                    last.then_inc(scores_taken, 1)
                    w = cols
                dve.wait_ge(scores_taken, n + 1)
                mx = small[0:qn, 44 + n % 4:45 + n % 4]
                link(v.tensor_reduce(mx, lg[:, 0:w], AX, ALU.max))
                v.tensor_scalar(small[0:qn, 32 + n % 4:33 + n % 4], mx, -1.0, None, ALU.mult).then_inc(logits_ready, 1)

            def probs(n):
                tt, kind, hd, q0, qn, segs, cols, rws, tl = item(n)
                dve.wait_ge(exp_done, n + 1)
                inv = small[0:qn, 48 + n % 4:49 + n % 4]
                link(v.reciprocal(inv, small[0:qn, 36 + n % 4:37 + n % 4]))
                v.tensor_scalar(prob[0:qn, n % 4, 0:cols], prob[0:qn, n % 4, 0:cols], inv, None, ALU.mult
                                ).then_inc(probs_ready, 1)

            for n in range(len(ITEMS) + 1):
                if n < len(ITEMS):
                    logits(n)
                if n >= 1:
                    probs(n - 1)
            meet(dve, 3)
            add_normed(y1, param("ln_post_mix"), L)
            meet(dve, 4)
            normalise(n_all, h_all, param("ln_pre_ffn"), L)
            v.memset(small[:, 6:7], 0.0).then_inc(ff_done, 2)
            c0 = FIRST_OF["gate_up"]
            with dve.Fori(0, FT // 2) as i:
                for j in range(2):
                    dve.wait_ge(gated, i * 2 + (j + 1))
                    dve.wait_ge(chunk_done, i * 4 + (c0 + 2 * j + 2))
                    v.tensor_tensor(ff[:, bass.ds(i * 2 + j, 1), :].rearrange("p o (a b) -> p (o a) b", b=HL),
                                    gtmp[:, j, :].rearrange("p (a b) -> p a b", b=HL),
                                    ps[:, 4 * j + 2:4 * j + 4, 0:HL], ALU.mult).then_inc(ff_done, 1)
            count["gated"] = FT
            meet(dve, 5)
            add_normed(y1, param("ln_post_ffn"), L)
            meet(dve, 6)
            hx, hn = h_all[:, :, META:L], n_all[:, :, META:L]
            normalise(hn, hx, param("norm1"), SEQ)
            cx = region(B[3], 2, SEQ + 4)
            acc = region(B[4], 2, SEQ)
            link(v.memset(cx[:, :, 0:3], 0.0))
            for n in range(24):
                dve.wait_ge(evac, TILE["a_q"] + n + 1)
                if n >= 2:
                    dve.wait_ge(silu_done, n - 1)
                a = acc[:, n % 2, :]
                link(v.tensor_scalar(a, cx[:, n % 2, 0:SEQ], conv_w[:, n, 0:1], None, ALU.mult))
                for j in range(1, 4):
                    ins = v.scalar_tensor_tensor(a, cx[:, n % 2, j:j + SEQ], conv_w[:, n, j:j + 1], a, ALU.mult, ALU.add)
                    if j < 3:
                        link(ins)
                ins.then_inc(conv_done, 1)
            meet(dve, 7)
            norm_tiles = 0

            def head_scale(tiles, target, factor):
                nonlocal norm_tiles
                for n in range(tiles):
                    dve.wait_ge(s["l2_rstd"], norm_tiles + 1)
                    v.scalar_tensor_tensor(target(n), target(n), factor(n), normr[:, n % 2, :], ALU.mult, ALU.mult
                                           ).then_inc(s["l2_done"], 1)
                    norm_tiles += 1

            v.memset(rows[:, :], 0.0)
            v.scalar_tensor_tensor(rowE[0:H, :], rowX[0:H, :], -1.0, rowX[0:H, :], ALU.mult, ALU.max
                                   ).then_inc(s["row_dve"], 1)
            normr = region(B[3], 2, SEQ)
            head_scale(16, lambda n: tokens(n // 8)[:, n % 8, :], lambda n: P ** -0.5 if n < 8 else 1.0)
            dve.wait_ge(s["row_act"], 2)
            link(v.scalar_tensor_tensor(rowX[0:H, :], rowX[0:H, :], 0.0, rowE[0:H, :], ALU.max, ALU.add))
            link(v.tensor_scalar(rowX[0:H, :], rowX[0:H, :], small[0:H, 4:5], -1.0, ALU.mult, ALU.mult))
            v.tensor_tensor_scan(rowG[0:H, :], const("reset")[0:H, :], rowX[0:H, :], 0.0, ALU.mult, ALU.add
                                 ).then_inc(s["row_dve"], 1)
            dve.wait_ge(s["row_dve"], 2)
            g3 = rowG[0:H, :].rearrange("p (c i) -> p c i", i=C)
            v.tensor_tensor(rowX[0:H, :].rearrange("p (c i) -> p c i", i=C), g3[:, :, C - 1:C].to_broadcast([H, NC, C]), g3,
                            ALU.subtract).then_inc(s["row_dve"], 1)
            v.tensor_scalar(rows[96:96 + H, :], rowG[0:H, :], -1.0, None, ALU.mult).then_inc(s["row_dve"], 1)
            dve.wait_ge(s["row_act"], 3)
            v.tensor_tensor(rows[32:32 + H, :], rows[0:H, :], rowE[0:H, :], ALU.mult).then_inc(s["row_dve"], 1)
            meet(dve, 8)
            DEC, LT, QD = blocks(4), blocks(5), tokens(3)
            bc = 0
            for hd in range(H):
                dve.wait_ge(s["bc_ready"], bc + 1)
                v.tensor_tensor(QD[:, hd, :], tokens(0)[:, hd, :], ps[:, bc % 4, :], ALU.mult).then_inc(s["bc_taken"], 1)
                bc += 1
            for hd in range(H):
                dve.wait_ge(s["bc_ready"], bc + 1)
                for t in range(TT):
                    last = v.tensor_scalar(DEC[:, t, hd, :], ps[:, bc % 4, t * P:(t + 1) * P],
                                           rowT[:, t, 96 + hd:97 + hd], 0.0, ALU.add, ALU.min)
                last.then_inc(s["bc_taken"], 1)
                bc += 1
            dve.wait_ge(s["bc_taken"], bc)
            v.memset(small[0:H, 5:6], 0.0).then_inc(s["dec_ready"], 1)
            cmask = const("chunk_causal").unsqueeze(1).to_broadcast([P, H, P])
            for t in range(TT):
                dve.wait_ge(s["dec_exp"], t + 1)
                last = v.tensor_tensor(DEC[:, t], DEC[:, t], cmask, ALU.mult)
            link(last)

            def quad(A, g):
                return A[:, g // 2, 4 * (g % 2):4 * (g % 2) + 4, :]

            def bank(b):
                return ps[:, b, :].rearrange("p (j m) -> p j m", m=P)

            for g in range(8):
                dve.wait_ge(s["kk_ready"], g + 1)
                v.tensor_tensor(quad(LT, g), bank(4 + g % 2), quad(DEC, g), ALU.mult).then_inc(s["kk_taken"], 1)
            dve.wait_ge(s["kk_taken"], 8)
            for hd in range(H):
                dve.wait_ge(s["bc_ready"], bc + 1)
                v.tensor_tensor(LT[:, :, hd, :], LT[:, :, hd, :], ps[:, bc % 4, :].rearrange("p (t i) -> p t i", i=P),
                                ALU.mult).then_inc(s["bc_taken"], 1)
                bc += 1
            for g in range(8):
                dve.wait_ge(s["kk_ready"], 8 + g + 1)
                v.tensor_tensor(quad(DEC, g), bank(4 + g % 2), quad(DEC, g), ALU.mult).then_inc(s["kk_taken"], 1)
            meet(dve, 9)
            meet(dve, 10)
            X, XT = blocks(1), blocks(2)

            def masks(m, w):
                return level_mask[:, m:m + 1, :].to_broadcast([P, w, P])

            for t in range(TT):
                last = v.tensor_tensor(XT[:, t], LT[:, t], masks(0, H), ALU.mult)
            link(last)
            ib = ident.unsqueeze(1).to_broadcast([P, H, P])
            for t in range(TT):
                last = v.tensor_tensor(XT[:, t], ib, XT[:, t], ALU.subtract)
            last.then_inc(s["inv_set"], 1)
            for lv in range(1, len(LEVELS)):
                last_level = lv == len(LEVELS) - 1
                for g in range(8):
                    n = 8 * (lv - 1) + g
                    if n >= 2:
                        dve.wait_ge(s["inv_t"], n - 1)
                    v.tensor_tensor(gtmp[:, g % 2, 0:4 * P].rearrange("p (j m) -> p j m", m=P), quad(LT, g),
                                    masks(lv, 4), ALU.mult).then_inc(s["inv_mask"], 1)
                for g in range(8):
                    n = 8 * (lv - 1) + g
                    dve.wait_ge(s["inv_x"], n + 1)
                    if lv == 1 and g == 0:
                        dve.wait_ge(s["tr_taken"], 24)
                    if not last_level:
                        v.tensor_tensor(quad(X, g), quad(X, g), bank(2 + g % 2), ALU.subtract)
                    v.tensor_tensor(quad(XT, g), quad(XT, g), bank(4 + g % 2), ALU.subtract).then_inc(s["inv_x_taken"], 1)
            meet(dve, 11)
            v.memset(state[:, 0:4, :], 0.0).then_inc(s["state_ready"], 1)
            v.memset(state[:, 4:8, :], 0.0).then_inc(s["state_ready"], 1)
            meet(dve, 12)
            U = blocks(5)
            for c in range(NC):
                t, r = c // 2, slice(C * (c % 2), C * (c % 2) + C)
                for g in range(2):
                    n = 2 * c + g
                    dve.wait_ge(s["ks_ready"], n + 1)
                    if n >= 2:
                        dve.wait_ge(s["os_ready"], n - 1)
                    v.tensor_tensor(vnew[r, 4 * g:4 * g + 4, :], U[r, t, 4 * g:4 * g + 4, :],
                                    ps[r, g, :].rearrange("p (j m) -> p j m", m=P), ALU.subtract).then_inc(s["vnew_ready"], 1)
                for g in range(2):
                    n = 2 * c + g
                    dve.wait_ge(s["os_ready"], n + 1)
                    S = state[:, 4 * g:4 * g + 4, :]
                    link(v.tensor_tensor(S, S, glast[:, 4 * g:4 * g + 4, c:c + 1].to_broadcast([P, 4, P]), ALU.mult))
                    v.tensor_tensor(S, S, bank(4 + g), ALU.add).then_inc(s["state_ready"], 1)
            meet(dve, 13)
            OA = tokens(8)
            head_scale(8, lambda n: OA[:, n, :], lambda n: param("a_onorm"))
            meet(dve, 14)

            def gate(name, n):
                count["gated"] += 1
                dve.wait_ge(gated, count["gated"])
                return gtmp[:, (TILE[name] + n) % 2, 0:SEQ]

            for n in range(8):
                v.tensor_tensor(OA[:, n, :], OA[:, n, :], gate("a_gate", n), ALU.mult).then_inc(evac, 1)
            meet(dve, 15)
            YA, MX = tokens(0), tokens(1)
            for n in range(8):
                v.tensor_tensor(MX[:, n, :], YA[:, n, :], gate("g_a", n), ALU.mult).then_inc(evac, 1)
            p0, p1 = param("lower0"), param("lower1")
            link(v.tensor_tensor(lbound[:, 2, :], p0, p1, ALU.max))
            v.tensor_tensor(lbound[:, 0, :], p0, lbound[:, 2, :], ALU.subtract)
            v.tensor_tensor(lbound[:, 1, :], p1, lbound[:, 2, :], ALU.subtract)
            meet(dve, 16)
            dve.wait_ge(s["hb_act"], 1)
            link(v.tensor_tensor(lbound[:, 1, :], lbound[:, 2, :], lbound[:, 3, :], ALU.add))
            link(v.reciprocal(lbound[:, 1, :], lbound[:, 1, :]))
            link(v.tensor_tensor(lbound[:, 0, :], lbound[:, 2, :], lbound[:, 1, :], ALU.mult))
            link(v.tensor_scalar(lbound[:, 1, :], lbound[:, 0, :], -1.0, 1.0, ALU.mult, ALU.add))
            FG, KB, BC = tokens(2), tokens(3), tokens(4)
            for n in range(8):
                link(v.tensor_scalar(FG[:, n, :], gate("b_f", n), lbound[:, 1, n:n + 1], lbound[:, 0, n:n + 1],
                                     ALU.mult, ALU.add))
                v.tensor_scalar(KB[:, n, :], FG[:, n, :], -1.0, 1.0, ALU.mult, ALU.add).then_inc(evac, 1)
            for n in range(8):
                dve.wait_ge(s["hb_act"], 1 + n + 1)
                last = v.tensor_tensor_scan(BC[:, n, :], const("reset"), FG[:, n, :], 0.0, ALU.mult, ALU.add)
            meet(dve, 17)
            E, KL, QL, QB, AT2 = tokens(7), tokens(8), tokens(0), tokens(6), blocks(2)
            link(v.memset(region(B[2], slot), 0.0))

            def join(lv):
                mask = (ident.unsqueeze(1).to_broadcast([P, 4, P]) if lv == 0 else masks(lv - 1, 4)).bitcast(I32)
                for g in range(8):
                    dve.wait_ge(s["lev_mm"], 8 * lv + g + 1)
                    v.copy_predicated(quad(AT2, g), mask, bank(g % 4)).then_inc(s["lev_taken"], 1)

            join(0)
            for lv, m in enumerate(LEVELS):
                if lv:
                    dve.wait_ge(s["lev_q"], lv)
                b4 = BC.rearrange("p h (n w) -> p (h n) w", w=2 * m)
                e4 = E.rearrange("p h (n w) -> p (h n) w", w=2 * m)
                ref = b4[:, :, m - 1:m].to_broadcast([P, H * SEQ // (2 * m), m])
                v.tensor_tensor(e4[:, :, 0:m], ref, b4[:, :, 0:m], ALU.subtract)
                v.tensor_tensor(e4[:, :, m:2 * m], b4[:, :, m:2 * m], ref, ALU.subtract).then_inc(s["lev_diff"], 1)
                dve.wait_ge(s["lev_exp"], lv + 1)
                dve.wait_ge(s["lev_mm"], 8 * lv + 8)
                v.tensor_tensor(KL, KB, E, ALU.mult).then_inc(s["lev_k"], 1)
                join(lv + 1)
            dve.wait_ge(s["lev_q"], 6)
            b3 = BC.rearrange("p h (n w) -> p (h n) w", w=C)
            v.tensor_tensor(E.rearrange("p h (n w) -> p (h n) w", w=C), b3[:, :, C - 1:C].to_broadcast([P, H * NC, C]), b3,
                            ALU.subtract).then_inc(s["hb_dve"], 1)
            dve.wait_ge(s["lev_exp"], 7)
            v.tensor_tensor(KL, KB, E, ALU.mult).then_inc(s["hb_dve"], 1)
            dve.wait_ge(s["lev_exp"], 8)
            v.tensor_tensor(E, QB, E, ALU.mult)
            v.memset(state[:, 0:4, :], 0.0).then_inc(s["state_ready"], 1)
            v.memset(state[:, 4:8, :], 0.0).then_inc(s["state_ready"], 1)
            meet(dve, 18)
            for c in range(NC):
                for g in range(2):
                    n = 2 * c + g
                    dve.wait_ge(s["os_ready"], 16 + n + 1)
                    for j in range(4):
                        hd = 4 * g + j
                        last = v.scalar_tensor_tensor(state[:, hd, :], state[:, hd, :], glast[:, hd, c:c + 1],
                                                      ps[:, 4 + g, j * P:(j + 1) * P], ALU.mult, ALU.add)
                    last.then_inc(s["state_ready"], 1)
            meet(dve, 19)
            normr = region(B[4], 2, SEQ)
            OBt = tokens(3)
            head_scale(8, lambda n: OBt[:, n, :], lambda n: param("b_onorm"))
            meet(dve, 20)
            for n in range(8):
                v.tensor_tensor(OBt[:, n, :], OBt[:, n, :], gate("b_gate", n), ALU.mult).then_inc(evac, 1)
            meet(dve, 21)
            for n in range(8):
                g_ = gate("g_b", n)
                link(v.tensor_tensor(g_, YA[:, n, :], g_, ALU.mult))
                v.tensor_tensor(MX[:, n, :], MX[:, n, :], g_, ALU.add).then_inc(evac, 1)
            dve.wait_ge(h_moved, 32)
            meet(dve, 22)
            for n in range(8):
                dve.wait_ge(chunk_done, FIRST_OF["out2"] + n + 1)
                v.tensor_tensor(hx[:, n, :], hx[:, n, :], ps[:, 2 * ((TILE["out2"] + n) % 3), :], ALU.add).then_inc(evac, 1)
            meet(dve, 23)
            normalise(hn, hx, param("norm2"), SEQ)
            meet(dve, 24)
            it16 = const("iota16")
            NEGS = -3e38

            def retrieve(n):
                t, part = n // PARTS, n % PARTS
                cols = slice(part * PART, (part + 1) * PART)
                lists = range(4)
                rest = cand.rearrange("p (n k) -> p n k", n=4)[:, :, 0:NKEYS]
                score = ps[:, 4 + n % 2, :].rearrange("p (n k) -> p n k", n=4)
                dve.wait_ge(s["sc_mm"], n + 1)
                link([v.max(top_v[:, j, 0:8], score[:, j, :]) for j in lists][-1])
                for j in lists:
                    v.max_index(top_i[:, j, 0:8], top_v[:, j, 0:8], score[:, j, :])
                last = [v.match_replace(rest[:, j, :], top_v[:, j, 0:8], score[:, j, :], NEGS) for j in lists][-1]
                last.then_inc(s["sc_taken"], 1)
                dve.wait_ge(s["sc_taken"], n + 1)
                link([v.max(top_v[:, j, 8:16], rest[:, j, :]) for j in lists][-1])
                for j in lists:
                    v.max_index(top_i[:, j, 8:16], top_v[:, j, 8:16], rest[:, j, :])
                for p in range(2):
                    last = v.tensor_tensor(pair_sum[:, p, :].rearrange("p (i j) -> p i j", j=TOPK),
                                           top_v[:, 2 * p, :].unsqueeze(2).to_broadcast([P, TOPK, TOPK]),
                                           top_v[:, 2 * p + 1, :].unsqueeze(1).to_broadcast([P, TOPK, TOPK]), ALU.add)
                link(last)
                v.tensor_copy(top_f, top_i)
                link([v.max(best[:, p, 0:8], pair_sum[:, p, :]) for p in range(2)][-1])
                left = cand.rearrange("p (n k) -> p n k", n=4)
                for p in range(2):
                    v.max_index(pos_u[:, p, 0:8], best[:, p, 0:8], pair_sum[:, p, :])
                link([v.match_replace(left[:, p, :], best[:, p, 0:8], pair_sum[:, p, :], NEGS) for p in range(2)][-1])
                link([v.max(best[:, p, 8:16], left[:, p, :]) for p in range(2)][-1])
                for p in range(2):
                    last = v.max_index(pos_u[:, p, 8:16], best[:, p, 8:16], left[:, p, :])
                gt = gates[:, t, cols].rearrange("p (a b) -> p a b", b=TOPK)
                v.tensor_tensor(gt, best, best[:, :, 0:1].to_broadcast([P, 2, TOPK]), ALU.subtract).then_inc(s["gate_in"], 1)
                link(last)
                posf = pos_u.rearrange("p a b -> p (a b)")
                v.tensor_scalar(pos_h[:, 0, :], posf, 4, None, ALU.logical_shift_right)
                link(v.tensor_scalar(pos_h[:, 1, :], posf, TOPK - 1, None, ALU.bitwise_and))
                link(v.tensor_copy(pos_f, pos_h))
                hit = cand.rearrange("p (h q k) -> p h q k", h=2, k=TOPK)
                for half in range(2):
                    last = v.tensor_tensor(hit[:, half], pos_f[:, half, :].unsqueeze(2).to_broadcast([P, PART, TOPK]),
                                           it16.unsqueeze(1).to_broadcast([P, PART, TOPK]), ALU.is_equal)
                link(last)
                for half in range(2):
                    for p in range(2):
                        hp = hit[:, half, p * TOPK:(p + 1) * TOPK, :]
                        last = v.tensor_tensor(hp, hp, top_f[:, 2 * p + half, :].unsqueeze(1).to_broadcast([P, TOPK, TOPK]),
                                               ALU.mult)
                link(last)
                dve.wait_ge(s["gate_exp"], n + 1)
                v.tensor_reduce(gsum[:, :], gt, AX, ALU.add)
                link(v.tensor_reduce(e_hl.rearrange("p a b -> p (a b)"), hit.rearrange("p h q k -> p (h q) k"), AX, ALU.add))
                v.reciprocal(gsum[:, :], gsum[:, :])
                link(v.scalar_tensor_tensor(e_hl[:, 0, :], e_hl[:, 0, :], float(NKEYS), e_hl[:, 1, :], ALU.mult, ALU.add))
                v.tensor_copy(idxu[:, t, cols], e_hl[:, 0, :]).then_inc(s["idx_ready"], 1)
                link(v.tensor_tensor(gt, gt, gsum[:, :].unsqueeze(2).to_broadcast([P, 2, TOPK]), ALU.mult))

            def scale_out(t):
                dve.wait_ge(s["y_act"], t + 1)
                if t >= 1:
                    dve.wait_ge(s["stored"], 16 * t)
                v.scalar_tensor_tensor(outb, ps[:, 2 * (t % 2):2 * (t % 2) + 2, :].rearrange("p a b -> p (a b)"),
                                       small[:, 42:43], fin_g, ALU.mult, ALU.mult).then_inc(s["y_out"], 1)

            retrieve(0)
            retrieve(1)
            for n in range(NPARTS):
                t, part = n // PARTS, n % PARTS
                if part == 0:
                    dve.wait_ge(s["tok_out"], 2 * t + 2)
                with dve.Fori(0, PART // UV) as i:
                    for g in range(UV // 2):
                        for sl in (2 * g, 2 * g + 1):
                            dve.wait_ge(uv_in[sl], (i + (n * (PART // UV) + 1)) * 16)
                            last = v.scalar_tensor_tensor(uv[:, sl, 0:D], uv[:, sl, 0:D], 1.0, h2tok[t % 2], ALU.mult, ALU.mult,
                                                          accum_out=hdot[:, sl:sl + 1])
                        last.then_inc(s["dots"], 1)
                        dve.wait_ge(s["gelu"], i * (UV // 2) + (PART // 2 * n + g + 1))
                        for sl in (2 * g, 2 * g + 1):
                            v.tensor_scalar(diag[:, sl, :], ident, hgel[:, sl:sl + 1],
                                            gates[:, t, bass.ds(i * UV + (part * PART + sl), 1)], ALU.mult, ALU.mult
                                            ).then_inc(s["diag"], 1)
                if n + 2 < NPARTS:
                    retrieve(n + 2)
                if part == 0 and t >= 1:
                    scale_out(t - 1)
            scale_out(TT - 1)

        @block.gpsimd
        def _(pool):
            g_ = nc.gpsimd
            for n in range(1, 18):
                meet(pool, n)
            E, QL, QB = tokens(7), tokens(0), tokens(6)
            for lv in range(len(LEVELS)):
                pool.wait_ge(s["lev_exp"], lv + 1)
                pool.wait_ge(s["lev_mm"], 8 * lv + 8)
                g_.tensor_tensor(QL, QB, E, ALU.mult).then_inc(s["lev_q"], 1)
            for n in range(18, 25):
                meet(pool, n)
            for n in range(TT * PAIRS):
                if n % PART == 0:
                    pool.wait_ge(s["idx_ready"], n // PART + 1)
                if n >= UV:
                    pool.wait_ge(s["v_used"], n - UV + 1)
                e = n % PAIRS
                g_.indirect_dma_start(uv[:, n % UV, :], None, experts,
                                      bass.IndirectOffsetOnAxis(ap=idxu[:, n // PAIRS, e:e + 1], axis=0)
                                      ).then_inc(uv_in[n % UV], 16)


def shape_constants():
    con = np.zeros((P, CONST_W), np.float32)

    def put(name, value, rows=P):
        a, b = CONST[name]
        con[:rows, a:b] = value.reshape(rows, b - a)

    j, i = np.arange(P)[:, None], np.arange(P)[None, :]
    put("ident", (j == i).astype(np.float32))
    put("flip", (j + i == P - 1).astype(np.float32))
    put("ones", np.ones((P, P), np.float32))
    put("causal", np.where(i <= j, np.float32(0), np.float32(NEG)))
    same = j // C == i // C
    put("chunk_causal", (same & (j <= i)).astype(np.float32))
    put("level", np.stack([((j // (2 * m) == i // (2 * m)) & (j % (2 * m) < m) & (i % (2 * m) >= m)).astype(np.float32)
                           for m in LEVELS], 1))
    put("sel", np.repeat(np.eye(H, dtype=np.float32)[:, :, None], P, 2), H)
    put("reset", np.tile((np.arange(SEQ) % C != 0).astype(np.float32), (P, 1)))
    put("iota16", np.tile(np.arange(TOPK, dtype=np.float32), (P, 1)))
    placing = np.zeros((P, 7 * P), np.float32)
    placing[:, 3 * P:4 * P] = np.eye(P, dtype=np.float32)

    def bucket(n):
        exact = BUCKETS // 2
        if n < exact:
            return n
        return min(exact + int(np.log(n / exact) / np.log(MAX_DISTANCE / exact) * (BUCKETS - exact)), BUCKETS - 1)

    toe = np.zeros((P, TOE), np.float32)
    for x in range(TOE_W):
        d = 2 * WIN - 1 - x
        toe[bucket(d) if 0 <= d < WIN else BUCKETS, x] = 1
    for x in range(TOE_M):
        d = L - 1 - x
        toe[bucket(d) if d >= 0 else BUCKETS, TOE_W + x] = 1
    return con, placing, toe


def weight_stream(w_in, w_out, w_gate_up, w_down, w_in2, branch_a, branch_b, w_out2, w_pq):
    def chunks(w, cols=None):
        w = w if cols is None else w[:, cols]
        k, m = w.shape[0] // P, w.shape[1] // P
        return w.reshape(k, P, m, P).transpose(2, 1, 0, 3).reshape(m, P, k * P)

    heads = [4 * half + m for m in range(4) for half in range(2)]
    head_cols = np.concatenate([np.arange(HD * hd, HD * hd + HD) for hd in heads])
    kv = KV * HD
    q = H * HD
    o_ka, o_va, o_qb = q, q + kv, q + 2 * kv
    o_kb, o_vb = o_qb + q, o_qb + 2 * q
    order = np.concatenate([head_cols, np.arange(o_ka, o_va), np.arange(o_qb, o_vb), np.arange(o_va, o_qb),
                            np.arange(o_vb, o_vb + q)])
    rows = np.concatenate([head_cols, np.arange(q, 2 * q)])
    gate_up = np.stack([chunks(w_gate_up[:, :DFF]), chunks(w_gate_up[:, DFF:])], 1).reshape(2 * FT, P, D)
    down = np.zeros((DT, DOWN_CH * DT, P, P), np.float32)
    down[:, :FT] = w_down.reshape(FT, P, DT, P).transpose(2, 0, 1, 3)
    down = down.reshape(DT, DOWN_CH, DT, P, P).transpose(0, 1, 3, 2, 4).reshape(DT * DOWN_CH, P, D)
    a = [0, D, 2 * D, 3 * D, 3 * D + 2 * H]
    g0 = a[4]
    sec = lambda n: chunks(w_in2[:, g0 + n * D:g0 + (n + 1) * D])
    parts = [chunks(w_in, order), chunks(w_out[rows]), gate_up, down,
             chunks(w_in2[:, :3 * D]), sec(0), chunks(branch_a), sec(5),
             sec(1), sec(2), sec(3), sec(4), chunks(branch_b), sec(6), chunks(w_out2), chunks(w_pq)]
    stream = np.concatenate(parts)
    assert stream.shape == (CHUNKS, P, D)
    return stream


def small_parameters(w):
    par = np.zeros((P, PARAM_W), np.float32)

    def put(name, value):
        a, b = PARAM[name]
        value = value.reshape(value.shape[0], b - a)
        par[:value.shape[0], a:b] = value

    cols = lambda x: x.reshape(-1, P).T
    for name, src in (("ln_pre_mix", "ln_pre_mix"), ("ln_post_mix", "ln_post_mix"), ("ln_pre_ffn", "ln_pre_ffn"),
                      ("ln_post_ffn", "ln_post_ffn"), ("norm1", "norm1_2"), ("norm2", "norm2_2"),
                      ("a_onorm", "a_onorm_2"), ("b_onorm", "b_onorm_2")):
        put(name, cols(w[src]))
    put("lower0", cols(w["b_lower_bound_2"][0]))
    put("lower1", cols(w["b_lower_bound_2"][1]))
    put("conv", w["conv_a_2"][0].reshape(4, 24, P).transpose(2, 1, 0))
    put("b_forget", w["b_forget"].reshape(H, 1))
    put("a_log", w["a_log_2"].reshape(H, 1))
    put("dt_bias", w["dt_bias_2"].reshape(H, 1))
    put("rel", np.concatenate([w["rel_bias"], np.full((1, H), NEG, np.float32)]))
    rows8 = lambda x: x.reshape(DT, P, H).transpose(1, 0, 2)
    put("w_f", rows8(w["w_in"][0][:, -H:]))
    put("w_beta", rows8(w["w_in_2"][0][:, 3 * D:3 * D + H]))
    put("w_alpha", rows8(w["w_in_2"][0][:, 3 * D + H:3 * D + 2 * H]))
    return par


def kernel(**inputs):
    import concourse.bacc as bacc
    from concourse.bass_utils import run_bass_kernel_spmd

    w = {name: np.ascontiguousarray(a) for name, a in inputs.items()}
    con, placing, toe = shape_constants()
    arrays = {
        "xT": np.ascontiguousarray(np.concatenate([w["meta_tokens"], w["x"][0]]).T),
        "weights": weight_stream(w["w_in"][0], w["w_out"][0], w["w_gate_up"][0], w["w_down"][0], w["w_in_2"][0],
                                 w["w_branch_a_2"][0], w["w_branch_b_2"][0], w["w_out_2"][0], w["w_pq_2"][0]),
        "params": small_parameters(w),
        "consts": con,
        "placing": placing,
        "toeplitz": toe,
        "sinks": w["sinks"][0],
        "keys": np.ascontiguousarray(w["sub_keys_2"][0].transpose(3, 1, 0, 2)).reshape(P, 2 * PH * NKEYS),
        "final_norm": w["final_norm_2"],
        "experts": np.concatenate([w["expert_u_2"][0], w["expert_v_2"][0]], 1),
    }
    nc = bacc.Bacc("TRN2", target_bir_lowering=False, num_devices=1)
    args = [nc.dram_tensor(f"in_{n}", a.shape, F32, kind="ExternalInput").ap() for n, a in arrays.items()]
    out = nc.dram_tensor("out", (SEQ, D), F32, kind="ExternalOutput").ap()
    build(nc, *args, out)
    r = run_bass_kernel_spmd(nc, [{f"in_{n}": a for n, a in arrays.items()}], core_ids=[0])
    return r.results[0]["out"].reshape(1, SEQ, D)
```

```python
from contextlib import ExitStack

import numpy as np

import concourse.bass as bass
from concourse import mybir

F32 = mybir.dt.float32
F32R = mybir.dt.float32r
I32 = mybir.dt.int32
U32 = mybir.dt.uint32
ALU = mybir.AluOpType
ACT = mybir.ActivationFunctionType
AX = mybir.AxisListType.X

P = 128
D = 1024
DT = D // P
META = 16
SEQ = 512
L = META + SEQ
HL = L // 2
TT = SEQ // P
HD = 64
H = 8
KV = 2
WIN = 128
BUCKETS = 32
MAX_DISTANCE = 128
DFF = 2816
FT = DFF // P
EPS = 1e-6
NEG = -1e30
C = 64
NC = SEQ // C
LEVELS = [1, 2, 4, 8, 16, 32]
PH = 8
TOPK = 16
NKEYS = 128
NEXP = NKEYS * NKEYS
PAIRS = PH * TOPK
UV = 8
PARTS = 4
PART = PAIRS // PARTS
NPARTS = TT * PARTS
RING = 4
PAIR = 2
DOWN_CH = 3

STREAM = [("in1", 13 + 3 * PAIR), ("out1", 8), ("gate_up", 2 * FT), ("down", DT * DOWN_CH),
          ("a_q", 8), ("a_k", 8), ("a_v", 8), ("a_gate", 8), ("branch_a", 8), ("g_a", 8),
          ("b_f", 8), ("b_i", 8), ("b_q", 8), ("b_gate", 8), ("branch_b", 8), ("g_b", 8),
          ("out2", 8), ("pq", 16)]
CHUNKS = sum(n for _, n in STREAM)
TILE = {"toeplitz": 0}
_at = 1
for _name, _n in STREAM:
    TILE[_name] = _at
    _at += {"in1": 13 + 3, "gate_up": 0, "down": DT, "b_i": 8 // PAIR}.get(_name, _n)
FIRST_OF = {}
_at = 0
for _name, _n in STREAM:
    FIRST_OF[_name] = _at
    _at += _n

CONST = {}
_at = 0
for _name, _w in [("ident", P), ("flip", P), ("ones", P), ("causal", P), ("chunk_causal", P), ("level", P * len(LEVELS)),
                  ("sel", H * P), ("reset", SEQ), ("iota16", TOPK)]:
    CONST[_name] = (_at, _at + _w)
    _at += _w
CONST_W = _at
TOE_W = 2 * WIN + WIN - 1
TOE_M = L + META - 1
TOE = 1024
PARAM = {}
_at = 0
for _name, _w in [("ln_pre_mix", DT), ("ln_post_mix", DT), ("ln_pre_ffn", DT), ("ln_post_ffn", DT),
                  ("norm1", DT), ("norm2", DT), ("lower0", H), ("lower1", H), ("a_onorm", 1), ("b_onorm", 1),
                  ("conv", 24 * 4), ("b_forget", 1), ("a_log", 1), ("dt_bias", 1), ("rel", H),
                  ("w_f", DT * H), ("w_beta", DT * H), ("w_alpha", DT * H)]:
    PARAM[_name] = (_at, _at + _w)
    _at += _w
PARAM_W = _at


def build(nc, xT, weights, params, consts, placing, toeplitz, sinks, keys, final_norm, experts, out):
    with ExitStack() as ctx:
        def sb(name, shape, dt=F32):
            return ctx.enter_context(nc.sbuf_tensor(name, shape, dt))

        def sem(name):
            return ctx.enter_context(nc.semaphore(name))

        low_rest = nc.dram_tensor("low_rest", [P, DT, SEQ], F32, kind="Internal")
        h_rest = nc.dram_tensor("h_rest", [P, DT, SEQ], F32, kind="Internal")
        scratch = nc.dram_tensor("toeplitz_rows", [H, TOE], F32, kind="Internal")

        ps = ctx.enter_context(nc.psum_tensor("ps", [P, 8, 512], F32))
        def second_names(*spans):
            tensors, at = [], 0
            with ExitStack() as given_back:
                for name, first, tiles, width in spans:
                    if first > at:
                        given_back.enter_context(nc.sbuf_tensor("up_to_" + name, [P, first - at], F32R))
                    tensors.append(given_back.enter_context(nc.sbuf_tensor(name, [P, tiles, width], F32R)))
                    at = first + tiles * width
            return tensors

        at_hi = RING * D
        at_n = at_hi + PAIR * D
        at_arena = at_n + DT * L
        ring_r, w_hi, n_hi, *slots_r = second_names(
            ("ring_r", 0, RING * DT, P), ("w_hi", at_hi, PAIR * DT, P), ("n_hi", at_n, DT, L),
            *[(f"slot{n}_r", at_arena + n * DT * SEQ, DT, SEQ) for n in range(8)])
        ring_r = ring_r[:, :, :].rearrange("p (c k) m -> p c k m", k=DT)
        w_hi = w_hi[:, :, :].rearrange("p (c k) m -> p c k m", k=DT)
        mix1_lo, low1 = second_names(("mix1_lo", at_arena + 13 * L + 5 * 640, DT, L),
                                     ("low1", at_arena + 8 * DT * SEQ - DT * L, DT, L))
        ff_lo, ff_hi = second_names(("ff_lo", at_arena + DT * L, FT, L), ("ff_hi", at_arena + (DT + FT) * L, FT, L))
        ring = sb("ring", [P, RING, DT, P])
        w_hi_f = sb("w_hi_f", [P, PAIR, DT, P])
        n_all = sb("n_all", [P, DT, L])
        arena = sb("arena", [P, 8 * DT * SEQ])
        con = sb("con", [P, CONST_W])
        par = sb("par", [P, PARAM_W])
        h_all = sb("h_all", [P, DT, L])
        gtmp = sb("gtmp", [P, 2, L])
        small = sb("small", [P, 64])

        def const(name):
            a, b = CONST[name]
            return con[:, a:b]

        def param(name):
            a, b = PARAM[name]
            return par[:, a:b]

        ident, ones, causal = const("ident"), const("ones"), const("causal")
        level_mask = const("level").rearrange("p (l i) -> p l i", i=P)
        sel = const("sel").rearrange("p (h i) -> p h i", i=P)
        conv_w = param("conv").rearrange("p (t j) -> p t j", j=4)
        w_f = param("w_f").rearrange("p (k h) -> p k h", h=H)
        w_beta = param("w_beta").rearrange("p (k h) -> p k h", h=H)
        w_alpha = param("w_alpha").rearrange("p (k h) -> p k h", h=H)

        slot = DT * SEQ
        flat_h = h_all[:, :, :].rearrange("p k t -> p (k t)")

        def region(at, *shape):
            n = int(np.prod(shape))
            v = arena[:, at:at + n] if at < 8 * slot else flat_h[:, at - 8 * slot:at - 8 * slot + n]
            if len(shape) == 2:
                v = v.rearrange("p (a b) -> p a b", b=shape[1])
            if len(shape) == 3:
                v = v.rearrange("p (a b c) -> p a b c", b=shape[1], c=shape[2])
            return v

        B = [at * slot for at in range(9)]
        at = 0
        qk1 = region(at, 13, L); at += 13 * L
        v1 = region(at, 5, 640); at += 5 * 640
        mix1 = region(at, DT, L); at += DT * L
        bias_wr = region(at - DT * L, H, 2 * WIN)
        bias_mr = region(at - DT * L + H * 2 * WIN, 5, H, META)
        bias_w = region(at, H, 2 * WIN); at += H * 2 * WIN
        bias_m = region(at, 5, H, META); at += 5 * H * META
        logit = region(at, 2, L + 2); at += 2 * (L + 2)
        prob = region(at, 4, L + 2); at += 4 * (L + 2)
        probT = region(at, 2, 5 * P); at += 2 * 5 * P
        toe_c = region(at, TOE); at += TOE
        toe_r = region(at, TOE); at += TOE
        f_row = region(at, L); at += L
        f_abs = region(at, L); at += L
        negcum = region(at, L); at += L
        ones_row = region(at, L); at += L
        sink = region(at, H); at += H
        rstd = region(at, L); at += L
        rstd2 = region(B[4] + slot // 2, SEQ)
        assert at <= 8 * slot - DT * L
        full1 = region(13 * L + 5 * 640 + DT * L + 512, DT, L)
        y1_squares = region(8 * slot - DT * L, DT, L)
        y1 = region(0, DT, L)
        ff = region(DT * L, FT, L)
        assert (DT + 2 * FT) * L <= 8 * slot - DT * L
        def tokens(n):
            return region(B[n], DT, SEQ)

        def parts(n):
            return slots_r[n][:, :, :]

        def blocks(n):
            return region(B[n], TT, H, P)

        rows = region(B[6], SEQ)
        rowG, rowE = region(B[6] + SEQ, SEQ), region(B[6] + 2 * SEQ, SEQ)
        rowX, rowY = region(B[5], SEQ), region(B[5] + SEQ, SEQ)
        glast = sb("glast", [P, H, NC])
        state = sel
        vnew = sb("vnew", [P, H, P])
        rowT = vnew[:, 0:TT, :]
        wide = vnew[:, 0:7, :].rearrange("p a b -> p (a b)")
        lbound = sb("lbound", [P, 4, H])

        consts_in = sem("consts_in")
        keys_in = sem("keys_in")
        h_moved = sem("h_moved")
        toe_out = sem("toe_out")
        bias_in = sem("bias_in")
        chunk_in = [sem(f"chunk_in{i}") for i in range(RING)]
        chunk_done = sem("chunk_done")
        hi_ready = sem("hi_ready")
        w_ready = sem("w_ready")
        full_ready = sem("full_ready")
        xhi_ready = sem("xhi_ready")
        low_moved = sem("low_moved")
        ff_upper = sem("ff_upper")
        evac = sem("evac")
        phase = sem("phase")
        pe_link = sem("pe_link")
        act_link = sem("act_link")
        dve_link = sem("dve_link")
        sq_ready = sem("sq_ready")
        h_ready = sem("h_ready")
        sumsq_ready = sem("sumsq_ready")
        rstd_ready = sem("rstd_ready")
        norm_ready = sem("norm_ready")
        toe_ready = sem("toe_ready")
        f_ready = sem("f_ready")
        f_act = sem("f_act")
        f_dve = sem("f_dve")
        scores_ready = sem("scores_ready")
        scores_taken = sem("scores_taken")
        logits_ready = sem("logits_ready")
        exp_done = sem("exp_done")
        probs_ready = sem("probs_ready")
        probsT_ready = sem("probsT_ready")
        probsT_taken = sem("probsT_taken")
        mixed = sem("mixed")
        mixed_taken = sem("mixed_taken")
        gated = sem("gated")
        ff_done = sem("ff_done")
        conv_in = sem("conv_in")
        conv_done = sem("conv_done")
        silu_done = sem("silu_done")
        s = {name: sem(name) for name in (
            "l2_sq", "l2_sum", "l2_rstd", "l2_done", "small_mm", "row_act", "row_dve", "rowT_ready",
            "rowT_taken", "bc_ready", "bc_taken", "dec_ready", "dec_exp", "dec_done", "kk_ready", "kk_taken",
            "tr_ready", "tr_taken", "inv_set", "inv_t", "inv_t_taken", "inv_x", "inv_x_taken", "inv_mask",
            "uw_ready", "uw_taken", "ks_ready", "vnew_ready", "os_ready", "o_taken", "state_ready",
            "lev_diff", "lev_exp", "lev_k", "lev_q", "lev_mm", "lev_taken", "hb_dve", "hb_act",
            "sc_mm", "sc_taken", "idx_ready", "gate_in", "gate_exp", "tok_mm", "tok_out",
            "dots", "gelu", "diag", "v_used", "y_ready", "y_act", "y_out", "stored")}
        uv_in = [sem(f"uv_in{i}") for i in range(UV)]

        block = ctx.enter_context(nc.Block())

        def meet(eng, n):
            eng.drain().then_inc(phase, 1)
            eng.wait_ge(phase, 3 * n)

        ITEMS = [(tt, kind, hd) for tt in range(TT + 1) for kind in range(2) for hd in range(H)]

        def item(n):
            tt, kind, hd = ITEMS[n]
            q0, qn = (0, META) if tt == 0 else (META + P * (tt - 1), P)
            tiles = [0] if tt == 0 else [0] + ([tt - 1] if kind == 0 and tt > 1 else
                                               list(range(1, tt)) if kind == 1 else []) + [tt]
            segs, col = [], 0
            for t in tiles:
                k0, kn = (0, META) if t == 0 else (META + P * (t - 1), P)
                segs.append((t, k0, kn, col))
                col += kn
            half, tile = (hd // 4, hd % 4) if kind == 0 else (hd % 2, hd // 2)
            return tt, kind, hd, q0, qn, segs, col, slice(HD * half, HD * half + HD), tile

        uv = region(0, UV, 2 * D)
        at = UV * 2 * D
        sk = region(at, 2 * PH, NKEYS); at += 2 * PH * NKEYS
        qpk = region(at, 2 * PH, SEQ); at += 2 * PH * SEQ
        fin_g = region(at, D); at += D
        diag = region(at, UV, P); at += UV * P
        top_v = region(at, 4, TOPK); at += 4 * TOPK
        top_f = region(at, 4, TOPK); at += 4 * TOPK
        top_i = region(at, 4, TOPK).bitcast(U32); at += 4 * TOPK
        cand = region(at, 4 * TOPK * TOPK); at += 4 * TOPK * TOPK
        pair_sum = region(at, 2, TOPK * TOPK); at += 2 * TOPK * TOPK
        best = region(at, 2, TOPK); at += 2 * TOPK
        pos_u = region(at, 2, TOPK).bitcast(U32); at += 2 * TOPK
        pos_h = region(at, 2, 2 * TOPK).bitcast(U32); at += 4 * TOPK
        pos_f = region(at, 2, 2 * TOPK); at += 4 * TOPK
        e_hl = region(at, 2, PART); at += 2 * PART
        idxu = region(at, TT, PAIRS).bitcast(U32); at += TT * PAIRS
        gates = region(at, TT, PAIRS); at += TT * PAIRS
        assert at <= 8 * slot, at
        h2tok = [ring[:, i, :, :].rearrange("p a b -> p (a b)") for i in range(TT)]
        outb, squares = (w_hi_f[:, i, :, :].rearrange("p a b -> p (a b)") for i in range(2))
        hdot = sb("hdot", [P, UV])
        hgel = sb("hgel", [P, UV])
        gsum = sb("gsum", [P, 2])

        @block.sync
        def _(sp):
            for j in range(RING):
                sp.dma_start(ring[:, j], weights[j].rearrange("p (k m) -> p k m", m=P)).then_inc(chunk_in[j], 16)
            with sp.Fori(0, (CHUNKS - RING) // RING) as i:
                for j in range(RING):
                    sp.wait_ge(chunk_done, i * RING + (j + 1))
                    sp.dma_start(ring[:, j], weights[bass.ds(i * RING + (RING + j), 1)].rearrange(
                        "o p (k m) -> (o p) k m", m=P)).then_inc(chunk_in[j], 16)
            for n in range(CHUNKS - CHUNKS % RING, CHUNKS):
                sp.wait_ge(chunk_done, n - RING + 1)
                sp.dma_start(ring[:, n % RING], weights[n].rearrange("p (k m) -> p k m", m=P)
                             ).then_inc(chunk_in[n % RING], 16)
            for t in range(TT):
                sp.wait_ge(s["y_out"], t + 1)
                sp.dma_start(out[t * P:(t + 1) * P, :], outb).then_inc(s["stored"], 16)
            sp.wait_ge(s["stored"], 16 * TT)

        @block.tensor
        def _(pe):
            mm, tr = nc.tensor.matmul, nc.tensor.transpose
            count = {"chunk": 0, "evac": 0, "sq": 0, "norm": 0, "link": 0}

            def take():
                n = count["chunk"]
                count["chunk"] += 1
                pe.wait_ge(w_ready, n + 1)
                return w_hi[:, n % PAIR], ring_r[:, n % RING]

            def banks():
                n = count["evac"]
                count["evac"] += 1
                if n >= 3:
                    pe.wait_ge(evac, n - 2)
                return 2 * (n % 3)

            def three(out, x, y, start, stop):
                mm(out, x[0], y[0], start=start, stop=False)
                mm(out, x[0], y[1], start=False, stop=False)
                return mm(out, x[1], y[0], start=False, stop=stop)

            def project(tiles, src, width, fresh=False, after=None):
                for n in range(tiles):
                    w = take()
                    b = banks()
                    halves = 2 if width > 512 else 1
                    hw = width // halves
                    for half in range(halves):
                        cs = slice(half * hw, half * hw + hw)
                        for k in range(DT):
                            if fresh and n == 0 and half == 0:
                                count["norm"] += 1
                                pe.wait_ge(norm_ready, count["norm"])
                            last = three(ps[:, b + half, 0:hw], [p[:, k, :] for p in w], [x[:, k, cs] for x in src],
                                         k == 0, k == DT - 1)
                    last.then_inc(chunk_done, 1)
                    if after:
                        after(n)

            def token_major(tiles, src, meta):
                for n in range(tiles):
                    at = count["evac"]
                    count["evac"] += 1
                    pe.wait_ge(evac, at if meta or n == 0 else at - 1)
                    b = 0 if meta else 4 * (n % 2)
                    for c in range(PAIR):
                        w = [p.rearrange("p (k a) b -> p k (a b)", a=PAIR) for p in take()]
                        groups = [(ps[:, b + t, 0:256], slice(META * meta + t * P, META * meta + (t + 1) * P)) for t in range(TT)]
                        if meta:
                            groups.append((ps[0:META, 6 + n % 2, 0:256], slice(0, META)))
                        for out_, cs in groups:
                            for k in range(DT // PAIR):
                                last = three(out_, [x[:, c * DT // PAIR + k, cs] for x in src], [p[:, k, :] for p in w],
                                             c == 0 and k == 0, c == PAIR - 1 and k == DT // PAIR - 1)
                        last.then_inc(chunk_done, 1)
                pe.wait_ge(evac, count["evac"])

            def sum_tile(src, k):
                count["sq"] += 1
                pe.wait_ge(sq_ready, count["sq"])
                width = src.shape[-1]
                halves = 2 if width > 512 else 1
                hw = width // halves
                for half in range(halves):
                    last = mm(ps[:, 6 + half, 0:hw], ones, src[:, k, half * hw:half * hw + hw],
                              start=(k == 0), stop=(k == DT - 1))
                if k == DT - 1:
                    last.then_inc(sumsq_ready, 1)

            def sum_squares(src):
                for k in range(DT):
                    sum_tile(src, k)

            def sums_behind(src):
                def after(n):
                    if n >= 2:
                        sum_tile(src, n - 2)
                    if n == DT - 1:
                        sum_tile(src, n - 1)
                        sum_tile(src, n)
                return after

            pe.wait_ge(consts_in, 16 * 5)
            for half in range(2):
                last = mm(ps[0:H, half, :], param("rel")[0:BUCKETS + 1, :], toe_c[0:BUCKETS + 1, half * 512:half * 512 + 512],
                          start=True, stop=True)
            last.then_inc(toe_ready, 1)
            sum_squares(n_all)
            pe.wait_ge(evac, 1)
            count["evac"] = 1

            def forget_logits(n):
                if n:
                    return
                for half in range(2):
                    for k in range(DT):
                        last = mm(ps[0:H, 6 + half, 0:HL], w_f[:, k, :], full1[:, k, half * HL:half * HL + HL],
                                  start=(k == 0), stop=(k == DT - 1))
                last.then_inc(f_ready, 1)

            project(13, (n_hi, low1), L, True, forget_logits)
            meet(pe, 1)
            token_major(3, (n_hi, low1), True)
            pe.wait_ge(bias_in, 16 * (TT + 2))
            flip = const("flip")
            flat_w = bias_wr.rearrange("p h k -> p (h k)")
            flat_m = bias_mr.rearrange("p t h m -> p (t h m)")
            for j in range(4):
                mm(ps[:, j, :], flip, flat_w[:, j * 512:j * 512 + 512], start=True, stop=True)
            mm(ps[:, 4, :], flip, flat_m[:, P:5 * P], start=True, stop=True)
            mm(ps[0:META, 5, 0:P], flip[0:META, P - META:P], flat_m[0:META, 0:P], start=True, stop=True
               ).then_inc(toe_ready, 1)
            meet(pe, 2)

            def scores(n):
                tt, kind, hd, q0, qn, segs, cols, rws, tile = item(n)
                if n >= 2:
                    pe.wait_ge(scores_taken, n - 1)
                q = qk1[rws, tile + (0 if kind == 0 else 5), q0:q0 + qn]
                b = 2 * (n % 2)
                if kind == 0:
                    runs = [(0, META, 0)] + ([(segs[1][1], cols - META, META)] if tt else [])
                    for k0, kn, c0 in runs:
                        last = mm(ps[0:qn, b, c0:c0 + kn], q, qk1[rws, 4, k0:k0 + kn], start=True, stop=True)
                else:
                    for k0 in range(0, cols, 512):
                        kn = min(512, cols - k0)
                        mm(ps[0:qn, b + k0 // 512, 0:kn], q, qk1[rws, 9 + tile, k0:k0 + kn], start=True, stop=False)
                        last = mm(ps[0:qn, b + k0 // 512, 0:kn], sel[0:H, hd, 0:qn], negcum[0:H, k0:k0 + kn],
                                  start=False, stop=True)
                last.then_inc(scores_ready, 1)

            def turn(n):
                tt, kind, hd, q0, qn, segs, cols, rws, tile = item(n)
                pe.wait_ge(probs_ready, n + 1)
                if n >= 1:
                    pe.wait_ge(probsT_taken, n)
                for j, (t, k0, kn, c0) in enumerate(segs):
                    last = tr(ps[0:kn, 4 + j // 4, (j % 4) * P:(j % 4) * P + qn], prob[0:qn, n % 4, c0:c0 + kn],
                              ident[0:qn, 0:qn])
                last.then_inc(probsT_ready, 1)

            def weigh(n):
                tt, kind, hd, q0, qn, segs, cols, rws, tile = item(n)
                pe.wait_ge(probsT_taken, n + 1)
                if n >= 2:
                    pe.wait_ge(mixed_taken, n - 1)
                v0 = HD * (hd // 4) if kind == 0 else P + HD * hd
                for j, (t, k0, kn, c0) in enumerate(segs):
                    last = mm(ps[rws, 6 + n % 2, 0:qn], v1[0:kn, t, v0:v0 + HD], probT[0:kn, n % 2, j * P:j * P + qn],
                              start=(j == 0), stop=(j == len(segs) - 1))
                last.then_inc(mixed, 1)

            for n in range(len(ITEMS) + 3):
                if n < len(ITEMS):
                    scores(n)
                if 2 <= n < len(ITEMS) + 2:
                    turn(n - 2)
                if n >= 3:
                    weigh(n - 3)
            meet(pe, 3)
            project(8, (n_hi, mix1_lo), L, True, sums_behind(y1_squares))
            sum_squares(n_all)
            meet(pe, 4)
            count["norm"] += DT
            pe.wait_ge(norm_ready, count["norm"])
            c0 = count["chunk"]
            with pe.Fori(0, FT // 2) as i:
                for j in range(4):
                    w = w_hi[:, (c0 + j) % PAIR], ring_r[:, (c0 + j) % RING]
                    pe.wait_ge(w_ready, i * 4 + (c0 + j + 1))
                    if j % 2 == 0:
                        pe.wait_ge(ff_done, i * 2 + (j // 2 + 1))
                    for half in range(2):
                        for k in range(DT):
                            cs = slice(half * HL, half * HL + HL)
                            last = three(ps[:, 2 * j + half, 0:HL], [p[:, k, :] for p in w],
                                         [x[:, k, cs] for x in (n_hi, low1)], k == 0, k == DT - 1)
                    last.then_inc(chunk_done, 1)
            count["chunk"] += 2 * FT
            meet(pe, 5)
            for m in range(DT):
                b = banks()
                for c in range(DOWN_CH):
                    w = take()
                    for k in range(c * DT, min(c * DT + DT, FT)):
                        for half in range(2):
                            cs = slice(half * HL, half * HL + HL)
                            last = three(ps[:, b + half, 0:HL], [p[:, k - c * DT, :] for p in w],
                                         [x[:, k, cs] for x in (ff_hi, ff_lo)], k == 0, k == FT - 1)
                    last.then_inc(chunk_done, 1)
                sums_behind(n_all)(m)
            sum_squares(n_all[:, :, META:L])
            meet(pe, 6)

            hi2 = n_hi[:, :, META:L]

            def beta_alpha(n):
                if n:
                    return
                for w, b in ((w_beta, 6), (w_alpha, 7)):
                    for k in range(DT):
                        last = mm(ps[0:H, b, :], w[:, k, :], tokens(2)[:, k, :], start=(k == 0), stop=(k == DT - 1))
                last.then_inc(s["small_mm"], 1)

            project(24, (hi2, parts(7)), SEQ, True, beta_alpha)
            meet(pe, 7)
            norm_quads = 0

            def head_sums(quads):
                nonlocal norm_quads
                for q in range(quads):
                    pe.wait_ge(s["l2_sq"], norm_quads + 1)
                    if q >= 2:
                        pe.wait_ge(s["l2_rstd"], norm_quads - 1)
                    for j in range(4):
                        last = mm(ps[:, 4 * (q % 2) + j, :], ones, normr[:, 4 * (q % 2) + j, :], start=True, stop=True)
                    last.then_inc(s["l2_sum"], 1)
                    norm_quads += 1

            normr = region(B[3], 8, SEQ)
            head_sums(4)
            pe.wait_ge(s["row_dve"], 5)
            pe.wait_ge(s["l2_rstd"], 4)
            for t in range(TT):
                last = tr(ps[:, 0, t * P:(t + 1) * P], rows[:, t * P:(t + 1) * P], ident)
            last.then_inc(s["rowT_ready"], 1)
            meet(pe, 8)
            bc = 0
            for which in range(3):
                src = (rowE, rowG, rows)[which]
                for hd in range(H):
                    if bc >= 4:
                        pe.wait_ge(s["bc_taken"], bc - 3)
                    mm(ps[:, bc % 4, :], sel[0:H, hd, :], src[0:H, :], start=True, stop=True).then_inc(s["bc_ready"], 1)
                    bc += 1
                if which == 1:
                    for hd in range(H):
                        last = mm(ps[:, 6, hd * NC:(hd + 1) * NC], sel[0:H, hd, :],
                                  rowE[0:H, C - 1:SEQ:C], start=True, stop=True)
                    last.then_inc(s["small_mm"], 1)
                    QT, KT = tokens(0), tokens(1)
                    for g in range(8):
                        t = g // 2
                        if g >= 2:
                            pe.wait_ge(s["kk_taken"], g - 1)
                        for j in range(4):
                            kk = KT[:, 4 * (g % 2) + j, t * P:(t + 1) * P]
                            last = mm(ps[:, 4 + g % 2, j * P:(j + 1) * P], kk, kk, start=True, stop=True)
                        last.then_inc(s["kk_ready"], 1)
            for g in range(8):
                t = g // 2
                pe.wait_ge(s["kk_taken"], 8 + g - 1)
                for j in range(4):
                    hd = 4 * (g % 2) + j
                    last = mm(ps[:, 4 + g % 2, j * P:(j + 1) * P], KT[:, hd, t * P:(t + 1) * P],
                              QT[:, hd, t * P:(t + 1) * P], start=True, stop=True)
                last.then_inc(s["kk_ready"], 1)
            meet(pe, 9)
            turned = 0

            def turn_groups(groups, source, banks=(0, 1)):
                nonlocal turned
                for g in range(groups):
                    if g >= 2:
                        pe.wait_ge(s["tr_taken"], turned - 1)
                    for j in range(4):
                        last = tr(ps[:, banks[g % 2], j * P:(j + 1) * P], source(g, j), ident)
                    last.then_inc(s["tr_ready"], 1)
                    turned += 1

            def by_token(T_):
                return lambda g, j: T_[:, 4 * (g % 2) + j, (g // 2) * P:(g // 2 + 1) * P]

            turn_groups(8, by_token(tokens(2)))
            pe.wait_ge(s["tr_taken"], 8)
            turn_groups(8, by_token(KT))
            meet(pe, 10)
            X, XT, T1, LT = blocks(1), blocks(2), blocks(8), blocks(5)
            def grp(A, g, j):
                return A[:, g // 2, 4 * (g % 2) + j, :]
            pe.wait_ge(s["inv_set"], 1)
            turn_groups(8, lambda g, j: grp(XT, g, j))
            pe.wait_ge(s["tr_taken"], 24)
            for lv in range(1, len(LEVELS)):
                last_level = lv == len(LEVELS) - 1
                for g in range(8):
                    pe.wait_ge(s["inv_mask"], 8 * (lv - 1) + g + 1)
                    n = 8 * (lv - 1) + g
                    if n >= 2:
                        pe.wait_ge(s["inv_t_taken"], n - 1)
                    if lv > 1:
                        pe.wait_ge(s["inv_x_taken"], 8 * (lv - 2) + g + 1)
                    for j in range(4):
                        last = mm(ps[:, g % 2, j * P:(j + 1) * P], gtmp[:, g % 2, j * P:(j + 1) * P], grp(X, g, j), start=True, stop=True)
                    last.then_inc(s["inv_t"], 1)
                for g in range(8):
                    n = 8 * (lv - 1) + g
                    pe.wait_ge(s["inv_t_taken"], n + 1)
                    if n >= 2:
                        pe.wait_ge(s["inv_x_taken"], n - 1)
                    for j in range(4):
                        if not last_level:
                            mm(ps[:, 2 + g % 2, j * P:(j + 1) * P], grp(XT, g, j), grp(T1, g, j), start=True, stop=True)
                        last = mm(ps[:, 4 + g % 2, j * P:(j + 1) * P], grp(T1, g, j), grp(XT, g, j), start=True, stop=True)
                    last.then_inc(s["inv_x"], 1)
            meet(pe, 11)
            VB, KG, KD = blocks(6), blocks(7), blocks(0)
            for g in range(8):
                if g >= 2:
                    pe.wait_ge(s["uw_taken"], g - 1)
                for j in range(4):
                    mm(ps[:, g % 2, j * P:(j + 1) * P], grp(XT, g, j), grp(VB, g, j), start=True, stop=True)
                    last = mm(ps[:, 2 + g % 2, j * P:(j + 1) * P], grp(KG, g, j), grp(XT, g, j), start=True, stop=True)
                last.then_inc(s["uw_ready"], 1)
            meet(pe, 12)
            QD, AT, WT = tokens(3), blocks(4), blocks(1)
            for c in range(NC):
                t, r = c // 2, slice(C * (c % 2), C * (c % 2) + C)
                for g in range(2):
                    n = 2 * c + g
                    pe.wait_ge(s["state_ready"], n + 1)
                    for j in range(4):
                        hd = 4 * g + j
                        last = mm(ps[r, g, j * P:(j + 1) * P], WT[:, t, hd, r], state[:, hd, :], start=True, stop=True)
                    last.then_inc(s["ks_ready"], 1)
                for g in range(2):
                    n = 2 * c + g
                    pe.wait_ge(s["vnew_ready"], n + 1)
                    if n >= 2:
                        pe.wait_ge(s["o_taken"], n - 1)
                    for j in range(4):
                        hd = 4 * g + j
                        mm(ps[:, 2 + g, j * C:(j + 1) * C], state[:, hd, :], QD[:, hd, c * C:(c + 1) * C],
                           start=True, stop=False)
                        mm(ps[:, 2 + g, j * C:(j + 1) * C], vnew[r, hd, :], AT[r, t, hd, r], start=False, stop=True)
                    for j in range(4):
                        hd = 4 * g + j
                        last = mm(ps[:, 4 + g, j * P:(j + 1) * P], KD[r, t, hd, :], vnew[r, hd, :], start=True, stop=True)
                    last.then_inc(s["os_ready"], 1)
            meet(pe, 13)
            head_sums(2)
            meet(pe, 14)
            project(8, (hi2, parts(7)), SEQ, True)
            meet(pe, 15)
            project(8, (parts(3), parts(4)), SEQ)
            project(8, (hi2, parts(7)), SEQ)
            meet(pe, 16)
            project(8, (hi2, parts(7)), SEQ)
            token_major(8 // PAIR, (hi2, parts(7)), False)
            project(8, (hi2, parts(7)), SEQ)
            meet(pe, 17)
            QB, KB, QL, KL = tokens(6), tokens(3), tokens(0), tokens(8)
            for lv in range(len(LEVELS) + 1):
                for half in range(2):
                    u = 2 * lv + half
                    if lv:
                        pe.wait_ge(s["lev_k"], u - 1)
                        pe.wait_ge(s["lev_q"], u - 1)
                    for t in range(TT):
                        n = TT * u + t
                        if n >= 8:
                            pe.wait_ge(s["lev_taken"], n - 7)
                        for j in range(4):
                            hd, cs = 4 * half + j, slice(t * P, (t + 1) * P)
                            last = mm(ps[:, n % 8, j * P:(j + 1) * P], (KL if lv else KB)[:, hd, cs],
                                      (QL if lv else QB)[:, hd, cs], start=True, stop=True)
                        last.then_inc(s["lev_mm"], 1)
            pe.wait_ge(s["hb_dve"], 2)
            pe.wait_ge(s["lev_taken"], 8 * len(LEVELS) + 8)
            turn_groups(8, by_token(KL), (4, 5))
            meet(pe, 18)
            AT2, QE, VI, KD2 = blocks(2), tokens(7), blocks(5), blocks(0)
            for c in range(NC):
                t, r = c // 2, slice(C * (c % 2), C * (c % 2) + C)
                for g in range(2):
                    n = 2 * c + g
                    pe.wait_ge(s["state_ready"], 18 + n + 1)
                    pe.wait_ge(s["o_taken"], 16 + n - 1 if n >= 2 else 16)
                    for j in range(4):
                        hd = 4 * g + j
                        mm(ps[:, 2 + g, j * C:(j + 1) * C], state[:, hd, :], QE[:, hd, c * C:(c + 1) * C],
                           start=True, stop=False)
                        mm(ps[:, 2 + g, j * C:(j + 1) * C], VI[r, t, hd, :], AT2[r, t, hd, r], start=False, stop=True)
                    for j in range(4):
                        hd = 4 * g + j
                        last = mm(ps[:, 4 + g, j * P:(j + 1) * P], KD2[r, t, hd, :], VI[r, t, hd, :], start=True, stop=True)
                    last.then_inc(s["os_ready"], 1)
            meet(pe, 19)
            normr = region(B[4], 8, SEQ)
            head_sums(2)
            meet(pe, 20)
            project(8, (hi2, parts(6)), SEQ, True)
            meet(pe, 21)
            project(8, (parts(5), parts(3)), SEQ)
            project(8, (hi2, parts(6)), SEQ)
            meet(pe, 22)
            project(8, (parts(2), parts(1)), SEQ, False, sums_behind(n_all[:, :, META:L]))
            def key_scores(n):
                t, part = n // PARTS, n % PARTS
                if n >= 2:
                    pe.wait_ge(s["sc_taken"], n - 1)
                for j in range(4):
                    last = mm(ps[:, 6 + n % 2, j * P:(j + 1) * P], qpk[:, 4 * part + j, t * P:(t + 1) * P],
                              sk[:, 4 * part + j, :], start=True, stop=True)
                last.then_inc(s["sc_mm"], 1)

            meet(pe, 23)

            def first_scores(n):
                if n in (4, 8):
                    pe.wait_ge(keys_in, 16)
                    pe.wait_ge(evac, TILE["pq"] + n)
                    key_scores(n // 4 - 1)

            project(16, (hi2, parts(3)), SEQ, True, first_scores)
            meet(pe, 24)
            def by_tokens(t):
                if t >= 1:
                    pe.wait_ge(s["tok_out"], 2 * t)
                for half in range(2):
                    for j in range(4):
                        last = tr(ps[:, 4 + half, j * P:(j + 1) * P],
                                  tokens(2)[:, 4 * half + j, t * P:(t + 1) * P], ident)
                last.then_inc(s["tok_mm"], 1)

            for t in range(TT):
                by_tokens(t)
            for n in range(NPARTS):
                t = n // PARTS
                yb = 2 * (t % 2)
                if n + 2 < NPARTS:
                    key_scores(n + 2)
                if n % PARTS == 0:
                    if t >= 2:
                        pe.wait_ge(s["y_out"], t - 1)
                    for half in range(2):
                        for j in range(3):
                            mm(ps[:, yb + half, :], h_all[:, 4 * half + j, META + t * P:META + (t + 1) * P],
                               wide[:, (3 - j) * P:(7 - j) * P], start=(j == 0), stop=False)
                with pe.Fori(0, PART // UV) as i:
                    for j in range(UV):
                        pe.wait_ge(s["diag"], (i * UV) + (n * PART + j + 1))
                        for half in range(2):
                            last = mm(ps[:, yb + half, :], diag[:, j, :], uv[:, j, D + half * 512:D + half * 512 + 512],
                                      start=False, stop=False)
                        last.then_inc(s["v_used"], 1)
                if n % PARTS == PARTS - 1:
                    for half in range(2):
                        last = mm(ps[:, yb + half, :], h_all[:, 4 * half + 3, META + t * P:META + (t + 1) * P],
                                  wide[:, 0:4 * P], start=False, stop=True)
                    last.then_inc(s["y_ready"], 1)

        @block.scalar
        def _(act):
            fn = nc.scalar.activation
            count = {"chunk": 0, "sumsq": 0, "link": 0, "full": 0, "h": 0}

            def link(ins):
                count["link"] += 1
                ins.then_inc(act_link, 1)
                act.wait_ge(act_link, count["link"])

            def upper(n):
                act.wait_ge(chunk_in[n % RING], 16 * (n // RING + 1))
                if n >= PAIR:
                    act.wait_ge(chunk_done, n - PAIR + 1)
                fn(w_hi[:, n % PAIR], ring[:, n % RING], ACT.Copy).then_inc(hi_ready, 1)

            def tile():
                count["chunk"] += 1
                act.wait_ge(chunk_done, count["chunk"])
                if count["chunk"] + 1 < CHUNKS:
                    upper(count["chunk"] + 1)

            def split(full, hi, wait=True):
                if wait:
                    count["full"] += 1
                    act.wait_ge(full_ready, count["full"])
                fn(hi, full, ACT.Copy).then_inc(xhi_ready, 1)

            def low_parts_back(n):
                act.wait_ge(low_moved, low_parts_moved(n))
                for k in range(DT):
                    fn(parts(n)[:, k, :], tokens(n)[:, k, :], ACT.Copy).then_inc(norm_ready, 1)

            def square(dst, src):
                fn(dst, src, ACT.Square).then_inc(sq_ready, 1)

            def squares_of_h(first):
                for k in range(DT):
                    count["h"] += 1
                    act.wait_ge(h_ready, count["h"])
                    square(n_all[:, k, first:L], h_all[:, k, first:L])

            def inverse_root(width, rstd=rstd):
                count["sumsq"] += 1
                act.wait_ge(sumsq_ready, count["sumsq"])
                halves = 2 if width > 512 else 1
                hw = width // halves
                link(fn(rstd[:, 0:width].rearrange("p (a b) -> p a b", b=hw), ps[:, 6:6 + halves, 0:hw], ACT.Ln,
                        scale=1.0 / D, bias=small[:, 0:1]))
                fn(rstd[:, 0:width], rstd[:, 0:width], ACT.Exp, scale=-0.5).then_inc(rstd_ready, 1)

            def bank_of(name, n):
                return 2 * ((TILE[name] + n) % 3)

            def two(name, n):
                b = bank_of(name, n)
                return ps[:, b:b + 2, 0:HL]

            def view2(x):
                return x.rearrange("p (a b) -> p a b", b=HL)

            tokens_low = parts(7).bitcast(F32)
            low_parts_moved = lambda n: {7: 32, 6: 48}[n]
            act.dma_start(con[:, :], consts).then_inc(consts_in, 16)
            act.dma_start(par[:, :], params).then_inc(consts_in, 16)
            act.dma_start(toe_c, toeplitz).then_inc(consts_in, 16)
            act.dma_start(h_all[:, :, :], xT.rearrange("(k p) t -> p k t", p=P)).then_inc(consts_in, 16)
            act.dma_start(sink, sinks.partition_broadcast(P)).then_inc(consts_in, 16)
            act.wait_ge(consts_in, 16 * 5)
            act.wait_ge(dve_link, 1)
            upper(0)
            upper(1)
            for k in range(DT):
                square(n_all[:, k, :], h_all[:, k, :])
            act.wait_ge(toe_ready, 1)
            fn(toe_r[0:H, :].rearrange("p (a b) -> p a b", b=512), ps[0:H, 0:2, :], ACT.Copy).then_inc(evac, 1)
            act.wait_ge(evac, 1)
            act.dma_start(scratch.ap(), toe_r[0:H, :]).then_inc(toe_out, 16)
            act.wait_ge(toe_out, 16)
            act.dma_start(bias_wr, bass.AP(scratch, 0, [[1, P], [TOE, H], [1, 2 * WIN]])).then_inc(bias_in, 16)
            for t in range(TT + 1):
                q0 = 0 if t == 0 else META + P * (t - 1)
                qn = META if t == 0 else P
                act.dma_start(bias_mr[0:qn, t], bass.AP(scratch, TOE_W + L - q0 - qn, [[1, qn], [TOE, H], [1, META]])
                              ).then_inc(bias_in, 16)
            inverse_root(L)
            for k in range(DT):
                split(full1[:, k, :], n_hi[:, k, :])
            act.wait_ge(f_ready, 1)
            fn(f_row[0:H, :].rearrange("p (a b) -> p a b", b=HL), ps[0:H, 6:8, 0:HL], ACT.Identity,
               bias=param("b_forget")[0:H, :]).then_inc(f_act, 1)
            act.wait_ge(f_dve, 1)
            link(fn(f_abs[0:H, :], f_abs[0:H, :], ACT.Exp, scale=-1.0))
            fn(f_abs[0:H, :], f_abs[0:H, :], ACT.Ln, bias=small[0:H, 1:2]).then_inc(f_act, 1)
            for n in range(13):
                tile()
                fn(view2(qk1[:, n, :]), two("in1", n), ACT.Copy,
                   scale=HD ** -0.5 if n < 4 or 5 <= n < 9 else 1.0).then_inc(evac, 1)
            meet(act, 1)
            for n in range(3):
                tile()
                tile()
                w = min(256, 640 - n * 256)
                fn(v1[0:META, 0, n * 256:n * 256 + w], ps[0:META, 6 + n % 2, 0:w], ACT.Copy)
                fn(v1[:, 1:5, n * 256:n * 256 + w], ps[:, 0:4, 0:w],
                   ACT.Copy).then_inc(evac, 1)
            act.wait_ge(toe_ready, 2)
            fn(bias_w.rearrange("p (a c) k -> p a (c k)", c=2), ps[:, 0:4, :], ACT.Copy)
            fn(bias_m[:, 1:5].rearrange("p t h m -> p (t h m)"), ps[:, 4, :], ACT.Copy)
            fn(bias_m[0:META, 0].rearrange("p h m -> p (h m)"), ps[0:META, 5, 0:P], ACT.Copy)
            meet(act, 2)

            def exps(n):
                tt, kind, hd, q0, qn, segs, cols, rws, tl = item(n)
                act.wait_ge(logits_ready, n + 1)
                if n >= 4:
                    act.wait_ge(probsT_ready, n - 3)
                w = cols + (1 if kind == 0 else 0)
                fn(prob[0:qn, n % 4, 0:w], logit[0:qn, n % 2, 0:w], ACT.Exp, bias=small[0:qn, 32 + n % 4:33 + n % 4],
                   accum_out=small[0:qn, 36 + n % 4:37 + n % 4]).then_inc(exp_done, 1)

            def take_turned(n):
                tt, kind, hd, q0, qn, segs, cols, rws, tl = item(n)
                act.wait_ge(probsT_ready, n + 1)
                if n >= 2:
                    act.wait_ge(mixed, n - 1)
                flat = ps[:, 4:6, :].rearrange("p a b -> p (a b)")
                last = fn(probT[0:META, n % 2, 0:qn], flat[0:META, 0:qn], ACT.Copy)
                if len(segs) > 1:
                    last = fn(probT[:, n % 2, P:len(segs) * P], flat[:, P:len(segs) * P], ACT.Copy)
                last.then_inc(probsT_taken, 1)

            def take_mixed(n):
                tt, kind, hd, q0, qn, segs, cols, rws, tl = item(n)
                act.wait_ge(mixed, n + 1)
                fn(mix1[rws, tl + 4 * kind, q0:q0 + qn], ps[rws, 6 + n % 2, 0:qn], ACT.Copy).then_inc(mixed_taken, 1)

            for n in range(len(ITEMS) + 3):
                if n < len(ITEMS):
                    exps(n)
                if 2 <= n < len(ITEMS) + 2:
                    take_turned(n - 2)
                if n >= 3:
                    take_mixed(n - 3)
            meet(act, 3)
            for k in range(DT):
                split(mix1[:, k, :], n_hi[:, k, :], False)
            for n in range(8):
                tile()
                square(view2(y1_squares[:, n, :]), two("out1", n))
                fn(view2(y1[:, n, :]), two("out1", n), ACT.Copy).then_inc(evac, 1)
            inverse_root(L)
            squares_of_h(0)
            meet(act, 4)
            inverse_root(L)
            for k in range(DT):
                split(y1[:, k, :], n_hi[:, k, :])
            c0 = count["chunk"]

            def upper_ahead(i, j):
                act.wait_ge(chunk_in[(c0 + j + 2) % RING], (i + ((c0 + j + 2) // RING + 1)) * 16)
                act.wait_ge(chunk_done, i * 4 + (c0 + j + 1))
                fn(w_hi[:, (c0 + j) % PAIR], ring[:, (c0 + j + 2) % RING], ACT.Copy).then_inc(hi_ready, 1)

            with act.Fori(0, FT // 2) as i:
                for j in range(2):
                    upper_ahead(i, 2 * j)
                    act.wait_ge(ff_done, i * 2 + (j + 1))
                    fn(view2(gtmp[:, j, :]), ps[:, 4 * j:4 * j + 2, 0:HL], ACT.Silu).then_inc(gated, 1)
                    upper_ahead(i, 2 * j + 1)
            count["chunk"] += 2 * FT
            meet(act, 5)
            for n in range(DT):
                for c in range(DOWN_CH):
                    tile()
                square(view2(n_all[:, n, :]), two("down", n))
                fn(view2(y1[:, n, :]), two("down", n), ACT.Copy).then_inc(evac, 1)
            inverse_root(L)
            squares_of_h(META)
            meet(act, 6)
            act.dma_start(h_rest.ap(), h_all[:, :, META:L]).then_inc(h_moved, 16)
            inverse_root(SEQ, rstd2)
            hi2 = n_hi[:, :, META:L]
            for k in range(DT):
                split(tokens(2)[:, k, :], hi2[:, k, :])
            act.wait_ge(norm_ready, 4 * DT)
            act.dma_start(low_rest.ap(), tokens_low).then_inc(low_moved, 16)
            act.wait_ge(s["small_mm"], 1)
            fn(rowY[0:H, :], ps[0:H, 6, :], ACT.Copy)
            fn(rowX[0:H, :], ps[0:H, 7, :], ACT.Identity, bias=param("dt_bias")[0:H, :]).then_inc(s["row_act"], 1)
            cx = region(B[3], 2, SEQ + 4)
            acc = region(B[4], 2, SEQ)
            dst3 = [tokens(0), tokens(1), tokens(2)]
            for n in range(25):
                if n < 24:
                    tile()
                    if n >= 2:
                        act.wait_ge(conv_done, n - 1)
                    fn(cx[:, n % 2, 3:3 + SEQ], ps[:, bank_of("a_q", n), :], ACT.Copy).then_inc(evac, 1)
                if n >= 1:
                    act.wait_ge(conv_done, n)
                    fn(dst3[(n - 1) // 8][:, (n - 1) % 8, :], acc[:, (n - 1) % 2, :], ACT.Silu).then_inc(silu_done, 1)
            meet(act, 7)
            norm_quads = 0

            def head_norms(quads, source, scale):
                nonlocal norm_quads
                base = norm_quads

                def sq(q):
                    if q >= 2:
                        act.wait_ge(s["l2_done"], base + q - 1)
                    fn(normr[:, 4 * (q % 2):4 * (q % 2) + 4, :], source(q), ACT.Square).then_inc(s["l2_sq"], 1)

                sq(0)
                sq(1)
                for q in range(quads):
                    act.wait_ge(s["l2_sum"], base + q + 1)
                    r = normr[:, 4 * (q % 2):4 * (q % 2) + 4, :]
                    link(fn(r, ps[:, 4 * (q % 2):4 * (q % 2) + 4, :], ACT.Ln, scale=scale, bias=small[:, 0:1]))
                    fn(r, r, ACT.Exp, scale=-0.5).then_inc(s["l2_rstd"], 1)
                    if q + 2 < quads:
                        sq(q + 2)
                norm_quads += quads

            normr = region(B[3], 8, SEQ)
            head_norms(4, lambda q: tokens(q // 2)[:, 4 * (q % 2):4 * (q % 2) + 4, :], 1.0)
            act.wait_ge(s["row_dve"], 1)
            link(fn(rows[0:H, :], rowY[0:H, :], ACT.Sigmoid))
            link(fn(rowE[0:H, :], rowE[0:H, :], ACT.Exp, scale=-1.0))
            link(fn(rowE[0:H, :], rowE[0:H, :], ACT.Ln, bias=small[0:H, 1:2]))
            fn(small[0:H, 4:5], param("a_log")[0:H, :], ACT.Exp).then_inc(s["row_act"], 1)
            act.wait_ge(s["row_dve"], 3)
            fn(rowE[0:H, :], rowG[0:H, :], ACT.Exp)
            fn(rows[64:64 + H, :], rowX[0:H, :], ACT.Exp).then_inc(s["row_act"], 1)
            act.wait_ge(s["rowT_ready"], 1)
            fn(rowT[:, :, :], ps[:, 0, :].rearrange("p (t r) -> p t r", r=P), ACT.Copy).then_inc(s["rowT_taken"], 1)
            meet(act, 8)
            DEC = blocks(4)
            act.wait_ge(s["small_mm"], 2)
            fn(glast[:, :, :], ps[:, 6, 0:H * NC].rearrange("p (h c) -> p h c", c=NC), ACT.Copy)
            act.wait_ge(s["dec_ready"], 1)
            for t in range(TT):
                fn(DEC[:, t], DEC[:, t], ACT.Exp).then_inc(s["dec_exp"], 1)
            meet(act, 9)
            act.wait_ge(low_moved, 16)
            VB, KG, KD = blocks(6), blocks(7), blocks(0)
            for g in range(8):
                act.wait_ge(s["tr_ready"], g + 1)
                for j in range(4):
                    hd = 4 * (g % 2) + j
                    last = fn(VB[:, g // 2, hd, :], ps[:, g % 2, j * P:(j + 1) * P], ACT.Copy,
                              scale=rowT[:, g // 2, hd:hd + 1])
                last.then_inc(s["tr_taken"], 1)
            for g in range(8):
                act.wait_ge(s["tr_ready"], 8 + g + 1)
                for j in range(4):
                    hd = 4 * (g % 2) + j
                    fn(KG[:, g // 2, hd, :], ps[:, g % 2, j * P:(j + 1) * P], ACT.Copy,
                       scale=rowT[:, g // 2, 32 + hd:33 + hd])
                    last = fn(KD[:, g // 2, hd, :], ps[:, g % 2, j * P:(j + 1) * P], ACT.Copy,
                              scale=rowT[:, g // 2, 64 + hd:65 + hd])
                last.then_inc(s["tr_taken"], 1)
            act.wait_ge(h_moved, 16)
            meet(act, 10)

            def quad(A, g):
                return A[:, g // 2, 4 * (g % 2):4 * (g % 2) + 4, :]

            def bank(b):
                return ps[:, b, :].rearrange("p (j m) -> p j m", m=P)

            X, XT, T1 = blocks(1), blocks(2), blocks(8)
            for g in range(8):
                act.wait_ge(s["tr_ready"], 16 + g + 1)
                fn(quad(X, g), bank(g % 2), ACT.Copy).then_inc(s["tr_taken"], 1)
            for lv in range(1, len(LEVELS)):
                for g in range(8):
                    n = 8 * (lv - 1) + g
                    act.wait_ge(s["inv_t"], n + 1)
                    if n >= 8:
                        act.wait_ge(s["inv_x"], n - 7)
                    fn(quad(T1, g), bank(g % 2), ACT.Copy).then_inc(s["inv_t_taken"], 1)
            meet(act, 11)
            U, WT = blocks(5), blocks(1)
            for g in range(8):
                act.wait_ge(s["uw_ready"], g + 1)
                fn(quad(U, g), bank(g % 2), ACT.Copy)
                fn(quad(WT, g), bank(2 + g % 2), ACT.Copy).then_inc(s["uw_taken"], 1)
            meet(act, 12)

            def outputs(OT, done):
                for n in range(2 * NC):
                    c, g = n // 2, n % 2
                    act.wait_ge(s["os_ready"], done + n + 1)
                    fn(OT[:, 4 * g:4 * g + 4, c * C:(c + 1) * C], ps[:, 2 + g, 0:4 * C].rearrange("p (j i) -> p j i", i=C),
                       ACT.Copy).then_inc(s["o_taken"], 1)

            act.dma_start(tokens(7), low_rest.ap()).then_inc(low_moved, 16)
            OA = tokens(8)
            outputs(OA, 0)
            meet(act, 13)
            head_norms(2, lambda q: OA[:, 4 * q:4 * q + 4, :], 1.0 / P)
            meet(act, 14)

            def gates_of(name, func, full=None, hi=None):
                for n in range(8 + (full is not None)):
                    if n >= 1 and full is not None:
                        act.wait_ge(evac, TILE[name] + n)
                        split(full[:, n - 1, :], hi[:, n - 1, :], False)
                    if n == 8:
                        break
                    tile()
                    at = TILE[name] + n
                    if n >= 2:
                        act.wait_ge(evac, at - 1)
                    fn(gtmp[:, at % 2, 0:SEQ], ps[:, bank_of(name, n), :], func).then_inc(gated, 1)

            def copies_of(name, target, func=ACT.Copy):
                for n in range(8):
                    tile()
                    fn(target[:, n, :], ps[:, bank_of(name, n), :], func).then_inc(evac, 1)

            low_parts_back(7)
            gates_of("a_gate", ACT.Silu, OA, parts(3))
            meet(act, 15)
            YA = tokens(0)
            copies_of("branch_a", YA)
            gates_of("g_a", ACT.Sigmoid)
            meet(act, 16)
            FG, BC = tokens(2), tokens(4)
            link(fn(lbound[:, 2, :], lbound[:, 0, :], ACT.Exp))
            fn(lbound[:, 3, :], lbound[:, 1, :], ACT.Exp).then_inc(s["hb_act"], 1)
            gates_of("b_f", ACT.Sigmoid)
            act.wait_ge(evac, TILE["b_i"])
            VI = blocks(5)
            for n in range(8 // PAIR):
                tile()
                tile()
                fn(VI[:, :, PAIR * n:PAIR * n + PAIR, :],
                   ps[:, 4 * (n % 2):4 * (n % 2) + 4, 0:256].rearrange("p t (h m) -> p t h m", m=P), ACT.Copy).then_inc(evac, 1)
            copies_of("b_q", tokens(6), ACT.Silu)
            for n in range(8):
                fn(FG[:, n, :], FG[:, n, :], ACT.Ln).then_inc(s["hb_act"], 1)
            meet(act, 17)
            E = tokens(7)
            for u in range(2 * len(LEVELS)):
                act.wait_ge(s["lev_diff"], u + 1)
                Eh = E[:, 4 * (u % 2):4 * (u % 2) + 4, :]
                fn(Eh, Eh, ACT.Exp).then_inc(s["lev_exp"], 1)
            act.wait_ge(s["hb_dve"], 1)
            fn(E, E, ACT.Exp).then_inc(s["lev_exp"], 1)
            KD2 = blocks(0)
            for g in range(8):
                act.wait_ge(s["tr_ready"], 24 + g + 1)
                fn(quad(KD2, g), bank(4 + g % 2), ACT.Copy).then_inc(s["tr_taken"], 1)
            act.wait_ge(s["hb_dve"], 2)
            fn(glast[:, :, :], BC[:, :, C - 1:SEQ:C], ACT.Exp)
            fn(E, BC, ACT.Exp).then_inc(s["lev_exp"], 1)
            meet(act, 18)
            act.dma_start(h_all[:, :, META:L], h_rest.ap()).then_inc(h_moved, 16)
            act.dma_start(tokens(6), low_rest.ap()).then_inc(low_moved, 16)
            OBt = tokens(3)
            outputs(OBt, 16)
            meet(act, 19)
            normr = region(B[4], 8, SEQ)
            head_norms(2, lambda q: OBt[:, 4 * q:4 * q + 4, :], 1.0 / P)
            meet(act, 20)
            low_parts_back(6)
            gates_of("b_gate", ACT.Sigmoid, OBt, parts(5))
            meet(act, 21)
            copies_of("branch_b", YA)
            gates_of("g_b", ACT.Sigmoid, tokens(1), parts(2))
            meet(act, 22)
            for n in range(8):
                tile()
                act.wait_ge(evac, TILE["out2"] + n + 1)
                square(n_all[:, n, META:L], h_all[:, n, META:L])
            act.dma_start(sk, keys.rearrange("p (n k) -> p n k", k=NKEYS)).then_inc(keys_in, 16)
            meet(act, 23)
            inverse_root(SEQ, rstd2)
            def gate_exp(n):
                act.wait_ge(s["gate_in"], n + 1)
                gt = gates[:, n // PARTS, (n % PARTS) * PART:(n % PARTS + 1) * PART]
                fn(gt, gt, ACT.Exp).then_inc(s["gate_exp"], 1)

            for k in range(DT):
                split(tokens(2)[:, k, :], hi2[:, k, :])
            for n in range(16):
                tile()
                fn(qpk[:, n, :], ps[:, bank_of("pq", n), :], ACT.Copy).then_inc(evac, 1)
                if n in (9, 13):
                    gate_exp((n - 9) // 4)
            act.dma_start(wide, placing).then_inc(consts_in, 16)
            act.wait_ge(consts_in, 16 * 6)
            act.dma_start(fin_g, final_norm.partition_broadcast(P)).then_inc(consts_in, 16)
            act.wait_ge(consts_in, 16 * 7)
            meet(act, 24)
            def tok_copy(t):
                act.wait_ge(s["tok_mm"], t + 1)
                for half in range(2):
                    fn(h2tok[t][:, half * 512:half * 512 + 512], ps[:, 4 + half, :], ACT.Copy).then_inc(s["tok_out"], 1)

            for t in range(TT):
                tok_copy(t)
            for n in range(NPARTS):
                t = n // PARTS
                with act.Fori(0, PART // UV) as i:
                    for g in range(UV // 2):
                        act.wait_ge(s["dots"], i * (UV // 2) + (PART // 2 * n + g + 1))
                        fn(hgel[:, 2 * g:2 * g + 2], hdot[:, 2 * g:2 * g + 2], ACT.Gelu).then_inc(s["gelu"], 1)
                if n + 2 < NPARTS:
                    gate_exp(n + 2)
                if n % PARTS == PARTS - 1:
                    act.wait_ge(s["y_ready"], t + 1)
                    if t >= 1:
                        act.wait_ge(s["y_out"], t)
                    link(fn(squares, ps[:, 2 * (t % 2):2 * (t % 2) + 2, :].rearrange("p a b -> p (a b)"), ACT.Square,
                            accum_out=small[:, 40:41]))
                    link(fn(small[:, 41:42], small[:, 40:41], ACT.Ln, scale=1.0 / D, bias=small[:, 0:1]))
                    fn(small[:, 42:43], small[:, 41:42], ACT.Exp, scale=-0.5).then_inc(s["y_act"], 1)

        @block.vector
        def _(dve):
            v = nc.vector
            count = {"link": 0, "rstd": 0, "gated": 0, "xhi": 0}

            def link(ins):
                count["link"] += 1
                ins.then_inc(dve_link, 1)
                dve.wait_ge(dve_link, count["link"])

            def lower(full, hi, lo):
                count["xhi"] += 1
                dve.wait_ge(xhi_ready, count["xhi"])
                return v.tensor_tensor(lo, full, hi.bitcast(F32), ALU.subtract)

            def normalise(full, src, gain, width, hi, lo, rstd=rstd):
                count["rstd"] += 1
                dve.wait_ge(rstd_ready, count["rstd"])
                for k in range(DT + 1):
                    if k < DT:
                        v.scalar_tensor_tensor(full[:, k, :], src[:, k, :], gain[:, k:k + 1], rstd[:, 0:width],
                                               ALU.mult, ALU.mult).then_inc(full_ready, 1)
                    if k >= 1:
                        lower(full[:, k - 1, :], hi[:, k - 1, :], lo[:, k - 1, :]).then_inc(norm_ready, 1)

            def add_normed(src, gain, width):
                count["rstd"] += 1
                dve.wait_ge(rstd_ready, count["rstd"])
                for k in range(DT + 1):
                    if k < DT:
                        count["link"] += 1
                        v.scalar_tensor_tensor(src[:, k, :], src[:, k, :], gain[:, k:k + 1], rstd[:, 0:width],
                                               ALU.mult, ALU.mult).then_inc(dve_link, 1)
                    if k >= 1:
                        dve.wait_ge(dve_link, count["link"] - (k < DT))
                        v.tensor_tensor(h_all[:, k - 1, :], h_all[:, k - 1, :], src[:, k - 1, :], ALU.add
                                        ).then_inc(h_ready, 1)

            v.memset(small[:, 0:1], EPS)
            v.memset(small[:, 1:2], 1.0)
            link(v.memset(ones_row[0:H, :], 1.0))
            dve.wait_ge(consts_in, 16 * 5)
            normalise(full1, h_all, param("ln_pre_mix"), L, n_hi, low1)
            dve.wait_ge(f_act, 1)
            v.scalar_tensor_tensor(f_abs[0:H, :], f_row[0:H, :], -1.0, f_row[0:H, :], ALU.mult, ALU.max
                                   ).then_inc(f_dve, 1)
            dve.wait_ge(f_act, 2)
            link(v.scalar_tensor_tensor(f_row[0:H, :], f_row[0:H, :], 0.0, f_abs[0:H, :], ALU.min, ALU.subtract))
            link(v.tensor_tensor_scan(f_abs[0:H, :], ones_row[0:H, :], f_row[0:H, :], 0.0, ALU.mult, ALU.add))
            v.tensor_scalar(negcum[0:H, :], f_abs[0:H, :], -1.0, None, ALU.mult)
            meet(dve, 1)
            meet(dve, 2)

            def logits(n):
                tt, kind, hd, q0, qn, segs, cols, rws, tl = item(n)
                dve.wait_ge(scores_ready, n + 1)
                if n >= 2:
                    dve.wait_ge(exp_done, n - 1)
                b = 2 * (n % 2)
                lg = logit[0:qn, n % 2, :]
                if kind == 0:
                    last = v.tensor_tensor(lg[:, 0:META], ps[0:qn, b, 0:META], bias_m[0:qn, tt, hd, :], ALU.add)
                    if tt:
                        wn = cols - META
                        last = v.tensor_tensor(lg[:, META:cols], ps[0:qn, b, META:cols],
                                               bias_w[:, hd, 2 * WIN - wn:2 * WIN], ALU.add)
                    last.then_inc(scores_taken, 1)
                    link(v.tensor_copy(lg[:, cols:cols + 1], sink[0:qn, hd:hd + 1]))
                    w = cols + 1
                else:
                    d0 = cols - qn
                    for a, e in ((0, min(d0, 512)),):
                        if e > a:
                            v.tensor_copy(lg[:, a:e], ps[0:qn, b, a:e])
                    for a, e in ((d0, min(cols, 512)), (max(512, d0), cols)):
                        if e > a:
                            last = v.tensor_tensor(lg[:, a:e], ps[0:qn, b + a // 512, a % 512:a % 512 + e - a],
                                                   causal[0:qn, a - d0:e - d0], ALU.add)
                    last.then_inc(scores_taken, 1)
                    w = cols
                dve.wait_ge(scores_taken, n + 1)
                mx = small[0:qn, 44 + n % 4:45 + n % 4]
                link(v.tensor_reduce(mx, lg[:, 0:w], AX, ALU.max))
                v.tensor_scalar(small[0:qn, 32 + n % 4:33 + n % 4], mx, -1.0, None, ALU.mult).then_inc(logits_ready, 1)

            def probs(n):
                tt, kind, hd, q0, qn, segs, cols, rws, tl = item(n)
                dve.wait_ge(exp_done, n + 1)
                inv = small[0:qn, 48 + n % 4:49 + n % 4]
                link(v.reciprocal(inv, small[0:qn, 36 + n % 4:37 + n % 4]))
                v.tensor_scalar(prob[0:qn, n % 4, 0:cols], prob[0:qn, n % 4, 0:cols], inv, None, ALU.mult
                                ).then_inc(probs_ready, 1)

            for n in range(len(ITEMS) + 1):
                if n < len(ITEMS):
                    logits(n)
                if n >= 1:
                    probs(n - 1)
            meet(dve, 3)
            for k in range(DT):
                lower(mix1[:, k, :], n_hi[:, k, :], mix1_lo[:, k, :]).then_inc(norm_ready, 1)
            add_normed(y1, param("ln_post_mix"), L)
            meet(dve, 4)
            normalise(y1, h_all, param("ln_pre_ffn"), L, n_hi, low1)
            v.memset(small[:, 6:7], 0.0).then_inc(ff_done, 2)
            c0 = FIRST_OF["gate_up"]
            with dve.Fori(0, FT // 2) as i:
                for j in range(2):
                    dve.wait_ge(gated, i * 2 + (j + 1))
                    dve.wait_ge(chunk_done, i * 4 + (c0 + 2 * j + 2))
                    v.tensor_tensor(ff[:, bass.ds(i * 2 + j, 1), :].rearrange("p o (a b) -> p (o a) b", b=HL),
                                    gtmp[:, j, :].rearrange("p (a b) -> p a b", b=HL),
                                    ps[:, 4 * j + 2:4 * j + 4, 0:HL], ALU.mult).then_inc(ff_done, 1)
                    m = bass.ds(i * 2 + j, 1)
                    dve.wait_ge(ff_done, i * 2 + (j + 3))
                    v.tensor_scalar(ff_hi[:, m, :], ff[:, m, :], 1.0, None, ALU.mult).then_inc(ff_upper, 1)
                    dve.wait_ge(ff_upper, i * 2 + (j + 1))
                    v.tensor_tensor(ff_lo[:, m, :], ff[:, m, :], ff_hi[:, m, :].bitcast(F32), ALU.subtract)
            count["gated"] = FT
            meet(dve, 5)
            add_normed(y1, param("ln_post_ffn"), L)
            meet(dve, 6)
            hx, hi2 = h_all[:, :, META:L], n_hi[:, :, META:L]
            normalise(tokens(2), hx, param("norm1"), SEQ, hi2, parts(7), rstd2)
            cx = region(B[3], 2, SEQ + 4)
            acc = region(B[4], 2, SEQ)
            link(v.memset(cx[:, :, 0:3], 0.0))
            for n in range(24):
                dve.wait_ge(evac, TILE["a_q"] + n + 1)
                if n >= 2:
                    dve.wait_ge(silu_done, n - 1)
                a = acc[:, n % 2, :]
                link(v.tensor_scalar(a, cx[:, n % 2, 0:SEQ], conv_w[:, n, 0:1], None, ALU.mult))
                for j in range(1, 4):
                    ins = v.scalar_tensor_tensor(a, cx[:, n % 2, j:j + SEQ], conv_w[:, n, j:j + 1], a, ALU.mult, ALU.add)
                    if j < 3:
                        link(ins)
                ins.then_inc(conv_done, 1)
            meet(dve, 7)
            norm_quads = 0

            def head_scale(quads, target, factor):
                nonlocal norm_quads
                for q in range(quads):
                    dve.wait_ge(s["l2_rstd"], norm_quads + 1)
                    v.scalar_tensor_tensor(target(q), target(q), factor(q), normr[:, 4 * (q % 2):4 * (q % 2) + 4, :],
                                           ALU.mult, ALU.mult).then_inc(s["l2_done"], 1)
                    norm_quads += 1

            v.memset(rows[:, :], 0.0)
            v.scalar_tensor_tensor(rowE[0:H, :], rowX[0:H, :], -1.0, rowX[0:H, :], ALU.mult, ALU.max
                                   ).then_inc(s["row_dve"], 1)
            normr = region(B[3], 8, SEQ)
            head_scale(4, lambda q: tokens(q // 2)[:, 4 * (q % 2):4 * (q % 2) + 4, :], lambda q: P ** -0.5 if q < 2 else 1.0)
            dve.wait_ge(s["row_act"], 2)
            link(v.scalar_tensor_tensor(rowX[0:H, :], rowX[0:H, :], 0.0, rowE[0:H, :], ALU.max, ALU.add))
            link(v.tensor_scalar(rowX[0:H, :], rowX[0:H, :], small[0:H, 4:5], -1.0, ALU.mult, ALU.mult))
            v.tensor_tensor_scan(rowG[0:H, :], const("reset")[0:H, :], rowX[0:H, :], 0.0, ALU.mult, ALU.add
                                 ).then_inc(s["row_dve"], 1)
            dve.wait_ge(s["row_dve"], 2)
            g3 = rowG[0:H, :].rearrange("p (c i) -> p c i", i=C)
            v.tensor_tensor(rowX[0:H, :].rearrange("p (c i) -> p c i", i=C), g3[:, :, C - 1:C].to_broadcast([H, NC, C]), g3,
                            ALU.subtract).then_inc(s["row_dve"], 1)
            v.tensor_scalar(rows[96:96 + H, :], rowG[0:H, :], -1.0, None, ALU.mult).then_inc(s["row_dve"], 1)
            dve.wait_ge(s["row_act"], 3)
            v.tensor_tensor(rows[32:32 + H, :], rows[0:H, :], rowE[0:H, :], ALU.mult).then_inc(s["row_dve"], 1)
            meet(dve, 8)
            DEC, LT, QD = blocks(4), blocks(5), tokens(3)
            bc = 0
            for hd in range(H):
                dve.wait_ge(s["bc_ready"], bc + 1)
                v.tensor_tensor(QD[:, hd, :], tokens(0)[:, hd, :], ps[:, bc % 4, :], ALU.mult).then_inc(s["bc_taken"], 1)
                bc += 1
            for hd in range(H):
                dve.wait_ge(s["bc_ready"], bc + 1)
                for t in range(TT):
                    last = v.tensor_scalar(DEC[:, t, hd, :], ps[:, bc % 4, t * P:(t + 1) * P],
                                           rowT[:, t, 96 + hd:97 + hd], 0.0, ALU.add, ALU.min)
                last.then_inc(s["bc_taken"], 1)
                bc += 1
            dve.wait_ge(s["bc_taken"], bc)
            v.memset(small[0:H, 5:6], 0.0).then_inc(s["dec_ready"], 1)
            cmask = const("chunk_causal").unsqueeze(1).to_broadcast([P, H, P])
            for t in range(TT):
                dve.wait_ge(s["dec_exp"], t + 1)
                last = v.tensor_tensor(DEC[:, t], DEC[:, t], cmask, ALU.mult)
            link(last)

            def quad(A, g):
                return A[:, g // 2, 4 * (g % 2):4 * (g % 2) + 4, :]

            def bank(b):
                return ps[:, b, :].rearrange("p (j m) -> p j m", m=P)

            for g in range(8):
                dve.wait_ge(s["kk_ready"], g + 1)
                v.tensor_tensor(quad(LT, g), bank(4 + g % 2), quad(DEC, g), ALU.mult).then_inc(s["kk_taken"], 1)
            dve.wait_ge(s["kk_taken"], 8)
            for hd in range(H):
                dve.wait_ge(s["bc_ready"], bc + 1)
                v.tensor_tensor(LT[:, :, hd, :], LT[:, :, hd, :], ps[:, bc % 4, :].rearrange("p (t i) -> p t i", i=P),
                                ALU.mult).then_inc(s["bc_taken"], 1)
                bc += 1
            for g in range(8):
                dve.wait_ge(s["kk_ready"], 8 + g + 1)
                v.tensor_tensor(quad(DEC, g), bank(4 + g % 2), quad(DEC, g), ALU.mult).then_inc(s["kk_taken"], 1)
            meet(dve, 9)
            meet(dve, 10)
            X, XT = blocks(1), blocks(2)

            def masks(m, w):
                return level_mask[:, m:m + 1, :].to_broadcast([P, w, P])

            for t in range(TT):
                last = v.tensor_tensor(XT[:, t], LT[:, t], masks(0, H), ALU.mult)
            link(last)
            ib = ident.unsqueeze(1).to_broadcast([P, H, P])
            for t in range(TT):
                last = v.tensor_tensor(XT[:, t], ib, XT[:, t], ALU.subtract)
            last.then_inc(s["inv_set"], 1)
            for lv in range(1, len(LEVELS)):
                last_level = lv == len(LEVELS) - 1
                for g in range(8):
                    n = 8 * (lv - 1) + g
                    if n >= 2:
                        dve.wait_ge(s["inv_t"], n - 1)
                    v.tensor_tensor(gtmp[:, g % 2, 0:4 * P].rearrange("p (j m) -> p j m", m=P), quad(LT, g),
                                    masks(lv, 4), ALU.mult).then_inc(s["inv_mask"], 1)
                for g in range(8):
                    n = 8 * (lv - 1) + g
                    dve.wait_ge(s["inv_x"], n + 1)
                    if lv == 1 and g == 0:
                        dve.wait_ge(s["tr_taken"], 24)
                    if not last_level:
                        v.tensor_tensor(quad(X, g), quad(X, g), bank(2 + g % 2), ALU.subtract)
                    v.tensor_tensor(quad(XT, g), quad(XT, g), bank(4 + g % 2), ALU.subtract).then_inc(s["inv_x_taken"], 1)
            meet(dve, 11)
            v.memset(state[:, 0:4, :], 0.0).then_inc(s["state_ready"], 1)
            v.memset(state[:, 4:8, :], 0.0).then_inc(s["state_ready"], 1)
            meet(dve, 12)
            U = blocks(5)
            for c in range(NC):
                t, r = c // 2, slice(C * (c % 2), C * (c % 2) + C)
                for g in range(2):
                    n = 2 * c + g
                    dve.wait_ge(s["ks_ready"], n + 1)
                    if n >= 2:
                        dve.wait_ge(s["os_ready"], n - 1)
                    v.tensor_tensor(vnew[r, 4 * g:4 * g + 4, :], U[r, t, 4 * g:4 * g + 4, :],
                                    ps[r, g, :].rearrange("p (j m) -> p j m", m=P), ALU.subtract).then_inc(s["vnew_ready"], 1)
                for g in range(2):
                    n = 2 * c + g
                    dve.wait_ge(s["os_ready"], n + 1)
                    S = state[:, 4 * g:4 * g + 4, :]
                    link(v.tensor_tensor(S, S, glast[:, 4 * g:4 * g + 4, c:c + 1].to_broadcast([P, 4, P]), ALU.mult))
                    v.tensor_tensor(S, S, bank(4 + g), ALU.add).then_inc(s["state_ready"], 1)
            meet(dve, 13)
            OA = tokens(8)
            head_scale(2, lambda q: OA[:, 4 * q:4 * q + 4, :], lambda q: param("a_onorm"))
            meet(dve, 14)

            def gate(name, n):
                count["gated"] += 1
                dve.wait_ge(gated, count["gated"])
                return gtmp[:, (TILE[name] + n) % 2, 0:SEQ]

            for n in range(8):
                v.tensor_tensor(OA[:, n, :], OA[:, n, :], gate("a_gate", n), ALU.mult).then_inc(evac, 1)
                if n >= 1:
                    lower(OA[:, n - 1, :], parts(3)[:, n - 1, :], parts(4)[:, n - 1, :])
            lower(OA[:, 7, :], parts(3)[:, 7, :], parts(4)[:, 7, :])
            meet(dve, 15)
            YA, MX = tokens(0), tokens(1)
            for n in range(8):
                v.tensor_tensor(MX[:, n, :], YA[:, n, :], gate("g_a", n), ALU.mult).then_inc(evac, 1)
            p0, p1 = param("lower0"), param("lower1")
            link(v.tensor_tensor(lbound[:, 2, :], p0, p1, ALU.max))
            v.tensor_tensor(lbound[:, 0, :], p0, lbound[:, 2, :], ALU.subtract)
            v.tensor_tensor(lbound[:, 1, :], p1, lbound[:, 2, :], ALU.subtract)
            meet(dve, 16)
            dve.wait_ge(s["hb_act"], 1)
            link(v.tensor_tensor(lbound[:, 1, :], lbound[:, 2, :], lbound[:, 3, :], ALU.add))
            link(v.reciprocal(lbound[:, 1, :], lbound[:, 1, :]))
            link(v.tensor_tensor(lbound[:, 0, :], lbound[:, 2, :], lbound[:, 1, :], ALU.mult))
            link(v.tensor_scalar(lbound[:, 1, :], lbound[:, 0, :], -1.0, 1.0, ALU.mult, ALU.add))
            FG, KB, BC = tokens(2), tokens(3), tokens(4)
            for n in range(8):
                link(v.tensor_scalar(FG[:, n, :], gate("b_f", n), lbound[:, 1, n:n + 1], lbound[:, 0, n:n + 1],
                                     ALU.mult, ALU.add))
                v.tensor_scalar(KB[:, n, :], FG[:, n, :], -1.0, 1.0, ALU.mult, ALU.add).then_inc(evac, 1)
            for n in range(8):
                dve.wait_ge(s["hb_act"], 1 + n + 1)
                last = v.tensor_tensor_scan(BC[:, n, :], const("reset"), FG[:, n, :], 0.0, ALU.mult, ALU.add)
            meet(dve, 17)
            E, KL, QL, QB, AT2 = tokens(7), tokens(8), tokens(0), tokens(6), blocks(2)
            link(v.memset(region(B[2], slot), 0.0))

            def join(u):
                lv, half = u // 2, u % 2
                mask = (ident.unsqueeze(1).to_broadcast([P, 4, P]) if lv == 0 else masks(lv - 1, 4)).bitcast(I32)
                for t in range(TT):
                    n = TT * u + t
                    dve.wait_ge(s["lev_mm"], n + 1)
                    v.copy_predicated(AT2[:, t, 4 * half:4 * half + 4, :], mask, bank(n % 8)).then_inc(s["lev_taken"], 1)

            def diff(u):
                if u >= 2:
                    dve.wait_ge(s["lev_q"], u - 1)
                    dve.wait_ge(s["lev_k"], u - 1)
                m = LEVELS[u // 2]
                hs = slice(4 * (u % 2), 4 * (u % 2) + 4)
                b4 = BC[:, hs, :].rearrange("p h (n w) -> p (h n) w", w=2 * m)
                e4 = E[:, hs, :].rearrange("p h (n w) -> p (h n) w", w=2 * m)
                ref = b4[:, :, m - 1:m].to_broadcast([P, 4 * SEQ // (2 * m), m])
                v.tensor_tensor(e4[:, :, 0:m], ref, b4[:, :, 0:m], ALU.subtract)
                v.tensor_tensor(e4[:, :, m:2 * m], b4[:, :, m:2 * m], ref, ALU.subtract).then_inc(s["lev_diff"], 1)

            diff(0)
            diff(1)
            join(0)
            for u in range(2 * len(LEVELS)):
                hs = slice(4 * (u % 2), 4 * (u % 2) + 4)
                dve.wait_ge(s["lev_exp"], u + 1)
                if u >= 2:
                    dve.wait_ge(s["lev_mm"], TT * (u + 1))
                v.tensor_tensor(KL[:, hs, :], KB[:, hs, :], E[:, hs, :], ALU.mult).then_inc(s["lev_k"], 1)
                join(u + 1)
                if u + 2 < 2 * len(LEVELS):
                    diff(u + 2)
            join(2 * len(LEVELS) + 1)
            dve.wait_ge(s["lev_q"], 2 * len(LEVELS))
            b3 = BC.rearrange("p h (n w) -> p (h n) w", w=C)
            v.tensor_tensor(E.rearrange("p h (n w) -> p (h n) w", w=C), b3[:, :, C - 1:C].to_broadcast([P, H * NC, C]), b3,
                            ALU.subtract).then_inc(s["hb_dve"], 1)
            dve.wait_ge(s["lev_exp"], 2 * len(LEVELS) + 1)
            v.tensor_tensor(KL, KB, E, ALU.mult).then_inc(s["hb_dve"], 1)
            dve.wait_ge(s["lev_exp"], 2 * len(LEVELS) + 2)
            v.tensor_tensor(E, QB, E, ALU.mult)
            v.memset(state[:, 0:4, :], 0.0).then_inc(s["state_ready"], 1)
            v.memset(state[:, 4:8, :], 0.0).then_inc(s["state_ready"], 1)
            meet(dve, 18)
            for c in range(NC):
                for g in range(2):
                    n = 2 * c + g
                    dve.wait_ge(s["os_ready"], 16 + n + 1)
                    for j in range(4):
                        hd = 4 * g + j
                        last = v.scalar_tensor_tensor(state[:, hd, :], state[:, hd, :], glast[:, hd, c:c + 1],
                                                      ps[:, 4 + g, j * P:(j + 1) * P], ALU.mult, ALU.add)
                    last.then_inc(s["state_ready"], 1)
            meet(dve, 19)
            normr = region(B[4], 8, SEQ)
            OBt = tokens(3)
            head_scale(2, lambda q: OBt[:, 4 * q:4 * q + 4, :], lambda q: param("b_onorm"))
            meet(dve, 20)
            for n in range(8):
                v.tensor_tensor(OBt[:, n, :], OBt[:, n, :], gate("b_gate", n), ALU.mult).then_inc(evac, 1)
                if n >= 1:
                    lower(OBt[:, n - 1, :], parts(5)[:, n - 1, :], parts(3)[:, n - 1, :])
            lower(OBt[:, 7, :], parts(5)[:, 7, :], parts(3)[:, 7, :])
            meet(dve, 21)
            for n in range(8):
                g_ = gate("g_b", n)
                link(v.tensor_tensor(g_, YA[:, n, :], g_, ALU.mult))
                v.tensor_tensor(MX[:, n, :], MX[:, n, :], g_, ALU.add).then_inc(evac, 1)
                if n >= 1:
                    lower(MX[:, n - 1, :], parts(2)[:, n - 1, :], parts(1)[:, n - 1, :])
            lower(MX[:, 7, :], parts(2)[:, 7, :], parts(1)[:, 7, :])
            dve.wait_ge(h_moved, 32)
            meet(dve, 22)
            for n in range(8):
                dve.wait_ge(chunk_done, FIRST_OF["out2"] + n + 1)
                v.tensor_tensor(hx[:, n, :], hx[:, n, :], ps[:, 2 * ((TILE["out2"] + n) % 3), :], ALU.add).then_inc(evac, 1)
            meet(dve, 23)
            normalise(tokens(2), hx, param("norm2"), SEQ, hi2, parts(3), rstd2)
            it16 = const("iota16")
            NEGS = -3e38

            def best_keys(n):
                lists = range(4)
                rest = cand.rearrange("p (n k) -> p n k", n=4)[:, :, 0:NKEYS]
                score = ps[:, 6 + n % 2, :].rearrange("p (n k) -> p n k", n=4)
                dve.wait_ge(s["sc_mm"], n + 1)
                link([v.max(top_v[:, j, 0:8], score[:, j, :]) for j in lists][-1])
                for j in lists:
                    v.max_index(top_i[:, j, 0:8], top_v[:, j, 0:8], score[:, j, :])
                last = [v.match_replace(rest[:, j, :], top_v[:, j, 0:8], score[:, j, :], NEGS) for j in lists][-1]
                last.then_inc(s["sc_taken"], 1)
                dve.wait_ge(s["sc_taken"], n + 1)
                link([v.max(top_v[:, j, 8:16], rest[:, j, :]) for j in lists][-1])
                for j in lists:
                    v.max_index(top_i[:, j, 8:16], top_v[:, j, 8:16], rest[:, j, :])
                for p in range(2):
                    last = v.tensor_tensor(pair_sum[:, p, :].rearrange("p (i j) -> p i j", j=TOPK),
                                           top_v[:, 2 * p, :].unsqueeze(2).to_broadcast([P, TOPK, TOPK]),
                                           top_v[:, 2 * p + 1, :].unsqueeze(1).to_broadcast([P, TOPK, TOPK]), ALU.add)
                link(last)

            def best_pairs(n):
                t, part = n // PARTS, n % PARTS
                cols = slice(part * PART, (part + 1) * PART)
                v.tensor_copy(top_f, top_i)
                link([v.max(best[:, p, 0:8], pair_sum[:, p, :]) for p in range(2)][-1])
                left = cand.rearrange("p (n k) -> p n k", n=4)
                for p in range(2):
                    v.max_index(pos_u[:, p, 0:8], best[:, p, 0:8], pair_sum[:, p, :])
                link([v.match_replace(left[:, p, :], best[:, p, 0:8], pair_sum[:, p, :], NEGS) for p in range(2)][-1])
                link([v.max(best[:, p, 8:16], left[:, p, :]) for p in range(2)][-1])
                for p in range(2):
                    last = v.max_index(pos_u[:, p, 8:16], best[:, p, 8:16], left[:, p, :])
                gt = gates[:, t, cols].rearrange("p (a b) -> p a b", b=TOPK)
                v.tensor_tensor(gt, best, best[:, :, 0:1].to_broadcast([P, 2, TOPK]), ALU.subtract).then_inc(s["gate_in"], 1)
                link(last)
                posf = pos_u.rearrange("p a b -> p (a b)")
                v.tensor_scalar(pos_h[:, 0, :], posf, 4, None, ALU.logical_shift_right)
                link(v.tensor_scalar(pos_h[:, 1, :], posf, TOPK - 1, None, ALU.bitwise_and))
                link(v.tensor_copy(pos_f, pos_h))
                hit = cand.rearrange("p (h q k) -> p h q k", h=2, k=TOPK)
                for half in range(2):
                    last = v.tensor_tensor(hit[:, half], pos_f[:, half, :].unsqueeze(2).to_broadcast([P, PART, TOPK]),
                                           it16.unsqueeze(1).to_broadcast([P, PART, TOPK]), ALU.is_equal)
                link(last)
                for half in range(2):
                    for p in range(2):
                        hp = hit[:, half, p * TOPK:(p + 1) * TOPK, :]
                        last = v.tensor_tensor(hp, hp, top_f[:, 2 * p + half, :].unsqueeze(1).to_broadcast([P, TOPK, TOPK]),
                                               ALU.mult)
                link(last)
                dve.wait_ge(s["gate_exp"], n + 1)
                v.tensor_reduce(gsum[:, :], gt, AX, ALU.add)
                link(v.tensor_reduce(e_hl.rearrange("p a b -> p (a b)"), hit.rearrange("p h q k -> p (h q) k"), AX, ALU.add))
                v.reciprocal(gsum[:, :], gsum[:, :])
                link(v.scalar_tensor_tensor(e_hl[:, 0, :], e_hl[:, 0, :], float(NKEYS), e_hl[:, 1, :], ALU.mult, ALU.add))
                v.tensor_copy(idxu[:, t, cols], e_hl[:, 0, :]).then_inc(s["idx_ready"], 1)
                link(v.tensor_tensor(gt, gt, gsum[:, :].unsqueeze(2).to_broadcast([P, 2, TOPK]), ALU.mult))

            def scale_out(t):
                dve.wait_ge(s["y_act"], t + 1)
                if t >= 1:
                    dve.wait_ge(s["stored"], 16 * t)
                v.scalar_tensor_tensor(outb, ps[:, 2 * (t % 2):2 * (t % 2) + 2, :].rearrange("p a b -> p (a b)"),
                                       small[:, 42:43], fin_g, ALU.mult, ALU.mult).then_inc(s["y_out"], 1)

            for n in range(2):
                best_keys(n)
                best_pairs(n)
            meet(dve, 24)
            for n in range(NPARTS):
                t, part = n // PARTS, n % PARTS
                if part == 0:
                    dve.wait_ge(s["tok_out"], 2 * t + 2)
                for loop in range(2):
                    first = (n * PART + loop * PART // 2) // UV
                    with dve.Fori(0, PART // UV // 2) as i:
                        for g in range(UV // 2):
                            for sl in (2 * g, 2 * g + 1):
                                dve.wait_ge(uv_in[sl], (i + (first + 1)) * 16)
                                last = v.scalar_tensor_tensor(uv[:, sl, 0:D], uv[:, sl, 0:D], 1.0, h2tok[t], ALU.mult, ALU.mult,
                                                              accum_out=hdot[:, sl:sl + 1])
                            last.then_inc(s["dots"], 1)
                            dve.wait_ge(s["gelu"], i * (UV // 2) + (UV // 2 * first + g + 1))
                            for sl in (2 * g, 2 * g + 1):
                                v.tensor_scalar(diag[:, sl, :], ident, hgel[:, sl:sl + 1],
                                                gates[:, t, bass.ds(i * UV + (first * UV % PAIRS + sl), 1)], ALU.mult, ALU.mult
                                                ).then_inc(s["diag"], 1)
                    if n + 2 < NPARTS:
                        (best_keys, best_pairs)[loop](n + 2)
                if part == 0 and t >= 1:
                    scale_out(t - 1)
            scale_out(TT - 1)

        @block.gpsimd
        def _(pool):
            g_ = nc.gpsimd

            def lower(n, wait):
                pool.wait_ge(hi_ready, wait)
                g_.tensor_tensor(ring_r[:, n % RING], ring[:, n % RING], w_hi[:, n % PAIR].bitcast(F32), ALU.subtract
                                 ).then_inc(w_ready, 1)

            levels_at = FIRST_OF["b_gate"]
            with pool.Fori(0, levels_at // RING) as i:
                for j in range(RING):
                    lower(j, i * RING + (j + 1))
            for n in range(levels_at - levels_at % RING, levels_at):
                lower(n, n + 1)
            E, QL, QB = tokens(7), tokens(0), tokens(6)
            for u in range(2 * len(LEVELS)):
                hs = slice(4 * (u % 2), 4 * (u % 2) + 4)
                pool.wait_ge(s["lev_exp"], u + 1)
                if u >= 2:
                    pool.wait_ge(s["lev_mm"], TT * (u + 1))
                g_.tensor_tensor(QL[:, hs, :], QB[:, hs, :], E[:, hs, :], ALU.mult).then_inc(s["lev_q"], 1)
            rest = levels_at + (-levels_at) % RING
            for n in range(levels_at, rest):
                lower(n, n + 1)
            with pool.Fori(0, (CHUNKS - rest) // RING) as i:
                for j in range(RING):
                    lower(j, i * RING + (rest + j + 1))
            for n in range(CHUNKS - CHUNKS % RING, CHUNKS):
                lower(n, n + 1)
            for n in range(TT * PAIRS):
                if n % PART == 0:
                    pool.wait_ge(s["idx_ready"], n // PART + 1)
                if n == UV // 2:
                    pool.wait_ge(s["tok_mm"], TT)
                if n >= UV:
                    pool.wait_ge(s["v_used"], n - UV + 1)
                e = n % PAIRS
                g_.indirect_dma_start(uv[:, n % UV, :], None, experts,
                                      bass.IndirectOffsetOnAxis(ap=idxu[:, n // PAIRS, e:e + 1], axis=0)
                                      ).then_inc(uv_in[n % UV], 16)


def shape_constants():
    con = np.zeros((P, CONST_W), np.float32)

    def put(name, value, rows=P):
        a, b = CONST[name]
        con[:rows, a:b] = value.reshape(rows, b - a)

    j, i = np.arange(P)[:, None], np.arange(P)[None, :]
    put("ident", (j == i).astype(np.float32))
    put("flip", (j + i == P - 1).astype(np.float32))
    put("ones", np.ones((P, P), np.float32))
    put("causal", np.where(i <= j, np.float32(0), np.float32(NEG)))
    same = j // C == i // C
    put("chunk_causal", (same & (j <= i)).astype(np.float32))
    put("level", np.stack([((j // (2 * m) == i // (2 * m)) & (j % (2 * m) < m) & (i % (2 * m) >= m)).astype(np.float32)
                           for m in LEVELS], 1))
    put("sel", np.repeat(np.eye(H, dtype=np.float32)[:, :, None], P, 2), H)
    put("reset", np.tile((np.arange(SEQ) % C != 0).astype(np.float32), (P, 1)))
    put("iota16", np.tile(np.arange(TOPK, dtype=np.float32), (P, 1)))
    placing = np.zeros((P, 7 * P), np.float32)
    placing[:, 3 * P:4 * P] = np.eye(P, dtype=np.float32)

    def bucket(n):
        exact = BUCKETS // 2
        if n < exact:
            return n
        return min(exact + int(np.log(n / exact) / np.log(MAX_DISTANCE / exact) * (BUCKETS - exact)), BUCKETS - 1)

    toe = np.zeros((P, TOE), np.float32)
    for x in range(TOE_W):
        d = 2 * WIN - 1 - x
        toe[bucket(d) if 0 <= d < WIN else BUCKETS, x] = 1
    for x in range(TOE_M):
        d = L - 1 - x
        toe[bucket(d) if d >= 0 else BUCKETS, TOE_W + x] = 1
    return con, placing, toe


def weight_stream(w_in, w_out, w_gate_up, w_down, w_in2, branch_a, branch_b, w_out2, w_pq):
    def chunks(w, cols=None):
        w = w if cols is None else w[:, cols]
        k, m = w.shape[0] // P, w.shape[1] // P
        return w.reshape(k, P, m, P).transpose(2, 1, 0, 3).reshape(m, P, k * P)

    heads = [4 * half + m for m in range(4) for half in range(2)]
    head_cols = np.concatenate([np.arange(HD * hd, HD * hd + HD) for hd in heads])
    kv = KV * HD
    q = H * HD
    o_ka, o_va, o_qb = q, q + kv, q + 2 * kv
    o_kb, o_vb = o_qb + q, o_qb + 2 * q
    order = np.concatenate([head_cols, np.arange(o_ka, o_va), np.arange(o_qb, o_vb), np.arange(o_va, o_qb),
                            np.arange(o_vb, o_vb + q)])
    rows = np.concatenate([head_cols, np.arange(q, 2 * q)])
    gate_up = np.stack([chunks(w_gate_up[:, :DFF]), chunks(w_gate_up[:, DFF:])], 1).reshape(2 * FT, P, D)
    down = np.zeros((DT, DOWN_CH * DT, P, P), np.float32)
    down[:, :FT] = w_down.reshape(FT, P, DT, P).transpose(2, 0, 1, 3)
    down = down.reshape(DT, DOWN_CH, DT, P, P).transpose(0, 1, 3, 2, 4).reshape(DT * DOWN_CH, P, D)
    a = [0, D, 2 * D, 3 * D, 3 * D + 2 * H]
    g0 = a[4]
    sec = lambda n: chunks(w_in2[:, g0 + n * D:g0 + (n + 1) * D])
    def half_deep(w):
        return w.reshape(PAIR, DT // PAIR, P, -1, 256).transpose(3, 0, 2, 1, 4).reshape(-1, P, D)

    fm, tm = order[:13 * P], order[13 * P:]
    v_cols = np.concatenate([w_in[:, tm], np.zeros((D, 128), np.float32)], 1)
    parts = [chunks(w_in, fm), half_deep(v_cols), chunks(w_out[rows]), gate_up, down,
             chunks(w_in2[:, :3 * D]), sec(0), chunks(branch_a), sec(5),
             sec(1), half_deep(w_in2[:, g0 + 2 * D:g0 + 3 * D]), sec(3), sec(4), chunks(branch_b), sec(6), chunks(w_out2), chunks(w_pq)]
    stream = np.concatenate(parts)
    assert stream.shape == (CHUNKS, P, D)
    return stream


def small_parameters(w):
    par = np.zeros((P, PARAM_W), np.float32)

    def put(name, value):
        a, b = PARAM[name]
        value = value.reshape(value.shape[0], b - a)
        par[:value.shape[0], a:b] = value

    cols = lambda x: x.reshape(-1, P).T
    for name, src in (("ln_pre_mix", "ln_pre_mix"), ("ln_post_mix", "ln_post_mix"), ("ln_pre_ffn", "ln_pre_ffn"),
                      ("ln_post_ffn", "ln_post_ffn"), ("norm1", "norm1_2"), ("norm2", "norm2_2"),
                      ("a_onorm", "a_onorm_2"), ("b_onorm", "b_onorm_2")):
        put(name, cols(w[src]))
    put("lower0", cols(w["b_lower_bound_2"][0]))
    put("lower1", cols(w["b_lower_bound_2"][1]))
    put("conv", w["conv_a_2"][0].reshape(4, 24, P).transpose(2, 1, 0))
    put("b_forget", w["b_forget"].reshape(H, 1))
    put("a_log", w["a_log_2"].reshape(H, 1))
    put("dt_bias", w["dt_bias_2"].reshape(H, 1))
    put("rel", np.concatenate([w["rel_bias"], np.full((1, H), NEG, np.float32)]))
    rows8 = lambda x: x.reshape(DT, P, H).transpose(1, 0, 2)
    put("w_f", rows8(w["w_in"][0][:, -H:]))
    put("w_beta", rows8(w["w_in_2"][0][:, 3 * D:3 * D + H]))
    put("w_alpha", rows8(w["w_in_2"][0][:, 3 * D + H:3 * D + 2 * H]))
    return par


def kernel(**inputs):
    import concourse.bacc as bacc
    from concourse.bass_utils import run_bass_kernel_spmd

    w = {name: np.ascontiguousarray(a) for name, a in inputs.items()}
    con, placing, toe = shape_constants()
    arrays = {
        "xT": np.ascontiguousarray(np.concatenate([w["meta_tokens"], w["x"][0]]).T),
        "weights": weight_stream(w["w_in"][0], w["w_out"][0], w["w_gate_up"][0], w["w_down"][0], w["w_in_2"][0],
                                 w["w_branch_a_2"][0], w["w_branch_b_2"][0], w["w_out_2"][0], w["w_pq_2"][0]),
        "params": small_parameters(w),
        "consts": con,
        "placing": placing,
        "toeplitz": toe,
        "sinks": w["sinks"][0],
        "keys": np.ascontiguousarray(w["sub_keys_2"][0].transpose(3, 1, 0, 2)).reshape(P, 2 * PH * NKEYS),
        "final_norm": w["final_norm_2"],
        "experts": np.concatenate([w["expert_u_2"][0], w["expert_v_2"][0]], 1),
    }
    nc = bacc.Bacc("TRN2", target_bir_lowering=False, num_devices=1)
    args = [nc.dram_tensor(f"in_{n}", a.shape, F32, kind="ExternalInput").ap() for n, a in arrays.items()]
    out = nc.dram_tensor("out", (SEQ, D), F32, kind="ExternalOutput").ap()
    build(nc, *args, out)
    r = run_bass_kernel_spmd(nc, [{f"in_{n}": a for n, a in arrays.items()}], core_ids=[0])
    return r.results[0]["out"].reshape(1, SEQ, D)
```
